# Optimizing a Trainium2 kernel written in Bass

```python
import math
import jax, jax.numpy as jnp
from jax import lax
import numpy as np

D_MODEL = 1024
BATCH = 1
SEQ = 256
DEPTH = 2

N_MIXERS = 2
SSM_EXPAND = 2
SSM_D_INNER = SSM_EXPAND * D_MODEL
SSM_HEADDIM = 64
SSM_N_HEADS = SSM_D_INNER // SSM_HEADDIM
SSM_N_GROUPS = 8
SSM_HEADS_PER_GROUP = SSM_N_HEADS // SSM_N_GROUPS
SSM_D_STATE = 128
SSM_CONV_K = 4
SSM_CHUNK = 128
SSM_CONV_DIM = SSM_D_INNER + 2 * SSM_N_GROUPS * SSM_D_STATE
SSM_IN_DIM = SSM_D_INNER + SSM_CONV_DIM + SSM_N_HEADS
ATTN_HEAD_DIM = 64
ATTN_N_HEADS = D_MODEL // (2 * ATTN_HEAD_DIM)
ATTN_V_DIM = 2 * ATTN_HEAD_DIM
ATTN_QKV_DIM = 3 * D_MODEL
ROT_DIM = ATTN_HEAD_DIM // 4
ROPE_THETA = 500000.0
Q_BLOCK = 128
MOE_GROUPS = 4
MOE_EXPERTS_PER_GROUP = 8
MOE_N_EXPERTS = MOE_GROUPS * MOE_EXPERTS_PER_GROUP
MOE_TOP_K = 2
MOE_D_FF = 512
MOE_BLOCK = 128
DEEPNORM_ALPHA = (2 * DEPTH) ** 0.25
DEEPNORM_BETA = (8 * DEPTH) ** -0.25
NORM_EPS = 1e-5
N_SSM_LAYERS = (DEPTH + N_MIXERS - 1) // N_MIXERS
N_ATTN_LAYERS = DEPTH // N_MIXERS


def layer_norm(x, g, b):
    xf = x.astype(jnp.float32)
    mu = jnp.mean(xf, axis=-1, keepdims=True)
    var = jnp.mean(jnp.square(xf - mu), axis=-1, keepdims=True)
    y = (xf - mu) * lax.rsqrt(var + NORM_EPS) * g.astype(jnp.float32) + b.astype(jnp.float32)
    return y.astype(x.dtype)

def causal_depthwise_conv(u, w, bias):
    k = w.shape[0]
    out = lax.conv_general_dilated(u, w[:, None, :], window_strides=(1,), padding=[(k - 1, 0)],
                                   dimension_numbers=("NWC", "WIO", "NWC"),
                                   feature_group_count=u.shape[-1])
    return out + bias

def ssd_chunked(xh, dt, a, bm, cm):
    b, s = xh.shape[0], xh.shape[1]
    c = s // SSM_CHUNK
    G, R, P, N, L = SSM_N_GROUPS, SSM_HEADS_PER_GROUP, SSM_HEADDIM, SSM_D_STATE, SSM_CHUNK
    dtc = dt.reshape(b, c, L, G, R)
    xdt = xh.reshape(b, c, L, G, R, P) * dtc[..., None]
    bc = bm.reshape(b, c, L, G, N)
    cc = cm.reshape(b, c, L, G, N)
    a_cum = jnp.cumsum(dtc * a, axis=2)
    causal = jnp.tril(jnp.ones((L, L), dtype=bool))
    seg = a_cum[:, :, :, None] - a_cum[:, :, None, :]
    decay_ls = jnp.exp(jnp.where(causal[:, :, None, None], seg, -jnp.inf))
    cb = jnp.einsum("bclgn,bcsgn->bclsg", cc, bc)
    y_diag = jnp.einsum("bclsgr,bcsgrp->bclgrp", cb[..., None] * decay_ls, xdt)
    decay_to_end = jnp.exp(a_cum[:, :, -1:] - a_cum)
    chunk_states = jnp.einsum("bclgn,bclgrp->bcgrpn", bc, xdt * decay_to_end[..., None])
    chunk_decay = jnp.exp(a_cum[:, :, -1])

    def step(h, inp):
        st, dec = inp
        return h * dec[..., None, None] + st, h

    h0 = jnp.zeros((b, G, R, P, N), jnp.float32)
    _, prev = lax.scan(step, h0, (jnp.moveaxis(chunk_states, 1, 0), jnp.moveaxis(chunk_decay, 1, 0)))
    prev = jnp.moveaxis(prev, 0, 1)
    y_off = jnp.einsum("bclgn,bcgrpn->bclgrp", cc, prev) * jnp.exp(a_cum)[..., None]
    return (y_diag + y_off).reshape(b, s, G, R, P)

def mamba2_mixer(x, w_in, conv_w, conv_b, dt_bias, a_log, d_skip, norm_w, w_out):
    b, s, _ = x.shape
    G, R, P, N = SSM_N_GROUPS, SSM_HEADS_PER_GROUP, SSM_HEADDIM, SSM_D_STATE
    zxbcdt = x @ w_in
    z = zxbcdt[..., :SSM_D_INNER]
    xbc = zxbcdt[..., SSM_D_INNER:SSM_D_INNER + SSM_CONV_DIM]
    dt_raw = zxbcdt[..., SSM_D_INNER + SSM_CONV_DIM:]
    xbc = jax.nn.silu(causal_depthwise_conv(xbc, conv_w, conv_b))
    xs = xbc[..., :SSM_D_INNER]
    bm = xbc[..., SSM_D_INNER:SSM_D_INNER + G * N].reshape(b, s, G, N).astype(jnp.float32)
    cm = xbc[..., SSM_D_INNER + G * N:].reshape(b, s, G, N).astype(jnp.float32)
    dt = jax.nn.softplus(dt_raw.astype(jnp.float32) + dt_bias.astype(jnp.float32)).reshape(b, s, G, R)
    a = -jnp.exp(a_log.astype(jnp.float32)).reshape(G, R)
    xh = xs.reshape(b, s, G, R, P).astype(jnp.float32)
    y = ssd_chunked(xh, dt, a, bm, cm) + d_skip.astype(jnp.float32).reshape(G, R)[..., None] * xh
    yg = (y.reshape(b, s, SSM_D_INNER) * jax.nn.silu(z.astype(jnp.float32))).reshape(b, s, G, SSM_D_INNER // G)
    yg = yg * lax.rsqrt(jnp.mean(jnp.square(yg), axis=-1, keepdims=True) + NORM_EPS)
    yg = yg.reshape(b, s, SSM_D_INNER) * norm_w.astype(jnp.float32)
    return yg.astype(x.dtype) @ w_out

def rope_tables(positions):
    inv = ROPE_THETA ** (-jnp.arange(0, ROT_DIM, 2, dtype=jnp.float32) / ROT_DIM)
    ang = positions.astype(jnp.float32)[..., None] * inv
    return jnp.cos(ang), jnp.sin(ang)

def apply_partial_rope(t, cos, sin):
    half = ROT_DIM // 2
    tf = t[..., :ROT_DIM].astype(jnp.float32)
    r1, r2 = tf[..., :half], tf[..., half:]
    c = cos[:, :, None, None, :]
    s = sin[:, :, None, None, :]
    rot = jnp.concatenate([r1 * c - r2 * s, r2 * c + r1 * s], axis=-1).astype(t.dtype)
    return jnp.concatenate([rot, t[..., ROT_DIM:]], axis=-1)

def diff_attention(x, cos, sin, w_qkv, lam_q1, lam_k1, lam_q2, lam_k2, subln_w, w_o, lambda_init):
    b, s, _ = x.shape
    H, Dh = ATTN_N_HEADS, ATTN_HEAD_DIM
    qkv = x @ w_qkv
    q = qkv[..., :D_MODEL].reshape(b, s, H, 2, Dh)
    k = qkv[..., D_MODEL:2 * D_MODEL].reshape(b, s, H, 2, Dh)
    v = qkv[..., 2 * D_MODEL:].reshape(b, s, H, ATTN_V_DIM)
    q = apply_partial_rope(q, cos, sin)
    k = apply_partial_rope(k, cos, sin)
    scale = Dh ** -0.5
    lam = (jnp.exp(jnp.sum(lam_q1.astype(jnp.float32) * lam_k1.astype(jnp.float32)))
           - jnp.exp(jnp.sum(lam_q2.astype(jnp.float32) * lam_k2.astype(jnp.float32))) + lambda_init)
    outs = []
    for i in range(s // Q_BLOCK):
        kv_len = (i + 1) * Q_BLOCK
        qb = q[:, i * Q_BLOCK:kv_len]
        kb = k[:, :kv_len]
        vb = v[:, :kv_len]
        sc = jnp.einsum("bqhcd,bkhcd->bhcqk", qb, kb).astype(jnp.float32) * scale
        q_pos = i * Q_BLOCK + jnp.arange(Q_BLOCK)
        mask = jnp.arange(kv_len)[None, :] <= q_pos[:, None]
        p = jax.nn.softmax(jnp.where(mask, sc, -jnp.inf), axis=-1)
        attn = p[:, :, 0] - lam * p[:, :, 1]
        outs.append(jnp.einsum("bhqk,bkhe->bqhe", attn.astype(v.dtype), vb))
    o = jnp.concatenate(outs, axis=1).astype(jnp.float32)
    o = o * lax.rsqrt(jnp.mean(jnp.square(o), axis=-1, keepdims=True) + NORM_EPS)
    o = o * subln_w.astype(jnp.float32) * (1.0 - lambda_init)
    return o.reshape(b, s, H * ATTN_V_DIM).astype(x.dtype) @ w_o

def hier_moe(x, w_group, w_expert, w_gate, w_up, w_down):
    b, s, d = x.shape
    T = b * s
    A = T * MOE_TOP_K
    xf = x.reshape(T, d)
    g_prob = jax.nn.softmax((xf @ w_group).astype(jnp.float32), axis=-1)
    g_sel = jnp.argmax(g_prob, axis=-1)
    g_gate = jnp.take_along_axis(g_prob, g_sel[:, None], axis=-1)[:, 0]
    e_logits = (xf @ w_expert).astype(jnp.float32).reshape(T, MOE_GROUPS, MOE_EXPERTS_PER_GROUP)
    e_logits = jnp.take_along_axis(e_logits, g_sel[:, None, None], axis=1)[:, 0]
    top_p, top_i = lax.top_k(jax.nn.softmax(e_logits, axis=-1), MOE_TOP_K)
    top_p = top_p / jnp.sum(top_p, axis=-1, keepdims=True)
    weight = (g_gate[:, None] * top_p).reshape(A)
    expert_id = (g_sel[:, None] * MOE_EXPERTS_PER_GROUP + top_i).reshape(A).astype(jnp.int32)
    token_id = jnp.repeat(jnp.arange(T, dtype=jnp.int32), MOE_TOP_K)
    order = jnp.argsort(expert_id)
    sorted_e = expert_id[order]
    counts = jax.ops.segment_sum(jnp.ones((A,), jnp.int32), expert_id, num_segments=MOE_N_EXPERTS)
    padded = ((counts + MOE_BLOCK - 1) // MOE_BLOCK) * MOE_BLOCK
    starts = jnp.cumsum(counts) - counts
    pends = jnp.cumsum(padded)
    pstarts = pends - padded
    dest = pstarts[sorted_e] + (jnp.arange(A, dtype=jnp.int32) - starts[sorted_e])
    n_blocks = -(-A // MOE_BLOCK) + MOE_N_EXPERTS
    P = n_blocks * MOE_BLOCK
    row_tok = jnp.full((P,), T, jnp.int32).at[dest].set(token_id[order])
    row_w = jnp.zeros((P,), x.dtype).at[dest].set(weight[order].astype(x.dtype))
    block_expert = jnp.minimum(jnp.searchsorted(pends, jnp.arange(n_blocks, dtype=jnp.int32) * MOE_BLOCK,
                                                side="right"), MOE_N_EXPERTS - 1)
    xpad = jnp.concatenate([xf, jnp.zeros((1, d), x.dtype)], axis=0)
    rows = xpad[row_tok].reshape(n_blocks, MOE_BLOCK, d)

    def expert_block(args):
        xb, e = args
        h = jax.nn.silu(xb @ w_gate[e]) * (xb @ w_up[e])
        return h @ w_down[e]

    yb = lax.map(expert_block, (rows, block_expert)).reshape(P, d)
    out = jax.ops.segment_sum(yb * row_w[:, None], row_tok, num_segments=T + 1)[:T]
    return out.reshape(b, s, d)

def first_inputs(seed: int = 0) -> dict:
    key = jax.random.key(seed)
    ks = jax.random.split(key, 32)
    f32 = jnp.float32
    nrm = lambda k, shape, sc: jax.random.normal(k, shape, f32) * sc
    x = jax.random.normal(ks[0], (BATCH, SEQ, D_MODEL), f32)
    start = jax.random.randint(ks[1], (BATCH, 1), 0, 1024, dtype=jnp.int32)
    positions = (start + jnp.arange(SEQ, dtype=jnp.int32)[None, :]).astype(jnp.int32)
    ln_mix_g = 1.0 + nrm(ks[2], (DEPTH, D_MODEL), 0.02)
    ln_mix_b = nrm(ks[3], (DEPTH, D_MODEL), 0.02)
    ln_ffn_g = 1.0 + nrm(ks[4], (DEPTH, D_MODEL), 0.02)
    ln_ffn_b = nrm(ks[5], (DEPTH, D_MODEL), 0.02)
    ns = N_SSM_LAYERS
    ssm_w_in = nrm(ks[6], (ns, D_MODEL, SSM_IN_DIM), D_MODEL ** -0.5)
    ssm_conv_w = nrm(ks[7], (ns, SSM_CONV_K, SSM_CONV_DIM), SSM_CONV_K ** -0.5)
    ssm_conv_b = nrm(ks[8], (ns, SSM_CONV_DIM), 0.02)
    u = jax.random.uniform(ks[9], (ns, SSM_N_HEADS), f32)
    dt0 = jnp.exp(u * (math.log(0.1) - math.log(0.001)) + math.log(0.001))
    ssm_dt_bias = dt0 + jnp.log(-jnp.expm1(-dt0))
    ssm_a_log = jnp.log(jax.random.uniform(ks[10], (ns, SSM_N_HEADS), f32, 1.0, 16.0))
    ssm_d = 1.0 + nrm(ks[11], (ns, SSM_N_HEADS), 0.02)
    ssm_norm_w = 1.0 + nrm(ks[12], (ns, SSM_D_INNER), 0.02)
    ssm_w_out = nrm(ks[13], (ns, SSM_D_INNER, D_MODEL), SSM_D_INNER ** -0.5 * DEEPNORM_BETA)
    na = N_ATTN_LAYERS
    attn_w_qkv = nrm(ks[14], (na, D_MODEL, ATTN_QKV_DIM), D_MODEL ** -0.5)
    attn_lam_q1 = nrm(ks[15], (na, ATTN_HEAD_DIM), 0.1)
    attn_lam_k1 = nrm(ks[16], (na, ATTN_HEAD_DIM), 0.1)
    attn_lam_q2 = nrm(ks[17], (na, ATTN_HEAD_DIM), 0.1)
    attn_lam_k2 = nrm(ks[18], (na, ATTN_HEAD_DIM), 0.1)
    attn_subln_w = 1.0 + nrm(ks[19], (na, ATTN_V_DIM), 0.02)
    attn_w_o = nrm(ks[20], (na, ATTN_N_HEADS * ATTN_V_DIM, D_MODEL), D_MODEL ** -0.5 * DEEPNORM_BETA)
    moe_w_group = nrm(ks[21], (DEPTH, D_MODEL, MOE_GROUPS), D_MODEL ** -0.5)
    moe_w_expert = nrm(ks[22], (DEPTH, D_MODEL, MOE_N_EXPERTS), D_MODEL ** -0.5)
    moe_w_gate = nrm(ks[23], (DEPTH, MOE_N_EXPERTS, D_MODEL, MOE_D_FF), D_MODEL ** -0.5)
    moe_w_up = nrm(ks[24], (DEPTH, MOE_N_EXPERTS, D_MODEL, MOE_D_FF), D_MODEL ** -0.5)
    moe_w_down = nrm(ks[25], (DEPTH, MOE_N_EXPERTS, MOE_D_FF, D_MODEL), MOE_D_FF ** -0.5 * DEEPNORM_BETA)
    return {"x": x, "positions": positions,
            "ln_mix_g": ln_mix_g, "ln_mix_b": ln_mix_b, "ln_ffn_g": ln_ffn_g, "ln_ffn_b": ln_ffn_b,
            "ssm_w_in": ssm_w_in, "ssm_conv_w": ssm_conv_w, "ssm_conv_b": ssm_conv_b,
            "ssm_dt_bias": ssm_dt_bias, "ssm_a_log": ssm_a_log, "ssm_d": ssm_d,
            "ssm_norm_w": ssm_norm_w, "ssm_w_out": ssm_w_out,
            "attn_w_qkv": attn_w_qkv, "attn_lam_q1": attn_lam_q1, "attn_lam_k1": attn_lam_k1,
            "attn_lam_q2": attn_lam_q2, "attn_lam_k2": attn_lam_k2, "attn_subln_w": attn_subln_w,
            "attn_w_o": attn_w_o,
            "moe_w_group": moe_w_group, "moe_w_expert": moe_w_expert,
            "moe_w_gate": moe_w_gate, "moe_w_up": moe_w_up, "moe_w_down": moe_w_down}

def first_block(x, positions, ln_mix_g, ln_mix_b, ln_ffn_g, ln_ffn_b,
              ssm_w_in, ssm_conv_w, ssm_conv_b, ssm_dt_bias, ssm_a_log, ssm_d, ssm_norm_w, ssm_w_out,
              attn_w_qkv, attn_lam_q1, attn_lam_k1, attn_lam_q2, attn_lam_k2, attn_subln_w, attn_w_o,
              moe_w_group, moe_w_expert, moe_w_gate, moe_w_up, moe_w_down):
    cos, sin = rope_tables(positions)
    h = x
    for layer in range(DEPTH):
        j = layer // N_MIXERS
        if layer % N_MIXERS == 0:
            mix = mamba2_mixer(h, ssm_w_in[j], ssm_conv_w[j], ssm_conv_b[j], ssm_dt_bias[j],
                               ssm_a_log[j], ssm_d[j], ssm_norm_w[j], ssm_w_out[j])
        else:
            lambda_init = 0.8 - 0.6 * math.exp(-0.3 * layer)
            mix = diff_attention(h, cos, sin, attn_w_qkv[j], attn_lam_q1[j], attn_lam_k1[j],
                                 attn_lam_q2[j], attn_lam_k2[j], attn_subln_w[j], attn_w_o[j], lambda_init)
        h = layer_norm(DEEPNORM_ALPHA * h + mix, ln_mix_g[layer], ln_mix_b[layer])
        ffn = hier_moe(h, moe_w_group[layer], moe_w_expert[layer], moe_w_gate[layer],
                       moe_w_up[layer], moe_w_down[layer])
        h = layer_norm(DEEPNORM_ALPHA * h + ffn, ln_ffn_g[layer], ln_ffn_b[layer])
    return h


HEAD_DIM = 64
HEADS_MLA = 4
HEADS_DIL = 8
HEADS_DSA = 4
D_MIX = (HEADS_MLA + HEADS_DIL + HEADS_DSA) * HEAD_DIM
Q_LORA = 256
KV_LORA = 128
MLA_NOPE = 64
MLA_ROPE = 32
MLA_V = HEAD_DIM
DIL_PAIRS = ((128, 1), (512, 4), (2048, 16))
IDX_HEADS = 8
IDX_DIM = 32
DSA_TOPK = 256
D_FF = 2816
CONV_WIDTH = 3
ROT_FRAC = 4
BLOCK = 128
NORM_EPS_2 = 1e-6
DIL_PAD = 16 * BLOCK
IN_SPLITS = (Q_LORA, KV_LORA, MLA_ROPE,
             3 * HEADS_DIL * HEAD_DIM,
             3 * HEADS_DSA * HEAD_DIM,
             IDX_HEADS * IDX_DIM, IDX_DIM, IDX_HEADS)
N_IN = sum(IN_SPLITS)


def rms_norm(x, g):
    xf = x.astype(jnp.float32)
    y = xf * lax.rsqrt(jnp.mean(xf * xf, axis=-1, keepdims=True) + NORM_EPS_2)
    return (y * g.astype(jnp.float32)).astype(x.dtype)

def rope_tables_2(seq, dim):
    inv = jnp.power(jnp.float32(ROPE_THETA), -jnp.arange(0, dim, 2, dtype=jnp.float32) / dim)
    ang = jnp.arange(seq, dtype=jnp.float32)[:, None] * inv[None, :]
    return jnp.cos(ang), jnp.sin(ang)

def apply_rope(x, cos, sin):
    h = x.shape[-1] // 2
    xf = x.astype(jnp.float32)
    x1, x2 = xf[..., :h], xf[..., h:]
    c, s = cos[None, :, None, :], sin[None, :, None, :]
    return jnp.concatenate([x1 * c - x2 * s, x2 * c + x1 * s], axis=-1).astype(x.dtype)

def partial_rope(x, cos, sin):
    r = 2 * cos.shape[-1]
    return jnp.concatenate([apply_rope(x[..., :r], cos, sin), x[..., r:]], axis=-1)

def mla_attention(c_q, c_kv, k_pe_raw, g_q, w_uq, g_kv, w_ukv, cos_a, sin_a):
    B, S, _ = c_q.shape
    q = (rms_norm(c_q, g_q) @ w_uq).reshape(B, S, HEADS_MLA, MLA_NOPE + MLA_ROPE)
    q_nope = q[..., :MLA_NOPE]
    q_pe = apply_rope(q[..., MLA_NOPE:], cos_a, sin_a)
    kv = (rms_norm(c_kv, g_kv) @ w_ukv).reshape(B, S, HEADS_MLA, MLA_NOPE + MLA_V)
    k_nope, v = kv[..., :MLA_NOPE], kv[..., MLA_NOPE:]
    k_pe = apply_rope(k_pe_raw[:, :, None, :], cos_a, sin_a)[:, :, 0]
    scale = (MLA_NOPE + MLA_ROPE) ** -0.5
    nb = S // BLOCK
    qn_b = q_nope.reshape(B, nb, BLOCK, HEADS_MLA, MLA_NOPE).transpose(1, 0, 2, 3, 4)
    qp_b = q_pe.reshape(B, nb, BLOCK, HEADS_MLA, MLA_ROPE).transpose(1, 0, 2, 3, 4)
    kpos = jnp.arange(S)

    def block(args):
        qn, qp, i = args
        s = (jnp.einsum('bqhe,bshe->bhqs', qn, k_nope).astype(jnp.float32)
             + jnp.einsum('bqhr,bsr->bhqs', qp, k_pe).astype(jnp.float32)) * scale
        qpos = i * BLOCK + jnp.arange(BLOCK)
        s = jnp.where((kpos[None, :] <= qpos[:, None])[None, None], s, -jnp.inf)
        p = jax.nn.softmax(s, axis=-1).astype(v.dtype)
        return jnp.einsum('bhqs,bshe->bqhe', p, v)

    o = lax.map(block, (qn_b, qp_b, jnp.arange(nb)))
    return o.transpose(1, 0, 2, 3, 4).reshape(B, S, HEADS_MLA, MLA_V)

def dilated_window(q, k, v, dilation, n_win):
    B, Sp, H, Dh = q.shape
    n = Sp // dilation
    nb = n // BLOCK

    def stride_split(t):
        return t.reshape(B, n, dilation, H, Dh).transpose(0, 2, 1, 3, 4)

    qs, ks, vs = stride_split(q), stride_split(k), stride_split(v)
    qb = qs.reshape(B, dilation, nb, BLOCK, H, Dh)

    def band(t):
        tp = jnp.pad(t, ((0, 0), (0, 0), (BLOCK, 0), (0, 0), (0, 0)))
        prev = tp[:, :, :n].reshape(B, dilation, nb, BLOCK, H, Dh)
        return jnp.concatenate([prev, t.reshape(B, dilation, nb, BLOCK, H, Dh)], axis=3)

    kb, vb = band(ks), band(vs)
    s = jnp.einsum('bdnqhe,bdnkhe->bdnhqk', qb, kb).astype(jnp.float32) * (Dh ** -0.5)
    qi = jnp.arange(BLOCK)[None, :, None]
    kj = jnp.arange(2 * BLOCK)[None, None, :]
    blk = jnp.arange(nb)[:, None, None]
    dist = BLOCK + qi - kj
    valid = (dist >= 0) & (dist <= n_win) & ((blk > 0) | (kj >= BLOCK))
    s = jnp.where(valid[None, None, :, None], s, -jnp.inf)
    m = jnp.max(s, axis=-1, keepdims=True)
    p = jnp.exp(s - m)
    l = jnp.sum(p, axis=-1, keepdims=True)
    o = jnp.einsum('bdnhqk,bdnkhe->bdnqhe', p / l, vb.astype(jnp.float32))
    o = o.reshape(B, dilation, n, H, Dh).transpose(0, 2, 1, 3, 4).reshape(B, Sp, H, Dh)

    def stat_back(t):
        t = t[..., 0].transpose(0, 1, 2, 4, 3).reshape(B, dilation, n, H)
        return t.transpose(0, 2, 1, 3).reshape(B, Sp, H)

    return o, stat_back(m), stat_back(l)

def dilated_attention(q, k, v):
    B, S, H, Dh = q.shape
    Sp = -(-S // DIL_PAD) * DIL_PAD
    pad = ((0, 0), (0, Sp - S), (0, 0), (0, 0))
    qp, kp, vp = jnp.pad(q, pad), jnp.pad(k, pad), jnp.pad(v, pad)
    os_, ms, ls = [], [], []
    for window, dil in DIL_PAIRS:
        o, m, l = dilated_window(qp, kp, vp, dil, window // dil)
        os_.append(o); ms.append(m); ls.append(l)
    m_all = jnp.stack(ms)
    a = jnp.stack(ls) * jnp.exp(m_all - jnp.max(m_all, axis=0))
    o = jnp.einsum('pbsh,pbshe->bshe', a, jnp.stack(os_)) / jnp.sum(a, axis=0)[..., None]
    return o[:, :S].astype(q.dtype)

def dsa_attention(q, k, v, q_idx, k_idx, w_idx):
    B, S, H, Dh = q.shape
    k_sel = min(DSA_TOPK, S // 4)
    nb = S // BLOCK
    idx_scale = (IDX_HEADS * IDX_DIM) ** -0.5
    kpos = jnp.arange(S)

    def to_blocks(t):
        return t.reshape((B, nb, BLOCK) + t.shape[2:]).swapaxes(0, 1)

    def block(args):
        qb, qib, wib, i = args
        qpos = i * BLOCK + jnp.arange(BLOCK)
        causal = kpos[None, :] <= qpos[:, None]
        dots = jnp.einsum('bqhd,bsd->bqhs', qib, k_idx).astype(jnp.float32)
        score = jnp.einsum('bqhs,bqh->bqs', jax.nn.relu(dots), wib.astype(jnp.float32) * idx_scale)
        score = jnp.where(causal[None], score, -jnp.inf)
        _, sel = lax.top_k(score, k_sel)
        flat = sel.reshape(B, BLOCK * k_sel)
        kg = jax.vmap(lambda a, j: a[j])(k, flat).reshape(B, BLOCK, k_sel, H, Dh)
        vg = jax.vmap(lambda a, j: a[j])(v, flat).reshape(B, BLOCK, k_sel, H, Dh)
        s = jnp.einsum('bqhe,bqkhe->bhqk', qb, kg).astype(jnp.float32) * (Dh ** -0.5)
        ok = sel <= qpos[None, :, None]
        s = jnp.where(ok[:, None], s, -jnp.inf)
        p = jax.nn.softmax(s, axis=-1).astype(v.dtype)
        return jnp.einsum('bhqk,bqkhe->bqhe', p, vg)

    o = lax.map(block, (to_blocks(q), to_blocks(q_idx), to_blocks(w_idx), jnp.arange(nb)))
    return o.swapaxes(0, 1).reshape(B, S, H, Dh)

def causal_dwconv(u, w, b):
    K = w.shape[0]
    S = u.shape[1]
    up = jnp.pad(u, ((0, 0), (K - 1, 0), (0, 0)))
    y = up[:, 0:S] * w[0]
    for j in range(1, K):
        y = y + up[:, j:j + S] * w[j]
    return y + b

def second_inputs(seed: int = 0) -> dict:
    key = jax.random.key(seed)
    ks = jax.random.split(key, 16)
    f32 = jnp.float32

    def nrm(k, shape, scale):
        return jax.random.normal(k, shape, f32) * scale

    def gain(k, shape):
        return 1.0 + 0.02 * jax.random.normal(k, shape, f32)

    L = DEPTH
    return {
        "x": nrm(ks[0], (BATCH, SEQ, D_MODEL), 1.0),
        "g_attn": gain(ks[1], (L, D_MODEL)),
        "w_in": nrm(ks[2], (L, D_MODEL, N_IN), D_MODEL ** -0.5),
        "g_q_lat": gain(ks[3], (L, Q_LORA)),
        "w_uq": nrm(ks[4], (L, Q_LORA, HEADS_MLA * (MLA_NOPE + MLA_ROPE)), Q_LORA ** -0.5),
        "g_kv_lat": gain(ks[5], (L, KV_LORA)),
        "w_ukv": nrm(ks[6], (L, KV_LORA, HEADS_MLA * (MLA_NOPE + MLA_V)), KV_LORA ** -0.5),
        "w_o": nrm(ks[7], (L, D_MIX, D_MODEL), D_MIX ** -0.5),
        "g_ffn": gain(ks[8], (L, D_MODEL)),
        "w_up": nrm(ks[9], (L, D_MODEL, 2 * D_FF), D_MODEL ** -0.5),
        "conv_w": nrm(ks[10], (L, CONV_WIDTH, 2 * D_FF), CONV_WIDTH ** -0.5),
        "conv_b": nrm(ks[11], (L, 2 * D_FF), 0.01),
        "w_down": nrm(ks[12], (L, D_FF, D_MODEL), D_FF ** -0.5),
        "g_final": gain(ks[13], (D_MODEL,)),
    }

def second_block(x, g_attn, w_in, g_q_lat, w_uq, g_kv_lat, w_ukv, w_o,
              g_ffn, w_up, conv_w, conv_b, w_down, g_final):
    B, S, _ = x.shape
    cos_a, sin_a = rope_tables_2(S, MLA_ROPE)
    cos_h, sin_h = rope_tables_2(S, HEAD_DIM // ROT_FRAC)
    cos_i, sin_i = rope_tables_2(S, IDX_DIM // ROT_FRAC)
    offsets = np.cumsum(IN_SPLITS)[:-1].tolist()
    for l in range(DEPTH):
        h = rms_norm(x, g_attn[l])
        z = h @ w_in[l]
        c_q, c_kv, k_pe, z_dil, z_dsa, z_qi, z_ki, z_wi = jnp.split(z, offsets, axis=-1)

        o_a = mla_attention(c_q, c_kv, k_pe, g_q_lat[l], w_uq[l], g_kv_lat[l], w_ukv[l], cos_a, sin_a)

        qkv_b = z_dil.reshape(B, S, 3, HEADS_DIL, HEAD_DIM)
        o_b = dilated_attention(partial_rope(qkv_b[:, :, 0], cos_h, sin_h),
                                partial_rope(qkv_b[:, :, 1], cos_h, sin_h),
                                qkv_b[:, :, 2])

        qkv_c = z_dsa.reshape(B, S, 3, HEADS_DSA, HEAD_DIM)
        q_idx = partial_rope(z_qi.reshape(B, S, IDX_HEADS, IDX_DIM), cos_i, sin_i)
        k_idx = partial_rope(z_ki[:, :, None, :], cos_i, sin_i)[:, :, 0]
        o_c = dsa_attention(partial_rope(qkv_c[:, :, 0], cos_h, sin_h),
                            partial_rope(qkv_c[:, :, 1], cos_h, sin_h),
                            qkv_c[:, :, 2], q_idx, k_idx, z_wi)

        mix = jnp.concatenate([o_a.reshape(B, S, -1), o_b.reshape(B, S, -1),
                               o_c.reshape(B, S, -1)], axis=-1)
        x = x + mix @ w_o[l]

        h = rms_norm(x, g_ffn[l])
        u = causal_dwconv(h @ w_up[l], conv_w[l], conv_b[l])
        gate, up = u[..., :D_FF], u[..., D_FF:]
        x = x + (jax.nn.silu(gate) * up) @ w_down[l]
    return rms_norm(x, g_final)


def setup_inputs(seed=0):
    out = dict(first_inputs(seed))
    for name, value in second_inputs(seed + 1).items():
        if name != "x":
            out[name + "_2"] = value
    return out


def reference(
    x, positions, ln_mix_g, ln_mix_b, ln_ffn_g, ln_ffn_b, ssm_w_in, ssm_conv_w, ssm_conv_b,
    ssm_dt_bias, ssm_a_log, ssm_d, ssm_norm_w, ssm_w_out, attn_w_qkv, attn_lam_q1, attn_lam_k1,
    attn_lam_q2, attn_lam_k2, attn_subln_w, attn_w_o, moe_w_group, moe_w_expert, moe_w_gate,
    moe_w_up, moe_w_down, g_attn_2, w_in_2, g_q_lat_2, w_uq_2, g_kv_lat_2, w_ukv_2, w_o_2,
    g_ffn_2, w_up_2, conv_w_2, conv_b_2, w_down_2, g_final_2,
):
    x = first_block(
        x, positions, ln_mix_g, ln_mix_b, ln_ffn_g, ln_ffn_b, ssm_w_in, ssm_conv_w, ssm_conv_b,
        ssm_dt_bias, ssm_a_log, ssm_d, ssm_norm_w, ssm_w_out, attn_w_qkv, attn_lam_q1,
        attn_lam_k1, attn_lam_q2, attn_lam_k2, attn_subln_w, attn_w_o, moe_w_group,
        moe_w_expert, moe_w_gate, moe_w_up, moe_w_down,
    )
    return second_block(
        x, g_attn_2, w_in_2, g_q_lat_2, w_uq_2, g_kv_lat_2, w_ukv_2, w_o_2, g_ffn_2, w_up_2,
        conv_w_2, conv_b_2, w_down_2, g_final_2,
    )


_drawn_inputs = setup_inputs


def setup_inputs(seed=0):
    import zlib

    import numpy as np

    out = dict(_drawn_inputs(seed))
    spreads = {}
    factors = {'ssm_d': 3.168,
     'attn_lam_k2': 3.386,
     'attn_subln_w': 3.959,
     'g_q_lat_2': 8.0,
     'g_kv_lat_2': 7.961,
     'conv_b_2': 4.396,
     'g_final_2': 2.778}
    for name, (base, spread) in spreads.items():
        noise = np.random.default_rng([zlib.crc32(name.encode()), seed]).standard_normal(out[name].shape)
        drawn = base * np.exp(spread * noise) if base else spread * noise
        out[name] = __import__('jax').numpy.asarray(drawn.astype(out[name].dtype))
    for name, factor in factors.items():
        out[name] = (out[name] * factor).astype(out[name].dtype)
    return out
```

```python
from contextlib import ExitStack

import concourse.bass as bass
from concourse import mybir

P = 128
SEQ, D = 256, 1024
TT = SEQ // P
KD = D // P
F32 = mybir.dt.float32
I32 = mybir.dt.int32
U32 = mybir.dt.uint32
ALU = mybir.AluOpType
ACT = mybir.ActivationFunctionType
AX_X = mybir.AxisListType.X
XY = mybir.AxisListType.XY

ALPHA = (2 * 2) ** 0.25
EPS, EPS2 = 1e-5, 1e-6
TWO_PI = 6.283185307179586
LAMBDA_INIT = 0.8 - 0.6 * 2.718281828459045 ** -0.3
ROUND = 12582912.0
RSQRT_GUESS = float(0x5F3759DF)
NEG = -1e30

RING_SLOTS, CHUNK = 6, 4096
G, R, HD, NST = 8, 4, 64, 128
NH = G * R
DI = NH * HD
CONV = DI + 2 * G * NST
NE, EG, NG, FF = 32, 8, 4, 512
CAP = 32
N_IN2 = 3016
DFF2 = 2816
Q_LAT, KV_LAT = 256, 128
FT2 = DFF2 // P
HALF_UP = 2 * FT2

C_ID, C_TRIU, C_STRIU, C_ONES, C_IOTA4 = 0, 128, 256, 384, 512
C_IOTA, C_JCOL, C_TOK8, C_INVF = 640, 672, 673, 675
C_CAUS0, C_MUL0, C_MUL1, C_WIN1, C_ROPE, C_CAUS1 = 683, 811, 939, 1195, 1451, 1563
C_ALL = 1819


class Sem:

    def __init__(self, ctx, nc, name):
        self.sem, self.base = ctx.enter_context(nc.semaphore(name)), 0

    def at(self, k):
        return self.base + k

    def advance(self, total):
        self.base += total


class Chain:

    def __init__(self, ctx, nc, name, eng):
        self.sem, self.eng, self.n, self.loop = ctx.enter_context(nc.semaphore(name)), eng, 0, None

    def link(self, ins):
        ins.then_inc(self.sem, 1)
        self.n += 1
        self.eng.wait_ge(self.sem, self.n if self.loop is None else self.loop + self.n)

    def enter_loop(self, turn, per_turn):
        self.loop, self.start, self.per_turn = turn * per_turn, self.n, per_turn

    def leave_loop(self, turns):
        assert self.n == self.start + self.per_turn, (self.n - self.start)
        self.n, self.loop = self.start + turns * self.per_turn, None


class Ring:

    def __init__(self, ctx, nc, buf):
        self.buf, self.chunks, self.issued, self.released = buf, [], 0, {}
        self.loaded = [ctx.enter_context(nc.semaphore(f"slot{s}_loaded")) for s in range(RING_SLOTS)]

    def rows8(self, c, n=512):
        s = c % RING_SLOTS
        return self.buf[:, s * CHUNK:s * CHUNK + KD * n].rearrange("p (t n) -> p t n", t=KD)

    def rows4(self, c, k=4):
        s = c % RING_SLOTS
        return self.buf[:, s * CHUNK:s * CHUNK + k * D].rearrange("p (t n) -> p t n", t=k)

    def dst(self, c, shape):
        return self.rows8(c, shape[2]) if shape[1] == KD else self.rows4(c, shape[1])

    def release(self, c, sem, count):
        self.released[c] = (sem.sem, sem.at(count))

    def issue(self, sp, upto):
        for c in range(self.issued, min(upto, len(self.chunks))):
            if c >= RING_SLOTS:
                sp.wait_ge(*self.released[c - RING_SLOTS])
            sp.dma_start(self.dst(c, self.chunks[c].shape), self.chunks[c]).then_inc(self.loaded[c % RING_SLOTS], 16)
        self.issued = max(self.issued, min(upto, len(self.chunks)))

    def arrived(self, pe, c, turn=0):
        pe.wait_ge(self.loaded[c % RING_SLOTS], 16 * (c // RING_SLOTS + 1 + turn))


def cols8(w, a, b):
    return w[:, a:b].rearrange("(t p) n -> p t n", p=P)


def bcast(ap, n):
    return ap.unsqueeze(2).to_broadcast([ap.shape[0], ap.shape[1], n])


def hybrid_stack(nc, t):
    out = t["out"]
    ctx = ExitStack()
    with ctx:
        def sb(name, cols, dt=F32):
            return ctx.enter_context(nc.sbuf_tensor(name, [P, cols], dt))

        def sem(name):
            return Sem(ctx, nc, name)

        ring = Ring(ctx, nc, sb("ring", RING_SLOTS * CHUNK))
        h = sb("h", TT * D)[:, :].rearrange("p (a n) -> p a n", a=TT)
        cst = sb("cst", C_ALL)
        pcol = sb("pcol", 256)
        tiny = sb("tiny", 300)
        ARENA = 20112
        arena = sb("arena", ARENA)
        ps = ctx.enter_context(nc.psum_tensor("ps", [P, 8, 512], F32))
        moe_rows = [nc.dram_tensor(f"moe_rows{i}", (2 * SEQ * 4, 256), F32, kind="Internal").ap() for i in range(2)]

        def area(a, *shape):
            n = 1
            for x in shape:
                n *= x
            assert a + n <= ARENA, (a, n)
            v = arena[:, a:a + n]
            if len(shape) == 2:
                v = v.rearrange("p (a b) -> p a b", a=shape[0])
            elif len(shape) == 3:
                v = v.rearrange("p (a b c) -> p a b c", a=shape[0], b=shape[1])
            elif len(shape) == 4:
                v = v.rearrange("p (a b c d) -> p a b c d", a=shape[0], b=shape[1], c=shape[2])
            return v

        ident = cst[:, C_ID:C_ID + P]
        triu = cst[:, C_TRIU:C_TRIU + P]
        striu = cst[:, C_STRIU:C_STRIU + P]
        ones = cst[:, C_ONES:C_ONES + P]

        w_in, w_out = t["ssm_w_in"][0], t["ssm_w_out"][0]
        qkv_w, o_w = t["attn_w_qkv"][0], t["attn_w_o"][0]

        def add(c):
            ring.chunks.append(c)
            return len(ring.chunks) - 1

        def rows4(w, i, k=4):
            return w[i * 512:i * 512 + k * P, :].rearrange("(t p) n -> p t n", p=P)

        def add_experts(layer):
            first = len(ring.chunks)
            for e in range(NE):
                add(cols8(t["moe_w_gate"][layer, e], 0, FF))
                add(cols8(t["moe_w_up"][layer, e], 0, FF))
                add(rows4(t["moe_w_down"][layer, e], 0))
            return first

        c_xbc = [add(cols8(w_in, DI + 512 * i, DI + 512 * i + 512)) for i in range(CONV // 512)]
        c_z = [add(cols8(w_in, 512 * i, 512 * i + 512)) for i in range(DI // 512)]
        c_wout = [add(rows4(w_out, i)) for i in range(DI // 512)]
        c_moe = [add_experts(0)]
        c_qkv = [add(cols8(qkv_w, 512 * i, 512 * i + 512)) for i in range(6)]
        c_wo = [add(rows4(o_w, i)) for i in range(2)]
        c_moe.append(add_experts(1))
        c_in2, c_wo2, c_up2, c_dn2 = [], [], [], []
        for l in range(2):
            c_in2.append([add(cols8(t["w_in_2"][l], 512 * i, min(N_IN2, 512 * i + 512))) for i in range(6)])
            c_wo2.append([add(rows4(t["w_o_2"][l], i)) for i in range(2)])
            c_up2.append([add(cols8(t["w_up_2"][l], 512 * i, 512 * i + 512)) for i in range(11)])
            c_dn2.append([add(rows4(t["w_down_2"][l], i, 4 if i < 5 else 2)) for i in range(6)])

        dve_step = Chain(ctx, nc, "dve_step", nc.vector)
        act_step = Chain(ctx, nc, "act_step", nc.scalar)
        pool_step = Chain(ctx, nc, "pool_step", nc.gpsimd)
        V, A, Q = dve_step.link, act_step.link, pool_step.link

        def rsqrt(r, v, tmp):
            V(nc.vector.tensor_scalar(tmp.bitcast(I32), v.bitcast(I32), 1, None, ALU.logical_shift_right))
            V(nc.vector.tensor_scalar(r.bitcast(I32), tmp.bitcast(I32), -1.0, RSQRT_GUESS, ALU.mult, ALU.add))
            for _ in range(3):
                V(nc.vector.tensor_tensor(tmp, r, r, ALU.mult))
                V(nc.vector.scalar_tensor_tensor(tmp, tmp, -0.5, v, ALU.mult, ALU.mult))
                V(nc.vector.scalar_tensor_tensor(r, tmp, 1.5, r, ALU.add, ALU.mult))

        turned, turned_copied = sem("turned"), sem("turned_copied")

        def pe_turn(pe, src):
            for n in range(4):
                tt, q = n // 2, n % 2
                for k in range(4):
                    mm = nc.tensor.transpose(ps[:, n, k * P:(k + 1) * P],
                                             src[:, tt, (4 * q + k) * P:(4 * q + k + 1) * P], ident)
                mm.then_inc(turned.sem, 1)

        def turn_dst(xT, n):
            return xT[:, 4 * (n % 2):4 * (n % 2) + 4, (n // 2) * P:(n // 2 + 1) * P]

        def dve_turn(dve, xT):
            for n in range(4):
                dve.wait_ge(turned.sem, turned.at(n + 1))
                nc.vector.tensor_copy(turn_dst(xT, n), ps[:, n, :].rearrange("p (k n) -> p k n", k=4))\
                    .then_inc(turned_copied.sem, 1)

        def dve_turn_scaled(dve, xT, gain):
            for n in range(4):
                dve.wait_ge(turned.sem, turned.at(n + 1))
                g = gain[:, 4 * (n % 2):4 * (n % 2) + 4]
                nc.vector.tensor_tensor(turn_dst(xT, n), ps[:, n, :].rearrange("p (k n) -> p k n", k=4),
                                        bcast(g, P), ALU.mult).then_inc(turned_copied.sem, 1)

        def turn_done():
            turned.advance(4)
            turned_copied.advance(4)

        summed = sem("summed")

        def pe_sum_chunks(pe, chunks, lhs):
            n_last = len(chunks) - 1
            for i, c in enumerate(chunks):
                k_tiles = ring.chunks[c].shape[1]
                w = ring.rows4(c, k_tiles)
                ring.arrived(pe, c)
                for tt in range(TT):
                    for half in range(2):
                        for k in range(k_tiles):
                            mm = nc.tensor.matmul(ps[:, 4 + 2 * tt + half, :], lhs(4 * i + k, tt),
                                                  w[:, k, half * 512:(half + 1) * 512],
                                                  start=(i == 0 and k == 0), stop=(i == n_last and k == k_tiles - 1))
                mm.then_inc(summed.sem, 1)

        def release_summed(chunks):
            for i, c in enumerate(chunks):
                ring.release(c, summed, i + 1)

        ln_loaded, ln_norm, ln_read = sem("ln_loaded"), sem("ln_norm"), sem("ln_read")
        ln_stats = tiny[:, 0:24].rearrange("p (a b c) -> p a b c", a=TT, b=2)
        ln_mv = tiny[:, 24:28].rearrange("p (a b) -> p a b", a=TT)
        ln_v, ln_r, ln_t, ln_b = tiny[:, 28:30], tiny[:, 30:32], tiny[:, 32:34], tiny[:, 34:36]

        def sp_ln_params(sp, lnp, g, b):
            sp.dma_start(lnp[:, 0, :], g.partition_broadcast(P)).then_inc(ln_loaded.sem, 16)
            sp.dma_start(lnp[:, 1, :], b.partition_broadcast(P)).then_inc(ln_loaded.sem, 16)

        def dve_layer_norm(dve, lnp):
            for tt in range(TT):
                for half in range(2):
                    nc.vector.bn_stats(ln_stats[:, tt, half, :], h[:, tt, half * 512:(half + 1) * 512])
            V(nc.vector.memset(ln_t, 0.0))
            for tt in range(TT):
                V(nc.vector.bn_aggr(ln_mv[:, tt, :], ln_stats[:, tt, :, :]))
            V(nc.vector.tensor_scalar(ln_v, ln_mv[:, :, 1], EPS, None, ALU.add))
            rsqrt(ln_r, ln_v, ln_t)
            V(nc.vector.scalar_tensor_tensor(ln_b, ln_mv[:, :, 0], -1.0, ln_r, ALU.mult, ALU.mult))
            dve.wait_ge(ln_loaded.sem, ln_loaded.at(32))
            for tt in range(TT):
                V(nc.vector.tensor_scalar(h[:, tt, :], h[:, tt, :], ln_r[:, tt:tt + 1], ln_b[:, tt:tt + 1],
                                          ALU.mult, ALU.add))
            for tt in range(TT):
                V(nc.vector.tensor_tensor(h[:, tt, :], h[:, tt, :], lnp[:, 0, :], ALU.mult))
            for tt in range(TT):
                V(nc.vector.tensor_tensor(h[:, tt, :], h[:, tt, :], lnp[:, 1, :], ALU.add))

        xT = area(0, KD, SEQ)
        silu_z = area(2048, TT, DI)
        xs = area(6144, TT, DI)
        bcT = area(10240, 2 * G, SEQ)
        b_tok = area(14336, G * NST)
        conv_acc = area(15360, 2, SEQ)
        xsT = area(15872, 2, 4, SEQ)
        prm = area(17920, 3, P)
        w_dt = area(18304, KD, NH)
        dt_rows = area(18560, 3, NH)
        dtx = tiny[:, 40:104].rearrange("p (a b) -> p a b", a=TT)

        loaded_x, loaded_p = sem("loaded_x"), sem("loaded_p")
        params_turned, params_copied = sem("params_turned"), sem("params_copied")
        dt_ready, dt_copied = sem("dt_ready"), sem("dt_copied")
        tile_ready, conv_begun, conv_summed, conv_done = (sem("tile_ready"), sem("conv_begun"), sem("conv_summed"),
                                                          sem("conv_done"))
        xs_turned, xs_copied = sem("xs_turned"), sem("xs_copied")
        z_ready, z_done = sem("z_ready"), sem("z_done")
        taps = pcol[:, 0:128].rearrange("p (j f) -> p j f", j=4)
        conv_bias = pcol[:, 128:160]
        norm_w = pcol[:, 160:176]

        for q, c in enumerate(c_xbc):
            ring.release(c, tile_ready, 4 * q + 4)
        for q, c in enumerate(c_z):
            ring.release(c, z_ready, 2 * q + 2)
        with nc.Block() as block:
            @block.sync
            def _(sp):
                sp.dma_start(h, t["x"][0].rearrange("(a p) n -> p a n", p=P)).then_inc(loaded_x.sem, 16)
                sp.dma_start(cst[:, :], t["constants"]).then_inc(loaded_x.sem, 16)
                ring.issue(sp, 2)
                sp.dma_start(w_dt, cols8(w_in, DI + CONV, DI + CONV + NH)).then_inc(loaded_p.sem, 16)
                sp.dma_start(prm[:, 0, :], t["ssm_conv_w"][0].rearrange("j (f p) -> (j f) p", p=P))\
                    .then_inc(loaded_p.sem, 16)
                sp.dma_start(prm[0:32, 1, :], t["ssm_conv_b"][0].rearrange("(f p) -> f p", p=P))\
                    .then_inc(loaded_p.sem, 16)
                sp.dma_start(prm[0:16, 2, :], t["ssm_norm_w"][0].rearrange("(f p) -> f p", p=P))\
                    .then_inc(loaded_p.sem, 16)
                for i, name in enumerate(("ssm_dt_bias", "ssm_a_log", "ssm_d")):
                    sp.dma_start(dt_rows[:, i, :], t[name][0].partition_broadcast(P)).then_inc(loaded_p.sem, 16)
                ring.issue(sp, c_z[-1] + 1 + RING_SLOTS)

            @block.tensor
            def _(pe):
                pe.wait_ge(loaded_x.sem, 32)
                pe_turn(pe, h)
                pe.wait_ge(loaded_p.sem, 7 * 16)
                nc.tensor.transpose(ps[:, 4, 0:128], prm[:, 0, :], ident)
                nc.tensor.transpose(ps[:, 4, 128:160], prm[0:32, 1, :], ident[0:32, 0:32])
                nc.tensor.transpose(ps[:, 4, 160:176], prm[0:16, 2, :], ident[0:16, 0:16])\
                    .then_inc(params_turned.sem, 1)
                pe.wait_ge(turned_copied.sem, 4)
                for tt in range(TT):
                    for k in range(KD):
                        mm = nc.tensor.matmul(ps[:, 0, tt * NH:(tt + 1) * NH], xT[:, k, tt * P:(tt + 1) * P],
                                              w_dt[:, k, :], start=(k == 0), stop=(k == KD - 1))
                mm.then_inc(dt_ready.sem, 1)

                def turn_chunk(q):
                    pe.wait_ge(conv_done.sem, 4 * q + 4)
                    if q:
                        pe.wait_ge(xs_copied.sem, 2 * q if q <= 4 else 8 + q - 4)
                    for tt in range(TT if q < 4 else 1):
                        for k in range(4):
                            src = xsT[:, q % 2, k, :] if q < 4 else bcT[:, 2 * (4 * (q - 4) + k), :]
                            mm = nc.tensor.transpose(ps[:, 6 + tt, k * P:(k + 1) * P], src[:, tt * P:(tt + 1) * P],
                                                     ident)
                        mm.then_inc(xs_turned.sem, 1)

                pe.wait_ge(dt_copied.sem, 1)
                for q, c in enumerate(c_xbc):
                    w = ring.rows8(c)
                    ring.arrived(pe, c)
                    for k4 in range(4):
                        n = 4 * q + k4
                        if n >= 4:
                            pe.wait_ge(conv_summed.sem, n - 3)
                        for k in range(KD):
                            mm = nc.tensor.matmul(ps[:, n % 4, 0:SEQ], w[:, k, k4 * P:(k4 + 1) * P], xT[:, k, :],
                                                  start=(k == 0), stop=(k == KD - 1))
                        mm.then_inc(tile_ready.sem, 1)
                    if 1 <= q <= 6:
                        turn_chunk(q - 1)
                for q, c in enumerate(c_z):
                    w = ring.rows8(c)
                    ring.arrived(pe, c)
                    for tt in range(TT):
                        n = 2 * q + tt
                        if n < 4:
                            pe.wait_ge(conv_summed.sem, 29 + n)
                        else:
                            pe.wait_ge(z_done.sem, n - 3)
                        for k in range(KD):
                            mm = nc.tensor.matmul(ps[:, n % 4, :], xT[:, k, tt * P:(tt + 1) * P], w[:, k, :],
                                                  start=(k == 0), stop=(k == KD - 1))
                        mm.then_inc(z_ready.sem, 1)

            @block.scalar
            def _(act):
                act.wait_ge(params_copied.sem, 1)

                def begin(n):
                    act.wait_ge(tile_ready.sem, n + 1)
                    if n >= 2:
                        act.wait_ge(conv_done.sem, n - 1)
                    nc.scalar.activation(conv_acc[:, n % 2, :], ps[:, n % 4, 0:SEQ], ACT.Identity,
                                         bias=conv_bias[:, n:n + 1], scale=taps[:, 3, n:n + 1])\
                        .then_inc(conv_begun.sem, 1)

                def end(n):
                    act.wait_ge(conv_summed.sem, n + 1)
                    if n < 16:
                        q = n // 4
                        if q >= 2:
                            act.wait_ge(xs_turned.sem, 2 * (q - 1))
                        dst = xsT[:, q % 2, n % 4, :]
                    elif n < 24:
                        dst = bcT[:, 2 * (n - 16), :]
                    else:
                        dst = bcT[:, 2 * (n - 24) + 1, :]
                    nc.scalar.activation(dst, conv_acc[:, n % 2, :], ACT.Silu).then_inc(conv_done.sem, 1)

                for n in range(32):
                    begin(n)
                    if n:
                        end(n - 1)
                end(31)
                for n in range(8):
                    act.wait_ge(z_ready.sem, n + 1)
                    nc.scalar.activation(silu_z[:, n % 2, (n // 2) * 512:(n // 2 + 1) * 512], ps[:, n % 4, :],
                                         ACT.Silu).then_inc(z_done.sem, 1)

            def copy_turned(dve, q):
                for tt in range(TT if q < 4 else 1):
                    n = 2 * q + tt if q <= 4 else 9
                    dve.wait_ge(xs_turned.sem, n + 1)
                    dst = xs[:, tt, q * 512:(q + 1) * 512] if q < 4 else b_tok[:, (q - 4) * 512:(q - 3) * 512]
                    nc.vector.tensor_copy(dst, ps[:, 6 + tt, :]).then_inc(xs_copied.sem, 1)

            @block.vector
            def _(dve):
                dve_turn(dve, xT)
                dve.wait_ge(params_turned.sem, 1)
                nc.vector.tensor_copy(pcol[:, 0:176], ps[:, 4, 0:176]).then_inc(params_copied.sem, 1)
                dve.wait_ge(dt_ready.sem, 1)
                dve.wait_ge(loaded_p.sem, 7 * 16)
                nc.vector.tensor_tensor(dtx, ps[:, 0, 0:TT * NH].rearrange("p (a b) -> p a b", a=TT),
                                        dt_rows[:, 0, :].unsqueeze(1).to_broadcast([P, TT, NH]), ALU.add)\
                    .then_inc(dt_copied.sem, 1)
                dve.wait_ge(params_copied.sem, 1)
                for n in range(32):
                    q = n // 4
                    dve.wait_ge(conv_begun.sem, n + 1)
                    for j in (2, 1, 0):
                        back = 3 - j
                        acc = conv_acc[:, n % 2, back:SEQ]
                        ins = nc.vector.scalar_tensor_tensor(acc, ps[:, n % 4, 0:SEQ - back],
                                                             taps[:, j, n:n + 1], acc, ALU.mult, ALU.add)
                        if j:
                            V(ins)
                    ins.then_inc(conv_summed.sem, 1)
                    if n % 4 == 3 and 2 <= q:
                        copy_turned(dve, q - 2)

        turn_done()

        UNITS = G * TT
        GW = R * HD
        cb_m = area(0, 2, P)
        seg = area(256, 2, R * P)
        state = area(1280, 2, GW)
        junk = area(1792, GW)
        decay = area(15360, 2, R * P)
        mixer = area(16384, 2, R * P)
        xdt = area(17408, 2, GW)
        xdt_end = area(17920, 2, GW)
        dt, dta, acum = area(18656, TT, NH), area(18720, TT, NH), area(18784, 3, NH)
        d_end, e_acum1, a_row = area(18880, NH), area(18912, NH), area(18944, NH)
        tmp1, tmp2 = area(18976, TT * NH), area(19040, TT * NH)
        xsd = area(19136, 2, GW)
        y_off = area(19648, GW)
        ssq = tiny[:, 104:120].rearrange("p (a b) -> p a b", a=G)
        nv, nr, nt = tiny[:, 120:122], tiny[:, 122:124], tiny[:, 124:126]

        dt_dve, dt_act, dt_pe = sem("dt_dve"), sem("dt_act"), sem("dt_pe")
        cb_ready, seg_ready, decay_ready, mixer_ready = (sem("cb_ready"), sem("seg_ready"), sem("decay_ready"),
                                                         sem("mixer_ready"))
        x_ready, y_ready, y_done = sem("x_ready"), sem("y_ready"), sem("y_done")
        ssq_ready, yn_ready, yn_turned, yT_ready = sem("ssq_ready"), sem("yn_ready"), sem("yn_turned"), sem("yT_ready")
        yT = bcT
        lnp = area(0, 2, D)
        release_summed(c_wout)

        def unit(u):
            return u // 2, u % 2, u % 2

        def grp(g):
            return slice(g * GW, (g + 1) * GW)

        with nc.Block() as block:
            @block.sync
            def _(sp):
                sp.wait_ge(yT_ready.sem, 2 * G)
                sp_ln_params(sp, lnp, t["ln_mix_g"][0], t["ln_mix_b"][0])
                ring.issue(sp, c_wout[-1] + 1 + RING_SLOTS)

            @block.tensor
            def _(pe):
                pe.wait_ge(dt_dve.sem, 4)
                for c in range(TT):
                    nc.tensor.matmul(ps[:, 6, c * NH:(c + 1) * NH], triu, dta[:, c, :], start=True, stop=True)
                nc.tensor.matmul(ps[:, 6, 64:96], ones, dta[:, 0, :], start=True, stop=True).then_inc(dt_pe.sem, 1)

                def scores(u):
                    g, c, b = unit(u)
                    if u >= 2:
                        pe.wait_ge(seg_ready.sem, u - 1)
                    tok = slice(c * P, (c + 1) * P)
                    nc.tensor.matmul(ps[:, b, 0:P], bcT[:, 2 * g, tok], bcT[:, 2 * g + 1, tok], start=True, stop=True)
                    for r in range(R):
                        hh = g * R + r
                        mm = nc.tensor.matmul(ps[:, 2 + b, r * P:(r + 1) * P],
                                              dta[:, c, hh:hh + 1].to_broadcast([P, P]), triu, start=True, stop=True)
                    mm.then_inc(cb_ready.sem, 1)

                def products(u):
                    g, c, b = unit(u)
                    pe.wait_ge(x_ready.sem, u + 1)
                    pe.wait_ge(mixer_ready.sem, u + 1)
                    if u >= 2:
                        pe.wait_ge(y_done.sem, u - 1)
                    for r in range(R):
                        nc.tensor.matmul(ps[:, 4 + b, r * HD:(r + 1) * HD], mixer[:, b, r * P:(r + 1) * P],
                                         xdt[:, b, r * HD:(r + 1) * HD], start=True, stop=True)
                    if c == 0:
                        mm = nc.tensor.matmul(ps[:, 4 + b, GW:2 * GW], b_tok[:, g * NST:(g + 1) * NST], xdt_end[:, g % 2, :],
                                              start=True, stop=True)
                    else:
                        pe.wait_ge(y_done.sem, u)
                        mm = nc.tensor.matmul(ps[:, 4 + b, GW:2 * GW], bcT[:, 2 * g + 1, P:SEQ], state[:, g % 2, :],
                                              start=True, stop=True)
                    mm.then_inc(y_ready.sem, 1)

                def turn_group(g):
                    pe.wait_ge(yn_ready.sem, g + 1)
                    if g >= 2:
                        pe.wait_ge(yT_ready.sem, 2 * (g - 1))
                    for f in range(2):
                        for c in range(TT):
                            mm = nc.tensor.transpose(ps[:, 6 + g % 2, (2 * f + c) * P:(2 * f + c + 1) * P],
                                                     xs[:, c, g * GW + f * P:g * GW + (f + 1) * P], ident)
                    mm.then_inc(yn_turned.sem, 1)

                scores(0)
                for u in range(UNITS):
                    if u + 1 < UNITS:
                        scores(u + 1)
                    products(u)
                    if u >= 4 and u % 2 == 0:
                        turn_group((u - 4) // 2)
                turn_group(G - 2)
                turn_group(G - 1)
                pe.wait_ge(yT_ready.sem, 2 * G)
                pe.wait_ge(y_done.sem, UNITS)
                pe_sum_chunks(pe, c_wout, lambda k, tt: yT[:, k, tt * P:(tt + 1) * P])

            @block.scalar
            def _(act):
                nc.scalar.activation(a_row, dt_rows[:, 1, :], ACT.Exp).then_inc(dt_act.sem, 1)
                act.wait_ge(dt_dve.sem, 1)
                nc.scalar.activation(tmp1, tmp1, ACT.Exp, scale=-1.0).then_inc(dt_act.sem, 1)
                act.wait_ge(dt_dve.sem, 2)
                nc.scalar.activation(y_off[:, 0:64], tmp2, ACT.Ln).then_inc(dt_act.sem, 1)
                act.wait_ge(dt_dve.sem, 5)
                nc.scalar.activation(e_acum1, acum[:, 1, :], ACT.Exp).then_inc(dt_act.sem, 1)
                nc.scalar.activation(d_end, d_end, ACT.Exp).then_inc(dt_act.sem, 1)

                def squares(g):
                    act.wait_ge(y_done.sem, 2 * g + 2)
                    if g:
                        act.wait_ge(ssq_ready.sem, g)
                    A(nc.scalar.activation(junk, xs[:, 0, grp(g)], ACT.Square, accum_out=ssq[:, g, 0:1]))
                    nc.scalar.activation(junk, xs[:, 1, grp(g)], ACT.Square, accum_out=ssq[:, g, 1:2])\
                        .then_inc(ssq_ready.sem, 1)

                def copy_group(g):
                    act.wait_ge(yn_turned.sem, g + 1)
                    for f in range(2):
                        nc.scalar.activation(yT[:, 2 * g + f, :], ps[:, 6 + g % 2, f * SEQ:(f + 1) * SEQ], ACT.Copy,
                                             scale=norm_w[:, 2 * g + f:2 * g + f + 1]).then_inc(yT_ready.sem, 1)

                for u in range(UNITS):
                    act.wait_ge(seg_ready.sem, u + 1)
                    if u >= 2:
                        act.wait_ge(mixer_ready.sem, u - 1)
                    nc.scalar.activation(decay[:, u % 2, :], seg[:, u % 2, :], ACT.Exp).then_inc(decay_ready.sem, 1)
                    if u >= 2 and u % 2 == 0:
                        squares((u - 2) // 2)
                    if u >= 4 and u % 2 == 0:
                        copy_group((u - 4) // 2)
                squares(G - 1)
                copy_group(G - 2)
                copy_group(G - 1)

            @block.gpsimd
            def _(pool):
                pool.wait_ge(dt_dve.sem, 3)
                pool.wait_ge(dt_act.sem, 5)
                for u in range(UNITS):
                    g, c, b = unit(u)
                    x3 = xs[:, c, grp(g)].rearrange("p (r d) -> p r d", r=R)
                    heads = slice(g * R, (g + 1) * R)
                    if u >= 2:
                        pool.wait_ge(y_done.sem, u - 1)
                    Q(nc.gpsimd.tensor_tensor(xdt[:, b, :].rearrange("p (r d) -> p r d", r=R), x3,
                                              bcast(dt[:, c, heads], HD), ALU.mult))
                    if c == 0:
                        Q(nc.gpsimd.tensor_tensor(xdt_end[:, g % 2, :].rearrange("p (r d) -> p r d", r=R),
                                                  xdt[:, b, :].rearrange("p (r d) -> p r d", r=R),
                                                  bcast(d_end[:, heads], HD), ALU.mult))
                    nc.gpsimd.tensor_tensor(xsd[:, b, :].rearrange("p (r d) -> p r d", r=R), x3,
                                            bcast(dt_rows[:, 2, heads], HD), ALU.mult).then_inc(x_ready.sem, 1)
                    pool.wait_ge(decay_ready.sem, u + 1)
                    nc.gpsimd.tensor_tensor(mixer[:, b, :].rearrange("p (r l) -> p r l", r=R),
                                            decay[:, b, :].rearrange("p (r l) -> p r l", r=R),
                                            cb_m[:, b, :].unsqueeze(1).to_broadcast([P, R, P]), ALU.mult)\
                        .then_inc(mixer_ready.sem, 1)

            @block.vector
            def _(dve):
                dx = dtx.rearrange("p a b -> p (a b)")
                dtf = dt.rearrange("p a b -> p (a b)")
                nc.vector.scalar_tensor_tensor(tmp1, dx, -1.0, dx, ALU.mult, ALU.max).then_inc(dt_dve.sem, 1)
                dve.wait_ge(dt_act.sem, 2)
                nc.vector.tensor_scalar(tmp2, tmp1, 1.0, None, ALU.add).then_inc(dt_dve.sem, 1)
                dve.wait_ge(dt_act.sem, 3)
                V(nc.vector.tensor_scalar(tmp2, tmp2, -1.0, 1e-30, ALU.add, ALU.max))
                V(nc.vector.reciprocal(dtf, tmp2))
                V(nc.vector.tensor_tensor(dtf, dtf, tmp1, ALU.mult))
                V(nc.vector.tensor_tensor(dtf, dtf, y_off[:, 0:64], ALU.mult))
                V(nc.vector.tensor_scalar(tmp2, tmp2, 1e-30, None, ALU.is_le))
                V(nc.vector.tensor_tensor(tmp2, tmp2, tmp1, ALU.mult))
                V(nc.vector.tensor_tensor(dtf, dtf, tmp2, ALU.add))
                nc.vector.scalar_tensor_tensor(dtf, dx, 0.0, dtf, ALU.max, ALU.add).then_inc(dt_dve.sem, 1)
                dve.wait_ge(dt_dve.sem, 3)
                nc.vector.scalar_tensor_tensor(dta, dt, -1.0, a_row.unsqueeze(1).to_broadcast([P, TT, NH]),
                                               ALU.mult, ALU.mult).then_inc(dt_dve.sem, 1)
                dve.wait_ge(dt_pe.sem, 1)
                V(nc.vector.tensor_copy(acum, ps[:, 6, 0:96].rearrange("p (a b) -> p a b", a=3)))
                nc.vector.tensor_tensor(d_end, acum[:, 2, :], acum[:, 0, :], ALU.subtract).then_inc(dt_dve.sem, 1)
                dve.wait_ge(dt_act.sem, 5)

                def segments(u):
                    g, c, b = unit(u)
                    dve.wait_ge(cb_ready.sem, u + 1)
                    if u >= 2:
                        dve.wait_ge(mixer_ready.sem, u - 1)
                    nc.vector.tensor_tensor(cb_m[:, b, :], ps[:, b, 0:P], triu, ALU.mult)
                    for r in range(R):
                        hh = g * R + r
                        ins = nc.vector.tensor_scalar(seg[:, b, r * P:(r + 1) * P], ps[:, 2 + b, r * P:(r + 1) * P],
                                                      acum[:, c, hh:hh + 1], 0.0, ALU.subtract, ALU.min)
                    ins.then_inc(seg_ready.sem, 1)

                def outputs(u):
                    g, c, b = unit(u)
                    y = xs[:, c, grp(g)]
                    dve.wait_ge(y_ready.sem, u + 1)
                    V(nc.vector.tensor_tensor(y, xsd[:, b, :], ps[:, 4 + b, 0:GW], ALU.add))
                    if c == 0:
                        V(nc.vector.tensor_copy(state[:, g % 2, :], ps[:, 4 + b, GW:2 * GW]))
                    else:
                        V(nc.vector.tensor_tensor(y_off.rearrange("p (r d) -> p r d", r=R),
                                                  ps[:, 4 + b, GW:2 * GW].rearrange("p (r d) -> p r d", r=R),
                                                  bcast(e_acum1[:, g * R:(g + 1) * R], HD), ALU.mult))
                        V(nc.vector.tensor_tensor(y, y, y_off, ALU.add))
                    nc.vector.tensor_tensor(y, y, silu_z[:, c, grp(g)], ALU.mult).then_inc(y_done.sem, 1)

                def normalise(g):
                    dve.wait_ge(ssq_ready.sem, g + 1)
                    V(nc.vector.tensor_scalar(nv, ssq[:, g, :], 1.0 / GW, EPS, ALU.mult, ALU.add))
                    rsqrt(nr, nv, nt)
                    for c in range(TT):
                        y = xs[:, c, grp(g)]
                        ins = nc.vector.tensor_scalar(y, y, nr[:, c:c + 1], None, ALU.mult)
                    ins.then_inc(yn_ready.sem, 1)

                for u in range(UNITS):
                    segments(u)
                    if u:
                        outputs(u - 1)
                    if u >= 3 and u % 2:
                        normalise((u - 3) // 2)
                outputs(UNITS - 1)
                normalise(G - 1)
                dve.wait_ge(summed.sem, summed.at(len(c_wout)))
                for tt in range(TT):
                    for half in range(2):
                        hs = h[:, tt, half * 512:(half + 1) * 512]
                        ins = nc.vector.scalar_tensor_tensor(hs, hs, ALPHA, ps[:, 4 + 2 * tt + half, :], ALU.mult,
                                                             ALU.add)
                V(ins)
                dve_layer_norm(dve, lnp)

        summed.advance(len(c_wout))
        ln_loaded.advance(32)

        W4 = 4 * CAP
        route_pe, route_act, route_dve = sem("route_pe"), sem("route_act"), sem("route_dve")
        router_loaded, pairs_loaded = sem("router_loaded"), sem("pairs_loaded")
        MAIN = {n: sem("moe_" + n) for n in ("slots", "picked", "xg", "gateup", "silu", "hidden", "turned", "hT",
                                             "down", "dest", "rows")}
        stored = [[sem(f"moe_stored{layer}{b}") for b in range(2)] for layer in range(2)]
        OVER = [{n: sem(f"over{layer}_" + n) for n in ("loaded", "shifted", "slots", "picked", "xg", "gateup", "silu", "hidden",
                                                       "turned", "hT", "down", "dest", "rows")} for layer in range(2)]
        ticked = [sem("ticked0"), sem("ticked1")]
        NECOL = NE + 2

        def moe(layer, lnp_g, lnp_b, router_norm_done=None):
            first = c_moe[layer]
            xT = area(0, KD, SEQ)
            wr = area(2048, KD, NG + NE)
            lg = area(2336, TT, NG + NE)
            slots = area(2408, 2, TT, W4)
            xg = area(2920, 2, KD * CAP + 2)
            sg = area(3436, 2, 256)
            hid = area(3948, 2, 256)
            hT = area(4460, 2, 2, 2 * CAP)
            rows = area(4716, 2, 256)
            pos1 = area(5228, TT, NECOL)
            info = area(5300, TT, NECOL, 2)
            chosen = area(5440, TT, 2, NE)
            both = area(5568, TT, NE)
            t8 = area(5632, TT, 8, 8)
            esel = area(5760, TT, 8)
            r1 = area(5776, TT, 16)
            dest = area(5808, 2)
            wcol = area(5810, 2)
            cnt = area(5812, 2)
            cnti = area(5814, 2).bitcast(I32)
            pairs = area(6144, TT, 2, D)
            lnp = area(10240, 2, D)
            tick = area(12288, 1, 1)[0:1, 0, :]
            m, o = MAIN, OVER[layer]
            y_st = stored[layer]

            def gate_w(c):
                return ring.rows8(c)

            def step_slots(dve, s, v, prev, b, e, pos):
                if prev:
                    dve.wait_ge(s["picked"].sem, prev(s["picked"]))
                for tt in range(TT):
                    ins = nc.vector.tensor_scalar(slots[:, b, tt, :], cst[:, C_IOTA4:C_IOTA4 + W4],
                                                  pos[:, tt, bass.ds(e, 1)], None, ALU.is_equal)
                ins.then_inc(s["slots"].sem, 1)

            def step_pick(pe, s, v, prev, b, e):
                pe.wait_ge(s["slots"].sem, v(s["slots"]))
                if prev:
                    pe.wait_ge(s["xg"].sem, prev(s["xg"]))
                for k in range(KD):
                    for tt in range(TT):
                        nc.tensor.matmul(ps[:, b, k * CAP:(k + 1) * CAP], h[:, tt, k * P:(k + 1) * P],
                                         slots[:, b, tt, 0:CAP], start=(tt == 0), stop=(tt == TT - 1))
                for tt in range(TT):
                    mm = nc.tensor.matmul(ps[:, b, KD * CAP:KD * CAP + 2], slots[:, b, tt, :],
                                          info[:, tt, bass.ds(e, 1), :].rearrange("p a b -> p (a b)"),
                                          start=(tt == 0), stop=(tt == TT - 1))
                mm.then_inc(s["picked"].sem, 1)

            def step_xg(act, s, v, prev, b):
                act.wait_ge(s["picked"].sem, v(s["picked"]))
                if prev:
                    act.wait_ge(s["gateup"].sem, prev(s["gateup"]))
                    act.wait_ge(s["dest"].sem, prev(s["dest"]))
                nc.scalar.activation(xg[:, b, :], ps[:, b, 0:KD * CAP + 2], ACT.Copy).then_inc(s["xg"].sem, 1)

            def step_gateup(pe, s, v, prev, b, wg, wu):
                pe.wait_ge(s["xg"].sem, v(s["xg"]))
                if prev:
                    pe.wait_ge(s["hidden"].sem, prev(s["hidden"]))
                for k in range(KD):
                    for j in range(4):
                        w = (wg, wu)[j // 2]
                        mm = nc.tensor.matmul(ps[j * CAP:(j + 1) * CAP, 2 + b, 0:256], xg[:, b, k * CAP:(k + 1) * CAP],
                                              w[:, k, (j % 2) * 256:(j % 2 + 1) * 256],
                                              start=(k == 0), stop=(k == KD - 1))
                mm.then_inc(s["gateup"].sem, 1)

            def step_silu(act, s, v, prev, b):
                act.wait_ge(s["gateup"].sem, v(s["gateup"]))
                if prev:
                    act.wait_ge(s["hidden"].sem, prev(s["hidden"]))
                nc.scalar.activation(sg[64:128, b, :], ps[0:64, 2 + b, 0:256], ACT.Silu).then_inc(s["silu"].sem, 1)

            def step_hidden(dve, s, v, prev, b):
                dve.wait_ge(s["silu"].sem, v(s["silu"]))
                if prev:
                    dve.wait_ge(s["turned"].sem, prev(s["turned"]))
                nc.vector.tensor_tensor(hid[64:128, b, :], sg[64:128, b, :], ps[64:128, 2 + b, 0:256], ALU.mult)\
                    .then_inc(s["hidden"].sem, 1)

            def step_turn(pe, s, v, prev, b):
                pe.wait_ge(s["hidden"].sem, v(s["hidden"]))
                if prev:
                    pe.wait_ge(s["hT"].sem, prev(s["hT"]))
                for c2 in range(2):
                    mm = nc.tensor.matmul(ps[:, 4 + b, c2 * 64:(c2 + 1) * 64], hid[64:128, b, c2 * P:(c2 + 1) * P],
                                          ident[64:128, 64:128], start=True, stop=True)
                mm.then_inc(s["turned"].sem, 1)

            def step_hT(dve, s, v, prev, b):
                dve.wait_ge(s["turned"].sem, v(s["turned"]))
                if prev:
                    dve.wait_ge(s["down"].sem, prev(s["down"]))
                nc.vector.tensor_copy(hT[:, b, :, :], ps[:, 4 + b, 0:128].rearrange("p (a b) -> p a b", a=2))\
                    .then_inc(s["hT"].sem, 1)

            def step_down(pe, s, v, prev, b, wd):
                pe.wait_ge(s["hT"].sem, v(s["hT"]))
                if prev:
                    pe.wait_ge(s["rows"].sem, prev(s["rows"]))
                for k in range(4):
                    for j in range(4):
                        mm = nc.tensor.matmul(ps[j * CAP:(j + 1) * CAP, 6 + b, 0:256],
                                              hT[:, b, k % 2, (k // 2) * CAP:(k // 2 + 1) * CAP],
                                              wd[:, k, j * 256:(j + 1) * 256], start=(k == 0), stop=(k == 3))
                mm.then_inc(s["down"].sem, 1)

            def step_dest(dve, s, v, prev, b, stored_before):
                dve.wait_ge(s["xg"].sem, v(s["xg"]))
                if prev:
                    dve.wait_ge(s["rows"].sem, prev(s["rows"]))
                if stored_before is not None:
                    dve.wait_ge(y_st[b].sem, stored_before)
                nc.vector.tensor_copy(wcol[:, b:b + 1], xg[:, b, KD * CAP + 1:KD * CAP + 2])
                nc.vector.tensor_tensor(dest[:, b:b + 1].bitcast(I32), xg[:, b, KD * CAP:KD * CAP + 1],
                                        cst[:, C_JCOL:C_JCOL + 1], ALU.add).then_inc(s["dest"].sem, 1)

            def step_rows(dve, s, v, b, stored_before):
                dve.wait_ge(s["down"].sem, v(s["down"]))
                dve.wait_ge(s["dest"].sem, v(s["dest"]))
                if stored_before is not None:
                    dve.wait_ge(y_st[b].sem, stored_before)
                nc.vector.tensor_scalar(rows[:, b, :], ps[:, 6 + b, 0:256], wcol[:, b:b + 1], None, ALU.mult)\
                    .then_inc(s["rows"].sem, 1)

            def step_store(pool, s, v, b, last_row, step):
                pool.wait_ge(s["dest"].sem, v(s["dest"]))
                pool.wait_ge(s["rows"].sem, v(s["rows"]))
                if not (isinstance(step, int) and step == 0):
                    pool.wait_ge(ticked[layer].sem, step)
                nc.gpsimd.tensor_tensor(tick, cst[0:1, 0:1], cst[0:1, 0:1], ALU.mult).then_inc(ticked[layer].sem, 1)
                nc.gpsimd.indirect_dma_start(moe_rows[layer], bass.IndirectOffsetOnAxis(
                    ap=dest[:, b:b + 1].bitcast(I32), axis=0), rows[:, b, :], None, bounds_check=last_row,
                    oob_is_err=False).then_inc(y_st[b].sem, 16)

            def pair_view(pair, b):
                e = 2 * pair + b
                v = lambda s: s.at(e + 1)
                prev = None if isinstance(pair, int) and pair == 0 else (lambda s: s.at(e - 1))
                before = None if prev is None else 16 * pair
                return e, v, prev, before

            def next_view(pair, b):
                return pair_view(pair, 1) if b == 0 else pair_view(pair + 1, 0)

            def over_view(z):
                return lambda s: s.at(z + 1)

            for e in (NE - 2, NE - 1):
                ring.release(first + 3 * e, m["gateup"], e + 1)
                ring.release(first + 3 * e + 1, m["gateup"], e + 1)
                ring.release(first + 3 * e + 2, m["down"], e + 1)
            wf = {b: [ring.rows8(first + 3 * b), ring.rows8(first + 3 * b + 1), ring.rows4(first + 3 * b + 2)]
                  for b in range(2)}

            with nc.Block() as block:
                @block.sync
                def _(sp):
                    sp.dma_start(wr[:, :, 0:NG], t["moe_w_group"][layer].rearrange("(k p) n -> p k n", p=P))\
                        .then_inc(router_loaded.sem, 16)
                    sp.dma_start(wr[:, :, NG:NG + NE], t["moe_w_expert"][layer].rearrange("(k p) n -> p k n", p=P))\
                        .then_inc(router_loaded.sem, 16)
                    sp_ln_params(sp, lnp, lnp_g, lnp_b)
                    with sp.Fori(1, NE // 2) as pair:
                        for b in range(2):
                            e = 2 * pair + b
                            for part, name in enumerate(("moe_w_gate", "moe_w_up", "moe_w_down")):
                                c = first + 3 * b + part
                                w = t[name][layer, bass.ds(e, 1)]
                                if part == 2:
                                    src, dst = w.rearrange("a (k p) n -> p (a k) n", p=P), ring.rows4(c)
                                else:
                                    src, dst = w.rearrange("a (k p) n -> p (a k) n", p=P), ring.rows8(c)
                                done = m["down"] if part == 2 else m["gateup"]
                                sp.wait_ge(done.sem, done.at(e - 1))
                                sp.dma_start(dst, src).then_inc(ring.loaded[c % RING_SLOTS], 16)
                    ring.issued = first + 3 * NE
                    sp.wait_ge(route_dve.sem, route_dve.at(7))
                    crowded = sp.value_load(cnti[0:1, 0:1], min_val=0, max_val=SEQ)
                    with sp.If(crowded > CAP):
                        for part in range(3):
                            done = m["down"] if part == 2 else m["gateup"]
                            sp.wait_ge(done.sem, done.at(NE))
                        with sp.Fori(1, SEQ // CAP) as r:
                            with sp.Fori(0, NE) as e:
                                z = (r - 1) * NE + e
                                sp.wait_ge(y_st[0].sem, 16 * (NE // 2) + 16 * z)
                                for part, name in enumerate(("moe_w_gate", "moe_w_up", "moe_w_down")):
                                    w = t[name][layer, bass.ds(e, 1)].rearrange("a (k p) n -> p (a k) n", p=P)
                                    dst = ring.rows4(first + part) if part == 2 else ring.rows8(first + part)
                                    sp.dma_start(dst, w).then_inc(o["loaded"].sem, 16)
                        sp.wait_ge(y_st[0].sem, 16 * (NE // 2) + 16 * (SEQ // CAP - 1) * NE)
                    for b in range(2):
                        sp.wait_ge(y_st[b].sem, 16 * (NE // 2))
                    for tt in range(TT):
                        sp.dma_start(pairs[:, tt, :, :].rearrange("p j d -> p (j d)"),
                                     moe_rows[layer][8 * P * tt:8 * P * (tt + 1), :].rearrange(
                                         "(p j) d -> p (j d)", p=P)).then_inc(pairs_loaded.sem, 16)
                    ring.issue(sp, first + 3 * NE + RING_SLOTS)

                @block.tensor
                def _(pe):
                    pe_turn(pe, h)
                    pe.wait_ge(router_loaded.sem, router_loaded.at(32))
                    pe.wait_ge(turned_copied.sem, turned_copied.at(4))
                    for tt in range(TT):
                        for k in range(KD):
                            mm = nc.tensor.matmul(ps[:, 4, tt * 36:(tt + 1) * 36], xT[:, k, tt * P:(tt + 1) * P],
                                                  wr[:, k, :], start=(k == 0), stop=(k == KD - 1))
                    mm.then_inc(route_pe.sem, 1)
                    pe.wait_ge(route_dve.sem, route_dve.at(5))
                    nc.tensor.matmul(ps[:, 5, 0:NE], striu, both[:, 0, :], start=True, stop=True)
                    nc.tensor.matmul(ps[:, 5, NE:2 * NE], striu, both[:, 1, :], start=True, stop=False)
                    nc.tensor.matmul(ps[:, 5, NE:2 * NE], ones, both[:, 0, :], start=False, stop=True)
                    nc.tensor.matmul(ps[:, 5, 64:64 + NE], ones, both[:, 0, :], start=True, stop=False)
                    nc.tensor.matmul(ps[:, 5, 64:64 + NE], ones, both[:, 1, :], start=False, stop=True)\
                        .then_inc(route_pe.sem, 1)
                    pe.wait_ge(route_dve.sem, route_dve.at(7))

                    def expert(pair, b):
                        e, v, prev, before = pair_view(pair, b)
                        for part in range(2):
                            ring.arrived(pe, first + 3 * b + part, pair)
                        step_gateup(pe, m, v, prev, b, wf[b][0], wf[b][1])
                        if not (isinstance(pair, int) and pair == NE // 2):
                            e1, v1, prev1, _ = next_view(pair, b)
                            step_pick(pe, m, v1, prev1, 1 - b, e1)
                        step_turn(pe, m, v, prev, b)
                        ring.arrived(pe, first + 3 * b + 2, pair)
                        step_down(pe, m, v, prev, b, wf[b][2])

                    step_pick(pe, m, lambda s: s.at(1), None, 0, 0)
                    expert(0, 0)
                    expert(0, 1)
                    with pe.Fori(1, NE // 2) as pair:
                        expert(pair, 0)
                        expert(pair, 1)
                    crowded = pe.value_load(cnti[0:1, 0:1], min_val=0, max_val=SEQ)
                    with pe.If(crowded > CAP):
                        with pe.Fori(1, SEQ // CAP) as r:
                            with pe.Fori(0, NE) as e:
                                z = (r - 1) * NE + e
                                v = over_view(z)
                                pe.wait_ge(o["loaded"].sem, 48 * (z + 1))
                                step_pick(pe, o, v, None, 0, e)
                                step_gateup(pe, o, v, None, 0, wf[0][0], wf[0][1])
                                step_turn(pe, o, v, None, 0)
                                step_down(pe, o, v, None, 0, wf[0][2])

                @block.scalar
                def _(act):
                    for tt in range(TT):
                        act.wait_ge(route_dve.sem, route_dve.at(1 + 2 * tt))
                        nc.scalar.activation(t8[:, tt, 0, 0:NG], lg[:, tt, 0:NG], ACT.Exp, bias=r1[:, tt, 1:2],
                                             accum_out=r1[:, tt, 2:3]).then_inc(route_act.sem, 1)
                        act.wait_ge(route_dve.sem, route_dve.at(2 + 2 * tt))
                        nc.scalar.activation(t8[:, tt, 1, :], esel[:, tt, :], ACT.Exp, bias=r1[:, tt, 4:5],
                                             accum_out=r1[:, tt, 5:6]).then_inc(route_act.sem, 1)

                    def expert(pair, b):
                        e, v, prev, before = pair_view(pair, b)
                        step_silu(act, m, v, prev, b)
                        e1, v1, prev1, _ = next_view(pair, b)
                        step_xg(act, m, v1, prev1, 1 - b)

                    step_xg(act, m, lambda s: s.at(1), None, 0)
                    expert(0, 0)
                    expert(0, 1)
                    with act.Fori(1, NE // 2) as pair:
                        expert(pair, 0)
                        expert(pair, 1)
                    act.wait_ge(route_dve.sem, route_dve.at(7))
                    crowded = act.value_load(cnti[0:1, 0:1], min_val=0, max_val=SEQ)
                    with act.If(crowded > CAP):
                        with act.Fori(1, SEQ // CAP) as r:
                            with act.Fori(0, NE) as e:
                                v = over_view((r - 1) * NE + e)
                                step_xg(act, o, v, None, 0)
                                step_silu(act, o, v, None, 0)

                @block.gpsimd
                def _(pool):
                    last_row = pool.to_reg(8 * SEQ - 1)
                    for b in range(2):
                        step_store(pool, m, pair_view(0, b)[1], b, last_row, b)
                    with pool.Fori(1, NE // 2) as pair:
                        for b in range(2):
                            step_store(pool, m, pair_view(pair, b)[1], b, last_row, 2 * pair + b)
                    pool.wait_ge(route_dve.sem, route_dve.at(7))
                    crowded = pool.value_load(cnti[0:1, 0:1], min_val=0, max_val=SEQ)
                    with pool.If(crowded > CAP):
                        with pool.Fori(1, SEQ // CAP) as r:
                            with pool.Fori(0, NE) as e:
                                step_store(pool, o, over_view((r - 1) * NE + e), 0, last_row, r * NE + e)

                @block.vector
                def _(dve):
                    dve_turn(dve, xT)
                    V(nc.vector.memset(t8, -1.0))
                    V(nc.vector.memset(pos1, 0.0))
                    V(nc.vector.memset(info.rearrange("p a b c -> p (a b c)"), 0.0))
                    dve.wait_ge(route_pe.sem, route_pe.at(1))
                    V(nc.vector.tensor_copy(lg, ps[:, 4, 0:72].rearrange("p (a b) -> p a b", a=TT)))
                    for tt in range(TT):
                        top, at = t8[:, tt, 2, :], t8[:, tt, 3, :].bitcast(U32)
                        ptop, pat = t8[:, tt, 4, :], t8[:, tt, 5, :].bitcast(U32)
                        c = [r1[:, tt, i:i + 1] for i in range(16)]
                        V(nc.vector.reduce_max(c[0], lg[:, tt, 0:NG], AX_X))
                        nc.vector.tensor_scalar(c[1], c[0], -1.0, None, ALU.mult).then_inc(route_dve.sem, 1)
                        dve.wait_ge(route_act.sem, route_act.at(2 * tt + 1))
                        V(nc.vector.reciprocal(c[3], c[2]))
                        V(nc.vector.tensor_scalar(t8[:, tt, 0, 0:NG], t8[:, tt, 0, 0:NG], c[3], None, ALU.mult))
                        V(nc.vector.max(top, t8[:, tt, 0, :]))
                        V(nc.vector.max_index(at, top, t8[:, tt, 0, :]))
                        V(nc.vector.tensor_copy(c[6], at[:, 0:1]))
                        V(nc.vector.tensor_scalar(c[7], c[6], 0.0, None, ALU.is_equal))
                        V(nc.vector.tensor_scalar(esel[:, tt, :], lg[:, tt, NG:NG + EG], c[7], None, ALU.mult))
                        for g in range(1, NG):
                            V(nc.vector.tensor_scalar(c[7], c[6], float(g), None, ALU.is_equal))
                            V(nc.vector.scalar_tensor_tensor(esel[:, tt, :], lg[:, tt, NG + g * EG:NG + (g + 1) * EG],
                                                             c[7], esel[:, tt, :], ALU.mult, ALU.add))
                        V(nc.vector.reduce_max(c[8], esel[:, tt, :], AX_X))
                        nc.vector.tensor_scalar(c[4], c[8], -1.0, None, ALU.mult).then_inc(route_dve.sem, 1)
                        dve.wait_ge(route_act.sem, route_act.at(2 * tt + 2))
                        V(nc.vector.reciprocal(c[9], c[5]))
                        V(nc.vector.tensor_scalar(t8[:, tt, 1, :], t8[:, tt, 1, :], c[9], None, ALU.mult))
                        V(nc.vector.max(ptop, t8[:, tt, 1, :]))
                        V(nc.vector.max_index(pat, ptop, t8[:, tt, 1, :]))
                        V(nc.vector.tensor_tensor(c[10], ptop[:, 0:1], ptop[:, 1:2], ALU.add))
                        V(nc.vector.reciprocal(c[11], c[10]))
                        V(nc.vector.tensor_tensor(c[11], c[11], top[:, 0:1], ALU.mult))
                        V(nc.vector.tensor_scalar(r1[:, tt, 12:14], ptop[:, 0:2], c[11], None, ALU.mult))
                        V(nc.vector.tensor_copy(r1[:, tt, 14:16], pat[:, 0:2]))
                        V(nc.vector.tensor_scalar(c[6], c[6], float(EG), None, ALU.mult))
                        V(nc.vector.tensor_scalar(r1[:, tt, 14:16], r1[:, tt, 14:16], c[6], None, ALU.add))
                        for j in range(2):
                            V(nc.vector.tensor_scalar(chosen[:, tt, j, :], cst[:, C_IOTA:C_IOTA + NE], c[14 + j], None,
                                                      ALU.is_equal))
                        V(nc.vector.tensor_tensor(both[:, tt, :], chosen[:, tt, 0, :], chosen[:, tt, 1, :], ALU.add))
                        V(nc.vector.tensor_scalar(info[:, tt, 0:NE, 1], chosen[:, tt, 0, :], c[12], None, ALU.mult))
                        V(nc.vector.scalar_tensor_tensor(info[:, tt, 0:NE, 1], chosen[:, tt, 1, :], c[13],
                                                         info[:, tt, 0:NE, 1], ALU.mult, ALU.add))
                        V(nc.vector.tensor_scalar(info[:, tt, 0:NE, 0], both[:, tt, :],
                                                  cst[:, C_TOK8 + tt:C_TOK8 + tt + 1], None, ALU.mult))
                        V(nc.vector.scalar_tensor_tensor(info[:, tt, 0:NE, 0], chosen[:, tt, 1, :], 4.0,
                                                         info[:, tt, 0:NE, 0], ALU.mult, ALU.add))
                    nc.vector.memset(cnt[:, 1:2], 0.0).then_inc(route_dve.sem, 1)
                    dve.wait_ge(route_pe.sem, route_pe.at(2))
                    for tt in range(TT):
                        V(nc.vector.scalar_tensor_tensor(pos1[:, tt, 0:NE], ps[:, 5, tt * NE:(tt + 1) * NE], 1.0,
                                                         both[:, tt, :], ALU.add, ALU.mult))
                    nc.vector.reduce_max(cnt[:, 0:1], ps[:, 5, 64:64 + NE], AX_X).then_inc(route_dve.sem, 1)
                    dve.wait_ge(route_dve.sem, route_dve.at(6))
                    nc.vector.tensor_copy(cnti[:, 0:1], cnt[:, 0:1]).then_inc(route_dve.sem, 1)

                    def expert(pair, b):
                        e, v, prev, before = pair_view(pair, b)
                        e1, v1, prev1, before1 = next_view(pair, b)
                        step_slots(dve, m, v1, prev1, 1 - b, e1, pos1)
                        step_hidden(dve, m, v, prev, b)
                        step_dest(dve, m, v1, prev1, 1 - b, before1)
                        step_hT(dve, m, v, prev, b)
                        step_rows(dve, m, v, b, before)

                    step_slots(dve, m, lambda s: s.at(1), None, 0, 0, pos1)
                    step_dest(dve, m, lambda s: s.at(1), None, 0, None)
                    expert(0, 0)
                    expert(0, 1)
                    with dve.Fori(1, NE // 2) as pair:
                        expert(pair, 0)
                        expert(pair, 1)
                    crowded = dve.value_load(cnti[0:1, 0:1], min_val=0, max_val=SEQ)
                    with dve.If(crowded > CAP):
                        with dve.Fori(1, SEQ // CAP) as r:
                            nc.vector.tensor_scalar(pos1[:, :, 0:NE], pos1[:, :, 0:NE], -float(CAP), None, ALU.add)\
                                .then_inc(o["shifted"].sem, 1)
                            with dve.Fori(0, NE) as e:
                                z = (r - 1) * NE + e
                                v = over_view(z)
                                dve.wait_ge(o["loaded"].sem, 48 * (z + 1))
                                dve.wait_ge(o["shifted"].sem, r)
                                step_slots(dve, o, v, None, 0, e, pos1)
                                step_dest(dve, o, v, None, 0, None)
                                step_hidden(dve, o, v, None, 0)
                                step_hT(dve, o, v, None, 0)
                                step_rows(dve, o, v, 0, None)
                    dve.wait_ge(pairs_loaded.sem, pairs_loaded.at(32))
                    for tt in range(TT):
                        V(nc.vector.scalar_tensor_tensor(h[:, tt, :], h[:, tt, :], ALPHA, pairs[:, tt, 0, :],
                                                         ALU.mult, ALU.add))
                    for tt in range(TT):
                        V(nc.vector.tensor_tensor(h[:, tt, :], h[:, tt, :], pairs[:, tt, 1, :], ALU.add))
                    dve_layer_norm(dve, lnp)

            turn_done()
            for s, n in ((route_pe, 2), (route_act, 4), (route_dve, 7), (router_loaded, 32), (pairs_loaded, 32),
                         (ln_loaded, 32)):
                s.advance(n)
            for name, s in m.items():
                s.advance(NE + 1 if name in ("slots", "picked", "xg", "dest") else NE)

        moe(0, t["ln_ffn_g"][0], t["ln_ffn_b"][0])

        projected, projected_copied = sem("projected"), sem("projected_copied")
        jobs_turned, jobs_copied = sem("jobs_turned"), sem("jobs_copied")

        def pe_project(pe, chunks):
            for q, c in enumerate(chunks):
                n_cols = ring.chunks[c].shape[2]
                w = ring.rows8(c, n_cols)
                ring.arrived(pe, c)
                for tt in range(TT):
                    n = 2 * q + tt
                    if n >= 4:
                        pe.wait_ge(projected_copied.sem, projected_copied.at(n - 3))
                    for k in range(KD):
                        mm = nc.tensor.matmul(ps[:, n % 4, 0:n_cols], xT_att[:, k, tt * P:(tt + 1) * P], w[:, k, :],
                                              start=(k == 0), stop=(k == KD - 1))
                    mm.then_inc(projected.sem, 1)

        def act_project(act, chunks, dst):
            for q, c in enumerate(chunks):
                n_cols = ring.chunks[c].shape[2]
                for tt in range(TT):
                    n = 2 * q + tt
                    act.wait_ge(projected.sem, projected.at(n + 1))
                    nc.scalar.activation(dst[:, tt, q * 512:q * 512 + n_cols], ps[:, n % 4, 0:n_cols], ACT.Copy)\
                        .then_inc(projected_copied.sem, 1)

        def release_projected(chunks):
            for q, c in enumerate(chunks):
                ring.release(c, projected, 2 * q + 2)

        def project_done(chunks):
            projected.advance(2 * len(chunks))
            projected_copied.advance(2 * len(chunks))

        def pe_jobs(pe, jobs, first=0):
            for m, (blocks, dst, gain) in enumerate(jobs, first):
                if m >= 4:
                    pe.wait_ge(jobs_copied.sem, jobs_copied.at(m - 3))
                n_rows = blocks[0].shape[1]
                for i, src in enumerate(blocks):
                    mm = nc.tensor.transpose(ps[0:n_rows, m % 4, i * P:(i + 1) * P], src, ident)
                mm.then_inc(jobs_turned.sem, 1)

        def dve_jobs(dve, jobs, first=0):
            for m, (blocks, dst, gain) in enumerate(jobs, first):
                dve.wait_ge(jobs_turned.sem, jobs_turned.at(m + 1))
                src = ps[0:blocks[0].shape[1], m % 4, 0:len(blocks) * P]
                if len(dst.shape) == 3:
                    src = src.rearrange("p (a b) -> p a b", a=dst.shape[1])
                if gain is None:
                    ins = nc.vector.tensor_copy(dst, src)
                else:
                    ins = nc.vector.tensor_scalar(dst, src, gain, None, ALU.mult)
                ins.then_inc(jobs_copied.sem, 1)

        def jobs_done(n):
            jobs_turned.advance(n)
            jobs_copied.advance(n)

        def rope(x, heads, half, cos, sin, tmp):
            r1, r2 = x[:, :, 0:half], x[:, :, half:2 * half]
            c = cos.unsqueeze(1).to_broadcast([P, heads, half])
            s = sin.unsqueeze(1).to_broadcast([P, heads, half])
            t = [tmp[:, i * heads * half:(i + 1) * heads * half].rearrange("p (a b) -> p a b", a=heads)
                 for i in range(4)]
            nc.vector.tensor_tensor(t[0], r1, c, ALU.mult)
            nc.vector.tensor_tensor(t[1], r2, s, ALU.mult)
            nc.vector.tensor_tensor(t[2], r2, c, ALU.mult)
            V(nc.vector.tensor_tensor(t[3], r1, s, ALU.mult))
            nc.vector.tensor_tensor(r1, t[0], t[1], ALU.subtract)
            V(nc.vector.tensor_tensor(r2, t[2], t[3], ALU.add))

        U = {n: sem("att_" + n) for n in ("scores", "masked", "exps", "probs", "turned", "probsT", "out", "copied")}
        st = tiny[:, 130:170]
        st_max = st[:, 0:4].rearrange("p (a b) -> p a b", a=2)
        st_nmax = st[:, 4:8].rearrange("p (a b) -> p a b", a=2)
        st_sum = st[:, 8:12].rearrange("p (a b) -> p a b", a=2)
        st_inv = st[:, 12:16].rearrange("p (a b) -> p a b", a=2)
        neg_lam = st[:, 16:17]

        class Unit:

            def __init__(self, i, q, k, mask, times, scale, v, pair):
                self.i, self.q, self.k, self.mask, self.times = i, q, k, mask, times
                self.scale, self.v, self.pair, self.kv = scale, v, pair, (i + 1) * P

        def pe_units(pe, units, pT, probs, joined):
            def scores(n):
                u, b = units[n], n % 2
                if n >= 2:
                    pe.wait_ge(U["masked"].sem, U["masked"].at(n - 1))
                for c in range(2):
                    mm = nc.tensor.matmul(ps[:, 2 * b + c, 0:u.kv], u.q[c], u.k[c], start=True, stop=True)
                mm.then_inc(U["scores"].sem, 1)

            def turn(n):
                u, b = units[n], n % 2
                pe.wait_ge(U["probs"].sem, U["probs"].at(n + 1))
                if n >= 2:
                    pe.wait_ge(U["probsT"].sem, U["probsT"].at(n - 1))
                nk = u.kv // P
                for c in range(1 if joined is not None else 2):
                    src = joined[:, b, :] if joined is not None else probs[:, b, c, :]
                    for kt in range(nk):
                        at = (c * nk + kt) * P
                        mm = nc.tensor.transpose(ps[:, 4 + b, at:at + P], src[:, kt * P:(kt + 1) * P], ident)
                mm.then_inc(U["turned"].sem, 1)

            def values(n):
                u, b = units[n], n % 2
                pe.wait_ge(U["probsT"].sem, U["probsT"].at(n + 1))
                if n >= 2:
                    pe.wait_ge(U["copied"].sem, U["copied"].at(n - 1))
                nk = u.kv // P
                if joined is not None:
                    for kt in range(nk):
                        mm = nc.tensor.matmul(ps[:, 6 + b, 0:P], pT[:, b, kt * P:(kt + 1) * P], u.v(0, kt),
                                              start=(kt == 0), stop=(kt == nk - 1))
                else:
                    for c in range(2):
                        for kt in range(nk):
                            at = (c * nk + kt) * P
                            mm = nc.tensor.matmul(ps[c * HD:(c + 1) * HD, 6 + b, 0:P], u.v(c, kt), pT[:, b, at:at + P],
                                                  start=(kt == 0), stop=(kt == nk - 1))
                mm.then_inc(U["out"].sem, 1)

            N = len(units)
            scores(0)
            scores(1)
            for n in range(N):
                turn(n)
                if n + 2 < N:
                    scores(n + 2)
                if n:
                    values(n - 1)
            values(N - 1)

        def act_units(act, units, sm, probs, pT, joined, copy_out):
            def exps(n):
                u, b = units[n], n % 2
                act.wait_ge(U["masked"].sem, U["masked"].at(n + 1))
                if n >= 2:
                    act.wait_ge(U["turned"].sem, U["turned"].at(n - 1))
                for c in range(2):
                    ins = nc.scalar.activation(probs[:, b, c, 0:u.kv], sm[:, b, c, 0:u.kv], ACT.Exp,
                                               bias=st_nmax[:, b, c:c + 1], scale=u.scale,
                                               accum_out=st_sum[:, b, c:c + 1])
                ins.then_inc(U["exps"].sem, 1)

            def copy_turned(n):
                u, b = units[n], n % 2
                act.wait_ge(U["turned"].sem, U["turned"].at(n + 1))
                if n >= 2:
                    act.wait_ge(U["out"].sem, U["out"].at(n - 1))
                w = u.kv * (1 if joined is not None else 2)
                nc.scalar.activation(pT[:, b, 0:w], ps[:, 4 + b, 0:w], ACT.Copy).then_inc(U["probsT"].sem, 1)

            def outputs(n):
                act.wait_ge(U["out"].sem, U["out"].at(n + 1))
                copy_out(act, units[n], n).then_inc(U["copied"].sem, 1)

            N = len(units)
            exps(0)
            for n in range(N):
                if n + 1 < N:
                    exps(n + 1)
                copy_turned(n)
                if n:
                    outputs(n - 1)
            outputs(N - 1)

        def dve_units(dve, units, sm, probs, joined):
            def mask(n):
                u, b = units[n], n % 2
                dve.wait_ge(U["scores"].sem, U["scores"].at(n + 1))
                if n >= 2:
                    dve.wait_ge(U["exps"].sem, U["exps"].at(n - 1))
                V(nc.vector.tensor_tensor(sm[:, b, :, 0:u.kv], ps[:, 2 * b:2 * b + 2, 0:u.kv],
                                          u.mask.unsqueeze(1).to_broadcast([P, 2, u.kv]), ALU.add))
                V(nc.vector.reduce_max(st_max[:, b, :], sm[:, b, :, 0:u.kv], AX_X))
                nc.vector.tensor_scalar(st_nmax[:, b, :], st_max[:, b, :], -u.scale, None, ALU.mult)\
                    .then_inc(U["masked"].sem, 1)

            def normalise(n):
                u, b = units[n], n % 2
                dve.wait_ge(U["exps"].sem, U["exps"].at(n + 1))
                if u.times is not None:
                    for c in range(2):
                        ins = nc.vector.scalar_tensor_tensor(probs[:, b, c, 0:u.kv], probs[:, b, c, 0:u.kv], 1.0,
                                                             u.times, ALU.mult, ALU.mult,
                                                             accum_out=st_sum[:, b, c:c + 1])
                    V(ins)
                V(nc.vector.reciprocal(st_inv[:, b, :], st_sum[:, b, :]))
                if joined is not None:
                    if n >= 2:
                        dve.wait_ge(U["turned"].sem, U["turned"].at(n - 1))
                    nc.vector.tensor_scalar(st_inv[:, b, 1:2], st_inv[:, b, 1:2], neg_lam, None, ALU.mult)
                    V(nc.vector.tensor_scalar(joined[:, b, 0:u.kv], probs[:, b, 0, 0:u.kv], st_inv[:, b, 0:1], None,
                                              ALU.mult))
                    nc.vector.scalar_tensor_tensor(joined[:, b, 0:u.kv], probs[:, b, 1, 0:u.kv], st_inv[:, b, 1:2],
                                                   joined[:, b, 0:u.kv], ALU.mult, ALU.add)\
                        .then_inc(U["probs"].sem, 1)
                else:
                    nc.vector.tensor_tensor(probs[:, b, :, 0:u.kv], probs[:, b, :, 0:u.kv],
                                            bcast(st_inv[:, b, :], u.kv), ALU.mult).then_inc(U["probs"].sem, 1)

            N = len(units)
            mask(0)
            mask(1)
            for n in range(N):
                normalise(n)
                if n + 2 < N:
                    mask(n + 2)

        def units_done(n):
            for s in U.values():
                s.advance(n)

        caus = [cst[:, C_CAUS0:C_CAUS0 + P], cst[:, C_CAUS1:C_CAUS1 + SEQ]]

        AH = 8
        qkv = area(0, TT, 3 * D)
        xT_att = area(6144, KD, SEQ)
        oT = xT_att
        qkT = area(8192, 2, AH, SEQ)
        sm = area(12288, 2, 2, SEQ)
        probs = area(13312, 2, 2, SEQ)
        joined = area(14336, 2, SEQ)
        pT = area(14848, 2, SEQ)
        o_tok = area(15360, TT, AH, P)
        lam_rows = area(17408, 4, 64)
        lam_prod = area(17664, 2, 64)
        rt = area(17792, 200)
        posi = rt[:, 0:2].bitcast(I32)
        posf = rt[:, 2:4]
        ang, turns, red, cosr = rt[:, 4:20], rt[:, 20:36], rt[:, 36:52], rt[:, 52:68]
        sin_t, cos_t, over_t = rt[:, 68:84], rt[:, 84:100], rt[:, 100:116]
        lam_sum = rt[:, 116:118]
        subln = rt[:, 118:119]
        subln_s = rt[:, 119:120]
        ossq = rt[:, 120:136].rearrange("p (a b) -> p a b", a=TT)
        ov, orr, ot = rt[:, 136:152], rt[:, 152:168], rt[:, 168:184]
        rope_tmp = area(17992, 4 * 32 * 8)
        osq = area(19016, P)
        lnp = area(0, 2, D)
        att_loaded, tables, lam_ready, tables_dve, o_scaled, oT_ready = (
            sem("att_loaded"), sem("tables"), sem("lam_ready"), sem("tables_dve"), sem("o_scaled"), sem("oT_ready"))
        roped = sem("roped")
        release_projected(c_qkv)
        release_summed(c_wo)

        units = []
        for hh in range(AH):
            for i in range(TT):
                units.append(Unit(
                    i, [qkT[64 * c:64 * c + 64, 0, hh, i * P:(i + 1) * P] for c in range(2)],
                    [qkT[64 * c:64 * c + 64, 1, hh, 0:(i + 1) * P] for c in range(2)], caus[i], None, 64 ** -0.5,
                    lambda c, kt, hh=hh: qkv[:, kt, 2 * D + hh * P:2 * D + (hh + 1) * P], hh))
        head_jobs = [([qkv[:, tt, a * D + hh * P:a * D + (hh + 1) * P] for hh in (2 * hp, 2 * hp + 1)
                       for tt in range(TT)],
                      qkT[:, a, 2 * hp:2 * hp + 2, :].rearrange("p a b -> p (a b)"), None)
                     for a in range(2) for hp in range(4)]
        out_jobs = [([o_tok[:, tt, hh, :] for hh in (2 * hp, 2 * hp + 1) for tt in range(TT)],
                     oT[:, 2 * hp:2 * hp + 2, :].rearrange("p a b -> p (a b)"), subln_s) for hp in range(4)]
        with nc.Block() as block:
            @block.sync
            def _(sp):
                for i, name in enumerate(("attn_lam_q1", "attn_lam_k1", "attn_lam_q2", "attn_lam_k2")):
                    sp.dma_start(lam_rows[:, i, :], t[name][0].partition_broadcast(P)).then_inc(att_loaded.sem, 16)
                sp.dma_start(posi, t["positions"][0].rearrange("(a p) -> p a", p=P), allow_slow_non_contiguous=True).then_inc(att_loaded.sem, 16)
                sp.dma_start(subln, t["attn_subln_w"][0].rearrange("(p a) -> p a", a=1),
                             allow_slow_non_contiguous=True).then_inc(att_loaded.sem, 16)
                ring.issue(sp, c_qkv[-1] + 1 + RING_SLOTS)
                sp.wait_ge(U["copied"].sem, U["copied"].at(len(units)))
                sp_ln_params(sp, lnp, t["ln_mix_g"][1], t["ln_mix_b"][1])
                ring.issue(sp, c_wo[-1] + 1 + RING_SLOTS)

            @block.tensor
            def _(pe):
                pe_turn(pe, h)
                pe.wait_ge(turned_copied.sem, turned_copied.at(4))
                pe_project(pe, c_qkv)
                pe.wait_ge(projected_copied.sem, projected_copied.at(12))
                pe.wait_ge(roped.sem, 1)
                pe_jobs(pe, head_jobs)
                pe.wait_ge(jobs_copied.sem, jobs_copied.at(8))
                pe_units(pe, units, pT, probs, joined)
                pe.wait_ge(o_scaled.sem, 1)
                pe_jobs(pe, out_jobs, 8)
                pe.wait_ge(jobs_copied.sem, jobs_copied.at(12))
                pe_sum_chunks(pe, c_wo, lambda k, tt: oT[:, k, tt * P:(tt + 1) * P])

            @block.scalar
            def _(act):
                act.wait_ge(tables.sem, 1)
                nc.scalar.activation(sin_t, red, ACT.Sin)
                nc.scalar.activation(cos_t, cosr, ACT.Sin).then_inc(tables_dve.sem, 1)
                act.wait_ge(tables.sem, 2)
                nc.scalar.activation(lam_sum, lam_sum, ACT.Exp).then_inc(tables_dve.sem, 1)
                act_project(act, c_qkv, qkv)

                def copy_out(act, u, n):
                    o = o_tok[:, u.i, u.pair, :]
                    nc.scalar.activation(o, ps[:, 6 + n % 2, 0:P], ACT.Copy)
                    if n:
                        act.wait_ge(U["copied"].sem, U["copied"].at(n))
                    return nc.scalar.activation(osq, ps[:, 6 + n % 2, 0:P], ACT.Square,
                                                accum_out=ossq[:, u.i, u.pair:u.pair + 1])

                act_units(act, units, sm, probs, pT, joined, copy_out)

            @block.vector
            def _(dve):
                dve_turn(dve, xT_att)
                dve.wait_ge(att_loaded.sem, 6 * 16)
                V(nc.vector.tensor_copy(posf, posi))
                for tt in range(TT):
                    V(nc.vector.tensor_scalar(ang[:, 8 * tt:8 * tt + 8], cst[:, C_INVF:C_INVF + 8], posf[:, tt:tt + 1],
                                              None, ALU.mult))
                V(nc.vector.tensor_scalar(turns, ang, 1 / TWO_PI, ROUND, ALU.mult, ALU.add))
                V(nc.vector.tensor_scalar(turns, turns, ROUND, None, ALU.subtract))
                V(nc.vector.scalar_tensor_tensor(red, turns, -6.28125, ang, ALU.mult, ALU.add))
                V(nc.vector.scalar_tensor_tensor(red, turns, -(TWO_PI - 6.28125), red, ALU.mult, ALU.add))
                V(nc.vector.tensor_scalar(cosr, red, TWO_PI / 4, None, ALU.add))
                V(nc.vector.tensor_scalar(over_t, cosr, TWO_PI / 2, -TWO_PI, ALU.is_gt, ALU.mult))
                V(nc.vector.tensor_tensor(cosr, cosr, over_t, ALU.add))
                V(nc.vector.tensor_scalar(cosr, cosr, 3.1415925, -3.1415925, ALU.min, ALU.max))
                nc.vector.tensor_scalar(red, red, 3.1415925, -3.1415925, ALU.min, ALU.max).then_inc(tables.sem, 1)
                V(nc.vector.tensor_tensor(lam_prod, lam_rows[:, 0:4:2, :], lam_rows[:, 1:4:2, :], ALU.mult))
                nc.vector.reduce_sum(lam_sum, lam_prod, AX_X).then_inc(tables.sem, 1)
                dve.wait_ge(tables_dve.sem, 2)
                V(nc.vector.tensor_tensor(neg_lam, lam_sum[:, 1:2], lam_sum[:, 0:1], ALU.subtract))
                V(nc.vector.tensor_scalar(neg_lam, neg_lam, -LAMBDA_INIT, None, ALU.add))
                V(nc.vector.tensor_scalar(subln_s, subln, 1.0 - LAMBDA_INIT, None, ALU.mult))
                dve.wait_ge(projected_copied.sem, projected_copied.at(8))
                for tt in range(TT):
                    rope(qkv[:, tt, 0:2 * D].rearrange("p (a b) -> p a b", b=64), 32, 8,
                         cos_t[:, 8 * tt:8 * tt + 8], sin_t[:, 8 * tt:8 * tt + 8], rope_tmp)
                nc.vector.memset(ot, 0.0).then_inc(roped.sem, 1)
                dve_jobs(dve, head_jobs)
                dve_units(dve, units, sm, probs, joined)
                dve.wait_ge(U["copied"].sem, U["copied"].at(len(units)))
                V(nc.vector.tensor_scalar(ov, ossq.rearrange("p a b -> p (a b)"), 1.0 / P, EPS, ALU.mult, ALU.add))
                rsqrt(orr, ov, ot)
                for tt in range(TT):
                    ins = nc.vector.tensor_tensor(o_tok[:, tt, :, :], o_tok[:, tt, :, :],
                                                  bcast(orr[:, 8 * tt:8 * tt + 8], P), ALU.mult)
                ins.then_inc(o_scaled.sem, 1)
                dve_jobs(dve, out_jobs, 8)
                dve.wait_ge(summed.sem, summed.at(len(c_wo)))
                for tt in range(TT):
                    for half in range(2):
                        hs = h[:, tt, half * 512:(half + 1) * 512]
                        ins = nc.vector.scalar_tensor_tensor(hs, hs, ALPHA, ps[:, 4 + 2 * tt + half, :], ALU.mult,
                                                             ALU.add)
                V(ins)
                dve_layer_norm(dve, lnp)

        turn_done()
        project_done(c_qkv)
        jobs_done(12)
        units_done(len(units))
        summed.advance(len(c_wo))
        ln_loaded.advance(32)

        moe(1, t["ln_ffn_g"][1], t["ln_ffn_b"][1])

        TOPK = min(256, SEQ // 4)
        LH, DH, SH, IH = 4, 8, 4, 8
        Z_KV, Z_PE, Z_DIL, Z_DSA, Z_IDX, Z_W = 256, 384, 416, 1952, 2720, 3008
        TAKEN = -3e38
        zz = area(0, TT, N_IN2)
        xT_att = area(6032, KD, SEQ)
        latT = area(6032, 2, LH, SEQ)
        tn = area(8080, TT, D)
        dilT = area(8080, 2, 4, SEQ)
        rtmp = area(8080, 4 * 16 * 8)
        mixT = area(10128, KD, SEQ)
        cn = area(10128, TT, 384)
        cT = area(10896, 3, SEQ)
        kidx4 = area(11664, TT, P)
        qkm = area(12176, TT, 2, LH, 96)
        kvb = area(13712, TT, 512)
        dsaT = area(14736, 2, 2, SEQ)
        idxT = area(15760, 3, SEQ)
        sm2, probs2, pT2 = area(16528, 2, 2, SEQ), area(17552, 2, 2, SEQ), area(18576, 2, 512)
        w_uq, w_ukv = area(16528, 2, 384), area(17296, 512)
        prm2 = area(17808, 2, P)
        best = area(18064, 2, 8)
        work = area(18576, 2, SEQ)
        dsa_mask = area(19600, 2, SEQ)
        idx_terms = zz[:, :, Z_DIL:Z_DIL + 1024].rearrange("p a (m k) -> p a m k", m=4)
        rms_s, rms_v, rms_r, rms_t = tiny[:, 170:176], tiny[:, 176:182], tiny[:, 182:188], tiny[:, 188:194]
        w_idx = tiny[:, 194:210].rearrange("p (a b) -> p a b", a=TT)
        taps2 = [pcol[:, 0:44], pcol[:, 44:88], pcol[:, 107:151]]
        bias2 = pcol[:, 151:195]
        g_att, g_mlp, g_ql, g_kvl = pcol[:, 88:96], pcol[:, 96:104], pcol[:, 104:106], pcol[:, 106:107]

        squared, scaled, small_loaded, lat_squared, lat_ready, lat_copied = (
            sem("squared"), sem("scaled"), sem("small_loaded"), sem("lat_squared"), sem("lat_ready"), sem("lat_copied"))
        params2_turned, params2_copied = sem("params2_turned"), sem("params2_copied")
        ready2, idx_scores, idx_read = sem("ready2"), sem("idx_scores"), sem("idx_read")
        dsa_masked = sem("dsa_masked")
        up_ready, up_begun, up_summed, gate_done, up_done = (sem("up_ready"), sem("up_begun"), sem("up_summed"),
                                                             sem("gate_done"), sem("up_done"))
        final_loaded, final_stored, final_done = sem("final_loaded"), sem("final_stored"), sem("final_done")

        def act_squares(act, junk):
            for tt in range(TT):
                A(nc.scalar.activation(junk[:, tt, :], h[:, tt, :], ACT.Square, accum_out=rms_s[:, tt:tt + 1]))
            nc.scalar.activation(rms_v[:, 2:3], rms_s[:, 0:1], ACT.Copy).then_inc(squared.sem, 1)

        def dve_scale(dve, dst):
            dve.wait_ge(squared.sem, squared.at(1))
            V(nc.vector.tensor_scalar(rms_v[:, 0:2], rms_s[:, 0:2], 1.0 / D, EPS2, ALU.mult, ALU.add))
            rsqrt(rms_r[:, 0:2], rms_v[:, 0:2], rms_t[:, 0:2])
            for tt in range(TT):
                ins = nc.vector.tensor_scalar(dst[:, tt, :], h[:, tt, :], rms_r[:, tt:tt + 1], None, ALU.mult)
            ins.then_inc(scaled.sem, 1)

        def attention_layer(l):
            release_projected(c_in2[l])
            release_summed(c_wo2[l])
            chunk_cols = [(tt, k) for tt in range(TT) for k in range(KD)]
            lat_jobs = [([cn[:, tt, i * P:(i + 1) * P] for tt in range(TT)], cT[:, i, :],
                         g_ql[:, i:i + 1] if i < 2 else g_kvl) for i in range(3)]
            head_jobs = [([qkm[:, tt, a, hh, :] for hh in (2 * hp, 2 * hp + 1) for tt in range(TT)],
                          latT[0:96, a, 2 * hp:2 * hp + 2, :].rearrange("p a b -> p (a b)"), None)
                         for a in range(2) for hp in range(2)]
            head_jobs += [([zz[:, tt, Z_DIL + a * 512 + p2 * P:Z_DIL + a * 512 + (p2 + 1) * P]
                            for p2 in (2 * hp, 2 * hp + 1) for tt in range(TT)],
                           dilT[:, a, 2 * hp:2 * hp + 2, :].rearrange("p a b -> p (a b)"), None)
                          for a in range(2) for hp in range(2)]
            head_jobs += [([zz[:, tt, Z_DSA + a * 256 + p2 * P:Z_DSA + a * 256 + (p2 + 1) * P]
                            for p2 in range(2) for tt in range(TT)],
                           dsaT[:, a, :, :].rearrange("p a b -> p (a b)"), None) for a in range(2)]
            head_jobs += [([zz[:, tt, Z_IDX + p2 * P:Z_IDX + (p2 + 1) * P] for p2 in range(2) for tt in range(TT)],
                           idxT[:, 0:2, :].rearrange("p a b -> p (a b)"), None),
                          ([kidx4[:, tt, :] for tt in range(TT)], idxT[:, 2, :], None)]
            units = []
            for p2 in range(LH // 2):
                for i in range(TT):
                    units.append(Unit(
                        i, [latT[0:96, 0, 2 * p2 + c, i * P:(i + 1) * P] for c in range(2)],
                        [latT[0:96, 1, 2 * p2 + c, 0:(i + 1) * P] for c in range(2)], caus[i], None, 96 ** -0.5,
                        lambda c, kt, p2=p2: kvb[:, kt, (2 * p2 + c) * P + HD:(2 * p2 + c + 1) * P], p2))
            for p2 in range(DH // 2):
                for i in range(TT):
                    mask = caus[0] if i == 0 else cst[:, C_WIN1:C_WIN1 + SEQ]
                    times = cst[:, C_MUL0:C_MUL0 + P] if i == 0 else cst[:, C_MUL1:C_MUL1 + SEQ]
                    units.append(Unit(
                        i, [dilT[64 * c:64 * c + 64, 0, p2, i * P:(i + 1) * P] for c in range(2)],
                        [dilT[64 * c:64 * c + 64, 1, p2, 0:(i + 1) * P] for c in range(2)], mask, times, HD ** -0.5,
                        lambda c, kt, p2=p2: zz[:, kt, Z_DIL + 1024 + (2 * p2 + c) * HD:
                                                Z_DIL + 1024 + (2 * p2 + c + 1) * HD], 2 + p2))
            for p2 in range(SH // 2):
                for i in range(TT):
                    units.append(Unit(
                        i, [dsaT[64 * c:64 * c + 64, 0, p2, i * P:(i + 1) * P] for c in range(2)],
                        [dsaT[64 * c:64 * c + 64, 1, p2, 0:(i + 1) * P] for c in range(2)],
                        dsa_mask[:, i, 0:(i + 1) * P], None, HD ** -0.5,
                        lambda c, kt, p2=p2: zz[:, kt, Z_DSA + 512 + (2 * p2 + c) * HD:
                                                Z_DSA + 512 + (2 * p2 + c + 1) * HD], 6 + p2))
            n_units = len(units)

            def tables_of(tt):
                out, col = [], C_ROPE + 56 * tt
                for half in (16, 8, 4):
                    out.append((cst[:, col:col + half], cst[:, col + half:col + 2 * half]))
                    col += 2 * half
                return out

            with nc.Block() as block:
                @block.sync
                def _(sp):
                    rows = [(0, 0, t["conv_w_2"][l, 0:2].rearrange("j (f p) -> (j f) p", p=P)),
                            (0, 88, t["g_attn_2"][l].rearrange("(f p) -> f p", p=P)),
                            (0, 96, t["g_ffn_2"][l].rearrange("(f p) -> f p", p=P)),
                            (0, 104, t["g_q_lat_2"][l].rearrange("(f p) -> f p", p=P)),
                            (0, 106, t["g_kv_lat_2"][l].rearrange("(f p) -> f p", p=P)),
                            (1, 0, t["conv_w_2"][l, 2].rearrange("(f p) -> f p", p=P)),
                            (1, 44, t["conv_b_2"][l].rearrange("(f p) -> f p", p=P))]
                    for a, r, src in rows:
                        sp.dma_start(prm2[r:r + src.shape[0], a, :], src).then_inc(small_loaded.sem, 16)
                    sp.dma_start(w_uq, t["w_uq_2"][l].rearrange("(k p) n -> p k n", p=P)).then_inc(small_loaded.sem, 16)
                    sp.dma_start(w_ukv, t["w_ukv_2"][l]).then_inc(small_loaded.sem, 16)
                    ring.issue(sp, c_wo2[l][-1] + 1 + RING_SLOTS)

                @block.tensor
                def _(pe):
                    pe.wait_ge(small_loaded.sem, small_loaded.at(9 * 16))
                    nc.tensor.transpose(ps[:, 4, 0:107], prm2[0:107, 0, :], ident[0:107, 0:107])
                    nc.tensor.transpose(ps[:, 4, 107:195], prm2[0:88, 1, :], ident[0:88, 0:88])\
                        .then_inc(params2_turned.sem, 1)
                    pe.wait_ge(scaled.sem, scaled.at(1))
                    pe_turn(pe, tn)
                    pe.wait_ge(turned_copied.sem, turned_copied.at(4))
                    pe_project(pe, c_in2[l])
                    pe.wait_ge(projected_copied.sem, projected_copied.at(12))
                    pe.wait_ge(ready2.sem, ready2.at(1))
                    pe_jobs(pe, lat_jobs)
                    pe.wait_ge(jobs_copied.sem, jobs_copied.at(3))
                    for tt in range(TT):
                        tok = slice(tt * P, (tt + 1) * P)
                        for k in range(2):
                            nc.tensor.matmul(ps[:, 4 + tt, 0:384], cT[:, k, tok], w_uq[:, k, :], start=(k == 0),
                                             stop=(k == 1))
                        mm = nc.tensor.matmul(ps[:, 6 + tt, :], cT[:, 2, tok], w_ukv, start=True, stop=True)
                    mm.then_inc(lat_ready.sem, 1)
                    pe.wait_ge(ready2.sem, ready2.at(2))
                    pe_jobs(pe, head_jobs, 3)
                    pe.wait_ge(jobs_copied.sem, jobs_copied.at(15))
                    for i in range(TT):
                        if i:
                            pe.wait_ge(idx_read.sem, idx_read.at(i))
                        kv = (i + 1) * P
                        for a in range(2):
                            for m in range(4):
                                rows = slice(32 * m, 32 * m + 32)
                                mm = nc.tensor.matmul(ps[:, m, a * SEQ:a * SEQ + kv], idxT[rows, a, i * P:(i + 1) * P],
                                                      idxT[rows, 2, 0:kv], start=True, stop=True)
                        mm.then_inc(idx_scores.sem, 1)
                    pe.wait_ge(idx_read.sem, idx_read.at(2))
                    pe_units(pe, units, pT2, probs2, None)
                    pe.wait_ge(U["copied"].sem, U["copied"].at(n_units))
                    pe_sum_chunks(pe, c_wo2[l], lambda k, tt: mixT[:, k, tt * P:(tt + 1) * P])

                @block.scalar
                def _(act):
                    act_squares(act, mixT.rearrange("p a b -> p (a b)").rearrange("p (a b) -> p a b", a=TT))
                    act_project(act, c_in2[l], zz)
                    act.wait_ge(projected_copied.sem, projected_copied.at(12))
                    for tt in range(TT):
                        A(nc.scalar.activation(cn[:, tt, 0:256], zz[:, tt, 0:256], ACT.Square,
                                               accum_out=rms_s[:, 2 + tt:3 + tt]))
                        ins = nc.scalar.activation(cn[:, tt, 256:384], zz[:, tt, Z_KV:Z_PE], ACT.Square,
                                                   accum_out=rms_s[:, 4 + tt:5 + tt])
                    ins.then_inc(lat_squared.sem, 1)
                    act.wait_ge(lat_ready.sem, lat_ready.at(1))
                    for tt in range(TT):
                        nc.scalar.activation(qkm[:, tt, 0, :, :].rearrange("p a b -> p (a b)"), ps[:, 4 + tt, 0:384],
                                             ACT.Copy)
                        ins = nc.scalar.activation(kvb[:, tt, :], ps[:, 6 + tt, :], ACT.Copy)
                    ins.then_inc(lat_copied.sem, 1)

                    def copy_out(act, u, n):
                        return nc.scalar.activation(mixT[:, u.pair, u.i * P:(u.i + 1) * P], ps[:, 6 + n % 2, 0:P],
                                                    ACT.Copy)

                    act_units(act, units, sm2, probs2, pT2, None, copy_out)

                @block.vector
                def _(dve):
                    dve_scale(dve, tn)
                    dve.wait_ge(params2_turned.sem, params2_turned.at(1))
                    V(nc.vector.tensor_copy(pcol[:, 0:195], ps[:, 4, 0:195]))
                    dve_turn_scaled(dve, xT_att, g_att)
                    dve.wait_ge(lat_squared.sem, lat_squared.at(1))
                    V(nc.vector.tensor_scalar(rms_v[:, 2:4], rms_s[:, 2:4], 1.0 / Q_LAT, EPS2, ALU.mult, ALU.add))
                    V(nc.vector.tensor_scalar(rms_v[:, 4:6], rms_s[:, 4:6], 1.0 / KV_LAT, EPS2, ALU.mult, ALU.add))
                    rsqrt(rms_r[:, 2:6], rms_v[:, 2:6], rms_t[:, 2:6])
                    for tt in range(TT):
                        V(nc.vector.tensor_scalar(cn[:, tt, 0:256], zz[:, tt, 0:256], rms_r[:, 2 + tt:3 + tt], None,
                                                  ALU.mult))
                        V(nc.vector.tensor_scalar(cn[:, tt, 256:384], zz[:, tt, Z_KV:Z_PE], rms_r[:, 4 + tt:5 + tt],
                                                  None, ALU.mult))
                    nc.vector.tensor_scalar(w_idx, zz[:, :, Z_W:N_IN2], 256 ** -0.5, None, ALU.mult)\
                        .then_inc(ready2.sem, 1)
                    dve_jobs(dve, lat_jobs)
                    for tt in range(TT):
                        (ca, sa), (ch, sh), (ci, si) = tables_of(tt)
                        z = zz[:, tt, :]
                        rope(z[:, Z_DIL:Z_DIL + 1024].rearrange("p (a b) -> p a b", b=HD), 16, 8, ch, sh, rtmp)
                        rope(z[:, Z_DSA:Z_DSA + 512].rearrange("p (a b) -> p a b", b=HD), 8, 8, ch, sh, rtmp)
                        rope(z[:, Z_IDX:Z_IDX + 288].rearrange("p (a b) -> p a b", b=32), 9, 4, ci, si, rtmp)
                        rope(z[:, Z_PE:Z_DIL].rearrange("p (a b) -> p a b", b=32), 1, 16, ca, sa, rtmp)
                        V(nc.vector.tensor_copy(kidx4[:, tt, :].rearrange("p (a b) -> p a b", a=4),
                                                z[:, Z_W - 32:Z_W].unsqueeze(1).to_broadcast([P, 4, 32])))
                    dve.wait_ge(lat_copied.sem, lat_copied.at(1))
                    for tt in range(TT):
                        (ca, sa), _, _ = tables_of(tt)
                        rope(qkm[:, tt, 0, :, 64:96], LH, 16, ca, sa, rtmp)
                        V(nc.vector.tensor_copy(qkm[:, tt, 1, :, 0:64],
                                                kvb[:, tt, :].rearrange("p (a b) -> p a b", a=LH)[:, :, 0:64]))
                        V(nc.vector.tensor_copy(qkm[:, tt, 1, :, 64:96],
                                                zz[:, tt, Z_PE:Z_DIL].unsqueeze(1).to_broadcast([P, LH, 32])))
                    nc.vector.memset(rms_t, 0.0).then_inc(ready2.sem, 1)
                    dve_jobs(dve, head_jobs, 3)
                    for i in range(TT):
                        kv = (i + 1) * P
                        dve.wait_ge(idx_scores.sem, idx_scores.at(i + 1))
                        for a in range(2):
                            for m in range(4):
                                ins = nc.vector.tensor_scalar(idx_terms[:, a, m, 0:kv], ps[:, m, a * SEQ:a * SEQ + kv],
                                                              0.0, w_idx[:, i, 4 * a + m:4 * a + m + 1], ALU.max,
                                                              ALU.mult)
                        ins.then_inc(idx_read.sem, 1)
                        dve.wait_ge(idx_read.sem, idx_read.at(i + 1))
                        wk = work[:, i, 0:kv]
                        V(nc.vector.tensor_reduce(wk, idx_terms[:, :, :, 0:kv].rearrange("p a m k -> p k a m"),
                                                  XY, ALU.add))
                        V(nc.vector.tensor_tensor(wk, wk, caus[i], ALU.add))
                        for _ in range(TOPK // 8):
                            V(nc.vector.max(best[:, i, :], wk))
                            V(nc.vector.match_replace(out=wk, in_to_replace=best[:, i, :], in_values=wk,
                                                      imm_value=TAKEN))
                        V(nc.vector.tensor_scalar(wk, wk, TAKEN, NEG, ALU.not_equal, ALU.mult))
                        V(nc.vector.tensor_tensor(dsa_mask[:, i, 0:kv], wk, caus[i], ALU.add))
                    dve_units(dve, units, sm2, probs2, None)
                    dve.wait_ge(summed.sem, summed.at(2))
                    for tt in range(TT):
                        for half in range(2):
                            hs = h[:, tt, half * 512:(half + 1) * 512]
                            ins = nc.vector.tensor_tensor(hs, hs, ps[:, 4 + 2 * tt + half, :], ALU.add)
                    V(ins)

            turn_done()
            project_done(c_in2[l])
            jobs_done(15)
            units_done(n_units)
            for s, n in ((squared, 1), (scaled, 1), (small_loaded, 9 * 16), (lat_squared, 1), (lat_ready, 1),
                         (lat_copied, 1), (params2_turned, 1), (ready2, 2), (idx_scores, 2), (idx_read, 2),
                         (summed, 2)):
                s.advance(n)

        gT = area(4096, FT2, SEQ)
        acc2 = area(9728, 2, SEQ)
        xT_mlp = area(0, KD, SEQ)
        tn_mlp = area(2048, TT, D)
        junk_mlp = area(10240, TT, D)

        def mlp_layer(l):
            for q, c in enumerate(c_up2[l]):
                ring.release(c, up_ready, 4 * q + 4)
            release_summed(c_dn2[l])

            def wait_acc_free(eng, n):
                if 2 <= n < FT2 + 2:
                    eng.wait_ge(gate_done.sem, gate_done.at(n - 1))
                elif n >= FT2 + 2:
                    eng.wait_ge(up_done.sem, up_done.at(n - 1 - FT2))

            with nc.Block() as block:
                @block.sync
                def _(sp):
                    ring.issue(sp, c_dn2[l][-1] + 1 + RING_SLOTS)

                @block.tensor
                def _(pe):
                    pe.wait_ge(scaled.sem, scaled.at(1))
                    pe_turn(pe, tn_mlp)
                    pe.wait_ge(turned_copied.sem, turned_copied.at(4))
                    for q, c in enumerate(c_up2[l]):
                        w = ring.rows8(c)
                        ring.arrived(pe, c)
                        for k4 in range(4):
                            n = 4 * q + k4
                            if n >= 4:
                                pe.wait_ge(up_summed.sem, up_summed.at(n - 3))
                            for k in range(KD):
                                mm = nc.tensor.matmul(ps[:, n % 4, 0:SEQ], w[:, k, k4 * P:(k4 + 1) * P], xT_mlp[:, k, :],
                                                      start=(k == 0), stop=(k == KD - 1))
                            mm.then_inc(up_ready.sem, 1)
                    pe.wait_ge(up_done.sem, up_done.at(FT2))
                    pe_sum_chunks(pe, c_dn2[l], lambda k, tt: gT[:, k, tt * P:(tt + 1) * P])

                @block.scalar
                def _(act):
                    act_squares(act, junk_mlp)

                    def begin(n):
                        act.wait_ge(up_ready.sem, up_ready.at(n + 1))
                        wait_acc_free(act, n)
                        nc.scalar.activation(acc2[:, n % 2, :], ps[:, n % 4, 0:SEQ], ACT.Identity,
                                             bias=bias2[:, n:n + 1], scale=taps2[2][:, n:n + 1])\
                            .then_inc(up_begun.sem, 1)

                    for n in range(HALF_UP):
                        begin(n)
                        if 1 <= n <= FT2:
                            act.wait_ge(up_summed.sem, up_summed.at(n))
                            nc.scalar.activation(gT[:, n - 1, :], acc2[:, (n - 1) % 2, :], ACT.Silu)\
                                .then_inc(gate_done.sem, 1)

                @block.gpsimd
                def _(pool):
                    for n in range(FT2):
                        pool.wait_ge(gate_done.sem, gate_done.at(n + 1))
                        pool.wait_ge(up_summed.sem, up_summed.at(FT2 + n + 1))
                        nc.gpsimd.tensor_tensor(gT[:, n, :], gT[:, n, :], acc2[:, (FT2 + n) % 2, :], ALU.mult)\
                            .then_inc(up_done.sem, 1)

                @block.vector
                def _(dve):
                    dve_scale(dve, tn_mlp)
                    dve_turn_scaled(dve, xT_mlp, g_mlp)
                    for n in range(HALF_UP):
                        dve.wait_ge(up_begun.sem, up_begun.at(n + 1))
                        for j in (1, 0):
                            acc = acc2[:, n % 2, 2 - j:SEQ]
                            ins = nc.vector.scalar_tensor_tensor(acc, ps[:, n % 4, 0:SEQ - 2 + j],
                                                                 taps2[j][:, n:n + 1], acc, ALU.mult, ALU.add)
                            if j:
                                V(ins)
                        ins.then_inc(up_summed.sem, 1)
                    dve.wait_ge(summed.sem, summed.at(6))
                    for tt in range(TT):
                        for half in range(2):
                            hs = h[:, tt, half * 512:(half + 1) * 512]
                            ins = nc.vector.tensor_tensor(hs, hs, ps[:, 4 + 2 * tt + half, :], ALU.add)
                    V(ins)

            turn_done()
            for s, n in ((squared, 1), (scaled, 1), (up_ready, HALF_UP), (up_begun, HALF_UP), (up_summed, HALF_UP),
                         (gate_done, FT2), (up_done, FT2), (summed, 6)):
                s.advance(n)

        for l in range(2):
            attention_layer(l)
            mlp_layer(l)

        g_final = area(0, D)
        result = area(2048, TT, D)
        with nc.Block() as block:
            @block.sync
            def _(sp):
                sp.dma_start(g_final, t["g_final_2"].partition_broadcast(P)).then_inc(final_loaded.sem, 16)
                sp.wait_ge(final_done.sem, 1)
                sp.dma_start(out[0].rearrange("(a p) n -> p a n", p=P), result).then_inc(final_stored.sem, 16)
                sp.wait_ge(final_stored.sem, 16)

            @block.scalar
            def _(act):
                act_squares(act, junk_mlp)

            @block.vector
            def _(dve):
                dve_scale(dve, result)
                dve.wait_ge(scaled.sem, scaled.at(1))
                dve.wait_ge(final_loaded.sem, 16)
                nc.vector.tensor_tensor(result, result, g_final.unsqueeze(1).to_broadcast([P, TT, D]), ALU.mult)\
                    .then_inc(final_done.sem, 1)


def shape_constants():
    import numpy as np

    c = np.zeros((P, C_ALL), np.float32)
    i, j = np.arange(P)[:, None], np.arange(P)[None, :]
    c[:, C_ID:C_ID + P] = i == j
    c[:, C_TRIU:C_TRIU + P] = i <= j
    c[:, C_STRIU:C_STRIU + P] = i < j
    c[:, C_ONES:C_ONES + P] = 1
    c[:, C_IOTA4:C_IOTA4 + P] = j % CAP + 1
    c[:, C_IOTA:C_IOTA + NE] = np.arange(NE)
    c[:, C_JCOL] = 4 * 1024 + np.arange(P) // CAP
    for tt in range(TT):
        c[:, C_TOK8 + tt] = 8 * (P * tt + np.arange(P)) - 4 * 1024
    c[:, C_INVF:C_INVF + 8] = np.float32(500000.0) ** (-np.arange(0, 16, 2, dtype=np.float32) / np.float32(16))
    c[:, C_CAUS0:C_CAUS0 + P] = np.where(j <= i, 0, NEG)
    k = np.arange(SEQ)[None, :]
    for tt, col, n in ((0, C_MUL0, P), (1, C_MUL1, SEQ)):
        q = P * tt + i
        dist = q - k[:, :n]
        c[:, col:col + n] = (dist >= 0) * ((dist <= 128) * 1.0 + (dist % 4 == 0) + (dist % 16 == 0))
    c[:, C_WIN1:C_WIN1 + SEQ] = np.where(c[:, C_MUL1:C_MUL1 + SEQ] > 0, 0, NEG)
    c[:, C_CAUS1:C_CAUS1 + SEQ] = np.where(k <= P + i, 0, NEG)
    col = C_ROPE
    for tt in range(TT):
        for dim in (32, 16, 8):
            inv = np.float32(500000.0) ** (-np.arange(0, dim, 2, dtype=np.float32) / np.float32(dim))
            ang = (P * tt + np.arange(P, dtype=np.float32))[:, None] * inv[None, :].astype(np.float32)
            for table in (np.cos(ang), np.sin(ang)):
                c[:, col:col + dim // 2] = table
                col += dim // 2
    return c


_INS = ["x", "positions", "ln_mix_g", "ln_mix_b", "ln_ffn_g", "ln_ffn_b", "ssm_w_in", "ssm_conv_w", "ssm_conv_b",
        "ssm_dt_bias", "ssm_a_log", "ssm_d", "ssm_norm_w", "ssm_w_out", "attn_w_qkv", "attn_lam_q1", "attn_lam_k1",
        "attn_lam_q2", "attn_lam_k2", "attn_subln_w", "attn_w_o", "moe_w_group", "moe_w_expert", "moe_w_gate",
        "moe_w_up", "moe_w_down", "g_attn_2", "w_in_2", "g_q_lat_2", "w_uq_2", "g_kv_lat_2", "w_ukv_2", "w_o_2",
        "g_ffn_2", "w_up_2", "conv_w_2", "conv_b_2", "w_down_2", "g_final_2"]


def kernel(**inputs):
    import numpy as _np
    import concourse.bacc as _bacc
    from concourse import mybir as _mybir
    from concourse.bass_utils import run_bass_kernel_spmd as _run

    nc = _bacc.Bacc("TRN2", target_bir_lowering=False, num_devices=1)
    arrays, tensors = {}, {}
    for name in _INS + ["constants"]:
        a = shape_constants() if name == "constants" else _np.ascontiguousarray(inputs[name])
        arrays[f"in_{name}_dram"] = a
        tensors[name] = nc.dram_tensor(f"in_{name}_dram", a.shape, _mybir.dt.from_np(a.dtype),
                                       kind="ExternalInput").ap()
    tensors["out"] = nc.dram_tensor("out_0_dram", (1, SEQ, D), F32, kind="ExternalOutput").ap()
    hybrid_stack(nc, tensors)
    r = _run(nc, [arrays], core_ids=[0])
    return r.results[0]["out_0_dram"]
```

```python
from contextlib import ExitStack

import concourse.bass as bass
from concourse import mybir

P = 128
SEQ, D = 256, 1024
TT = SEQ // P
KD = D // P
F32 = mybir.dt.float32
I32 = mybir.dt.int32
U32 = mybir.dt.uint32
ALU = mybir.AluOpType
ACT = mybir.ActivationFunctionType
AX_X = mybir.AxisListType.X
XY = mybir.AxisListType.XY

ALPHA = (2 * 2) ** 0.25
EPS, EPS2 = 1e-5, 1e-6
TWO_PI = 6.283185307179586
LAMBDA_INIT = 0.8 - 0.6 * 2.718281828459045 ** -0.3
ROUND = 12582912.0
RSQRT_GUESS = float(0x5F3759DF)
NEG = -1e30

RING_SLOTS, CHUNK = 6, 4096
G, R, HD, NST = 8, 4, 64, 128
NH = G * R
DI = NH * HD
CONV = DI + 2 * G * NST
NE, EG, NG, FF = 32, 8, 4, 512
CAP = 32
N_IN2 = 3016
DFF2 = 2816
Q_LAT, KV_LAT = 256, 128
FT2 = DFF2 // P
HALF_UP = 2 * FT2
IN2_ORDER = (5, 0, 1, 2, 3, 4)

C_ID, C_TRIU, C_STRIU, C_ONES, C_IOTA4 = 0, 128, 256, 384, 512
C_IOTA, C_JCOL, C_TOK8, C_INVF = 640, 672, 673, 675
C_CAUS0, C_MUL0, C_MUL1, C_WIN1, C_ROPE, C_CAUS1 = 683, 811, 939, 1195, 1451, 1563
C_ALL = 1819


class Sem:

    def __init__(self, ctx, nc, name):
        self.sem, self.base = ctx.enter_context(nc.semaphore(name)), 0

    def at(self, k):
        return self.base + k

    def advance(self, total):
        self.base += total


class Chain:

    def __init__(self, ctx, nc, name, eng):
        self.sem, self.eng, self.n, self.loop = ctx.enter_context(nc.semaphore(name)), eng, 0, None

    def link(self, ins):
        ins.then_inc(self.sem, 1)
        self.n += 1
        self.eng.wait_ge(self.sem, self.n if self.loop is None else self.loop + self.n)

    def enter_loop(self, turn, per_turn):
        self.loop, self.start, self.per_turn = turn * per_turn, self.n, per_turn

    def leave_loop(self, turns):
        assert self.n == self.start + self.per_turn, (self.n - self.start)
        self.n, self.loop = self.start + turns * self.per_turn, None


class Ring:

    def __init__(self, ctx, nc, buf):
        self.buf, self.chunks, self.issued, self.released = buf, [], 0, {}
        self.loaded = [ctx.enter_context(nc.semaphore(f"slot{s}_loaded")) for s in range(RING_SLOTS)]

    def rows8(self, c, n=512):
        s = c % RING_SLOTS
        return self.buf[:, s * CHUNK:s * CHUNK + KD * n].rearrange("p (t n) -> p t n", t=KD)

    def rows4(self, c, k=4):
        s = c % RING_SLOTS
        return self.buf[:, s * CHUNK:s * CHUNK + k * D].rearrange("p (t n) -> p t n", t=k)

    def dst(self, c, shape):
        return self.rows8(c, shape[2]) if shape[1] == KD else self.rows4(c, shape[1])

    def release(self, c, sem, count):
        self.released[c] = (sem.sem, sem.at(count))

    def issue(self, sp, upto):
        for c in range(self.issued, min(upto, len(self.chunks))):
            if c >= RING_SLOTS:
                sp.wait_ge(*self.released[c - RING_SLOTS])
            sp.dma_start(self.dst(c, self.chunks[c].shape), self.chunks[c]).then_inc(self.loaded[c % RING_SLOTS], 16)
        self.issued = max(self.issued, min(upto, len(self.chunks)))

    def arrived(self, pe, c, turn=0):
        pe.wait_ge(self.loaded[c % RING_SLOTS], 16 * (c // RING_SLOTS + 1 + turn))


def cols8(w, a, b):
    return w[:, a:b].rearrange("(t p) n -> p t n", p=P)


def bcast(ap, n):
    return ap.unsqueeze(2).to_broadcast([ap.shape[0], ap.shape[1], n])


def hybrid_stack(nc, t):
    out = t["out"]
    ctx = ExitStack()
    with ctx:
        def sb(name, cols, dt=F32):
            return ctx.enter_context(nc.sbuf_tensor(name, [P, cols], dt))

        def sem(name):
            return Sem(ctx, nc, name)

        ring = Ring(ctx, nc, sb("ring", RING_SLOTS * CHUNK))
        h = sb("h", TT * D)[:, :].rearrange("p (a n) -> p a n", a=TT)
        cst = sb("cst", C_ALL)
        pcol = sb("pcol", 256)
        tiny = sb("tiny", 300)
        ARENA = 20112
        arena = sb("arena", ARENA)
        ps = ctx.enter_context(nc.psum_tensor("ps", [P, 8, 512], F32))
        moe_rows = [nc.dram_tensor(f"moe_rows{i}", (2 * SEQ * 4, 256), F32, kind="Internal").ap() for i in range(2)]

        def area(a, *shape):
            n = 1
            for x in shape:
                n *= x
            assert a + n <= ARENA, (a, n)
            v = arena[:, a:a + n]
            if len(shape) == 2:
                v = v.rearrange("p (a b) -> p a b", a=shape[0])
            elif len(shape) == 3:
                v = v.rearrange("p (a b c) -> p a b c", a=shape[0], b=shape[1])
            elif len(shape) == 4:
                v = v.rearrange("p (a b c d) -> p a b c d", a=shape[0], b=shape[1], c=shape[2])
            return v

        ident = cst[:, C_ID:C_ID + P]
        triu = cst[:, C_TRIU:C_TRIU + P]
        striu = cst[:, C_STRIU:C_STRIU + P]
        ones = cst[:, C_ONES:C_ONES + P]

        w_in, w_out = t["ssm_w_in"][0], t["ssm_w_out"][0]
        qkv_w, o_w = t["attn_w_qkv"][0], t["attn_w_o"][0]

        def add(c):
            ring.chunks.append(c)
            return len(ring.chunks) - 1

        def rows4(w, i, k=4):
            return w[i * 512:i * 512 + k * P, :].rearrange("(t p) n -> p t n", p=P)

        def add_experts(layer):
            first = len(ring.chunks)
            for e in (0, *range(2, NE)):
                add(cols8(t["moe_w_gate"][layer, e], 0, FF))
                add(cols8(t["moe_w_up"][layer, e], 0, FF))
                add(rows4(t["moe_w_down"][layer, e], 0))
            return first

        c_xbc = [add(cols8(w_in, DI + 512 * i, DI + 512 * i + 512)) for i in range(CONV // 512)]
        c_z = [add(cols8(w_in, 512 * i, 512 * i + 512)) for i in range(DI // 512)]
        c_wout = [add(rows4(w_out, i)) for i in range(DI // 512)]
        c_moe = [add_experts(0)]
        c_qkv = [add(cols8(qkv_w, 512 * i, 512 * i + 512)) for i in range(6)]
        c_wo = [add(rows4(o_w, i)) for i in range(2)]
        c_moe.append(add_experts(1))
        c_in2, c_wo2, c_up2, c_dn2 = [], [], [], []
        for l in range(2):
            c_in2.append([add(cols8(t["w_in_2"][l], 512 * i, min(N_IN2, 512 * i + 512))) for i in IN2_ORDER])
            c_wo2.append([add(rows4(t["w_o_2"][l], i)) for i in range(2)])
            c_up2.append([add(cols8(t["w_up_2"][l], 512 * i, 512 * i + 512)) for i in range(11)])
            c_dn2.append([add(rows4(t["w_down_2"][l], i, 4 if i < 5 else 2)) for i in range(6)])

        dve_step = Chain(ctx, nc, "dve_step", nc.vector)
        act_step = Chain(ctx, nc, "act_step", nc.scalar)
        pool_step = Chain(ctx, nc, "pool_step", nc.gpsimd)
        V, A, Q = dve_step.link, act_step.link, pool_step.link

        def rsqrt(r, v, tmp):
            V(nc.vector.tensor_scalar(tmp.bitcast(I32), v.bitcast(I32), 1, None, ALU.logical_shift_right))
            V(nc.vector.tensor_scalar(r.bitcast(I32), tmp.bitcast(I32), -1.0, RSQRT_GUESS, ALU.mult, ALU.add))
            for _ in range(3):
                V(nc.vector.tensor_tensor(tmp, r, r, ALU.mult))
                V(nc.vector.scalar_tensor_tensor(tmp, tmp, -0.5, v, ALU.mult, ALU.mult))
                V(nc.vector.scalar_tensor_tensor(r, tmp, 1.5, r, ALU.add, ALU.mult))

        turned, turned_copied = sem("turned"), sem("turned_copied")

        def pe_turn(pe, src):
            for n in range(4):
                tt, q = n // 2, n % 2
                for k in range(4):
                    mm = nc.tensor.transpose(ps[:, n, k * P:(k + 1) * P],
                                             src[:, tt, (4 * q + k) * P:(4 * q + k + 1) * P], ident)
                mm.then_inc(turned.sem, 1)

        def turn_dst(xT, n):
            return xT[:, 4 * (n % 2):4 * (n % 2) + 4, (n // 2) * P:(n // 2 + 1) * P]

        def dve_turn(dve, xT):
            for n in range(4):
                dve.wait_ge(turned.sem, turned.at(n + 1))
                nc.vector.tensor_copy(turn_dst(xT, n), ps[:, n, :].rearrange("p (k n) -> p k n", k=4))\
                    .then_inc(turned_copied.sem, 1)

        def dve_turn_scaled(dve, xT, gain):
            for n in range(4):
                dve.wait_ge(turned.sem, turned.at(n + 1))
                g = gain[:, 4 * (n % 2):4 * (n % 2) + 4]
                nc.vector.tensor_tensor(turn_dst(xT, n), ps[:, n, :].rearrange("p (k n) -> p k n", k=4),
                                        bcast(g, P), ALU.mult).then_inc(turned_copied.sem, 1)

        def turn_done():
            turned.advance(4)
            turned_copied.advance(4)

        summed, summed_first = sem("summed"), sem("summed_first")

        def pe_sum_chunks(pe, chunks, lhs, operands_ready=None):
            n_last = len(chunks) - 1
            for i, c in enumerate(chunks):
                k_tiles = ring.chunks[c].shape[1]
                w = ring.rows4(c, k_tiles)
                ring.arrived(pe, c)
                if operands_ready:
                    operands_ready(4 * i + k_tiles)
                for tt in range(TT):
                    for half in range(2):
                        for k in range(k_tiles):
                            mm = nc.tensor.matmul(ps[:, 4 + 2 * tt + half, :], lhs(4 * i + k, tt),
                                                  w[:, k, half * 512:(half + 1) * 512],
                                                  start=(i == 0 and k == 0), stop=(i == n_last and k == k_tiles - 1))
                    if i == n_last and tt == 0:
                        mm.then_inc(summed_first.sem, 1)
                mm.then_inc(summed.sem, 1)

        def release_summed(chunks):
            for i, c in enumerate(chunks):
                ring.release(c, summed, i + 1)

        ln_loaded, ln_norm, ln_scaled = sem("ln_loaded"), sem("ln_norm"), sem("ln_scaled")
        ln_stats = tiny[:, 0:24].rearrange("p (a b c) -> p a b c", a=TT, b=2)
        ln_mv = tiny[:, 24:28].rearrange("p (a b) -> p a b", a=TT)
        ln_v, ln_r, ln_t, ln_b = tiny[:, 28:30], tiny[:, 30:32], tiny[:, 32:34], tiny[:, 34:36]

        def sp_ln_params(sp, lnp, g, b):
            sp.dma_start(lnp[:, 0, :], g.partition_broadcast(P)).then_inc(ln_loaded.sem, 16)
            sp.dma_start(lnp[:, 1, :], b.partition_broadcast(P)).then_inc(ln_loaded.sem, 16)

        def dve_stats(tt):
            for half in range(2):
                nc.vector.bn_stats(ln_stats[:, tt, half, :], h[:, tt, half * 512:(half + 1) * 512])

        def dve_add_sums(dve, n_chunks, stats):
            for tt in range(TT):
                if tt == 0:
                    dve.wait_ge(summed_first.sem, summed_first.at(1))
                else:
                    dve.wait_ge(summed.sem, summed.at(n_chunks))
                for half in range(2):
                    hs = h[:, tt, half * 512:(half + 1) * 512]
                    bank = ps[:, 4 + 2 * tt + half, :]
                    if stats:
                        ins = nc.vector.scalar_tensor_tensor(hs, hs, ALPHA, bank, ALU.mult, ALU.add)
                    else:
                        ins = nc.vector.tensor_tensor(hs, hs, bank, ALU.add)
                V(ins)
                if stats:
                    dve_stats(tt)

        def sums_done(n_chunks):
            summed.advance(n_chunks)
            summed_first.advance(1)

        def act_norm(act):
            act.wait_ge(ln_norm.sem, ln_norm.at(1))
            nc.scalar.activation(h[:, 0, :], h[:, 0, :], ACT.Identity, bias=ln_b[:, 0:1], scale=ln_r[:, 0:1])\
                .then_inc(ln_scaled.sem, 1)

        def pool_norm(pool, lnp):
            pool.wait_ge(ln_scaled.sem, ln_scaled.at(1))
            pool.wait_ge(ln_loaded.sem, ln_loaded.at(32))
            Q(nc.gpsimd.tensor_tensor(h[:, 0, :], h[:, 0, :], lnp[:, 0, :], ALU.mult))
            Q(nc.gpsimd.tensor_tensor(h[:, 0, :], h[:, 0, :], lnp[:, 1, :], ALU.add))

        def norm_done():
            ln_norm.advance(1)
            ln_scaled.advance(1)
            ln_loaded.advance(32)

        def dve_layer_norm(dve, lnp):
            V(nc.vector.memset(ln_t, 0.0))
            for tt in range(TT):
                V(nc.vector.bn_aggr(ln_mv[:, tt, :], ln_stats[:, tt, :, :]))
            V(nc.vector.tensor_scalar(ln_v, ln_mv[:, :, 1], EPS, None, ALU.add))
            rsqrt(ln_r, ln_v, ln_t)
            nc.vector.scalar_tensor_tensor(ln_b, ln_mv[:, :, 0], -1.0, ln_r, ALU.mult, ALU.mult)\
                .then_inc(ln_norm.sem, 1)
            dve.wait_ge(ln_norm.sem, ln_norm.at(1))
            V(nc.vector.tensor_scalar(h[:, 1, :], h[:, 1, :], ln_r[:, 1:2], ln_b[:, 1:2], ALU.mult, ALU.add))
            dve.wait_ge(ln_loaded.sem, ln_loaded.at(32))
            V(nc.vector.tensor_tensor(h[:, 1, :], h[:, 1, :], lnp[:, 0, :], ALU.mult))
            V(nc.vector.tensor_tensor(h[:, 1, :], h[:, 1, :], lnp[:, 1, :], ALU.add))

        xT = area(0, KD, SEQ)
        silu_z = area(2048, TT, DI)
        xs = area(6144, TT, DI)
        bcT = area(10240, 2 * G, SEQ)
        b_tok = area(14336, G * NST)
        conv_acc = area(15360, 2, SEQ)
        xsT = area(15872, 2, 4, SEQ)
        prm = area(17920, 3, P)
        w_dt = area(18304, KD, NH)
        dt_rows = area(18560, 3, NH)
        dtx = tiny[:, 40:104].rearrange("p (a b) -> p a b", a=TT)

        loaded_x, loaded_p, loaded_dt, loaded_c = sem("loaded_x"), sem("loaded_p"), sem("loaded_dt"), sem("loaded_c")
        params_turned, params_copied = sem("params_turned"), sem("params_copied")
        dt_ready = sem("dt_ready")
        tile_ready, conv_begun, conv_summed, conv_done = (sem("tile_ready"), sem("conv_begun"), sem("conv_summed"),
                                                          sem("conv_done"))
        xs_turned, xs_copied = sem("xs_turned"), sem("xs_copied")
        z_ready, z_done = sem("z_ready"), sem("z_done")
        taps = pcol[:, 0:128].rearrange("p (j f) -> p j f", j=4)
        conv_bias = pcol[:, 128:160]
        norm_w = pcol[:, 160:176]

        for q, c in enumerate(c_xbc):
            ring.release(c, tile_ready, 4 * q + 4)
        for q, c in enumerate(c_z):
            ring.release(c, z_ready, 2 * q + 2)
        with nc.Block() as block:
            @block.sync
            def _(sp):
                sp.dma_start(h, t["x"][0].rearrange("(a p) n -> p a n", p=P)).then_inc(loaded_x.sem, 16)
                sp.dma_start(ident, t["constants"][:, C_ID:C_ID + P]).then_inc(loaded_x.sem, 16)
                sp.dma_start(prm[:, 0, :], t["ssm_conv_w"][0].rearrange("j (f p) -> (j f) p", p=P))\
                    .then_inc(loaded_p.sem, 16)
                sp.dma_start(prm[0:32, 1, :], t["ssm_conv_b"][0].rearrange("(f p) -> f p", p=P))\
                    .then_inc(loaded_p.sem, 16)
                sp.dma_start(prm[0:16, 2, :], t["ssm_norm_w"][0].rearrange("(f p) -> f p", p=P))\
                    .then_inc(loaded_p.sem, 16)
                ring.issue(sp, 2)
                sp.dma_start(w_dt, cols8(w_in, DI + CONV, DI + CONV + NH)).then_inc(loaded_dt.sem, 16)
                for i, name in enumerate(("ssm_dt_bias", "ssm_a_log", "ssm_d")):
                    sp.dma_start(dt_rows[:, i, :], t[name][0].partition_broadcast(P)).then_inc(loaded_dt.sem, 16)
                ring.issue(sp, RING_SLOTS)
                sp.dma_start(cst[:, P:C_ALL], t["constants"][:, P:C_ALL]).then_inc(loaded_c.sem, 16)
                ring.issue(sp, c_z[-1] + 1 + RING_SLOTS)
                sp.wait_ge(loaded_c.sem, 16)

            @block.tensor
            def _(pe):
                pe.wait_ge(loaded_x.sem, 32)
                pe_turn(pe, h)
                pe.wait_ge(loaded_p.sem, 3 * 16)
                nc.tensor.transpose(ps[:, 4, 0:128], prm[:, 0, :], ident)
                nc.tensor.transpose(ps[:, 4, 128:160], prm[0:32, 1, :], ident[0:32, 0:32])
                nc.tensor.transpose(ps[:, 4, 160:176], prm[0:16, 2, :], ident[0:16, 0:16])\
                    .then_inc(params_turned.sem, 1)
                pe.wait_ge(turned_copied.sem, 4)

                def step_sizes():
                    pe.wait_ge(loaded_dt.sem, 4 * 16)
                    for tt in range(TT):
                        for k in range(KD):
                            mm = nc.tensor.matmul(ps[:, 5, tt * NH:(tt + 1) * NH], xT[:, k, tt * P:(tt + 1) * P],
                                                  w_dt[:, k, :], start=(k == 0), stop=(k == KD - 1))
                    mm.then_inc(dt_ready.sem, 1)

                def turn_chunk(q):
                    pe.wait_ge(conv_done.sem, 4 * q + 4)
                    if q:
                        pe.wait_ge(xs_copied.sem, 2 * q if q <= 4 else 8 + q - 4)
                    for tt in range(TT if q < 4 else 1):
                        for k in range(4):
                            src = xsT[:, q % 2, k, :] if q < 4 else bcT[:, 2 * (4 * (q - 4) + k), :]
                            mm = nc.tensor.transpose(ps[:, 6 + tt, k * P:(k + 1) * P], src[:, tt * P:(tt + 1) * P],
                                                     ident)
                        mm.then_inc(xs_turned.sem, 1)

                for q, c in enumerate(c_xbc):
                    w = ring.rows8(c)
                    ring.arrived(pe, c)
                    for k4 in range(4):
                        n = 4 * q + k4
                        if n >= 4:
                            pe.wait_ge(conv_summed.sem, n - 3)
                        for k in range(KD):
                            mm = nc.tensor.matmul(ps[:, n % 4, 0:SEQ], w[:, k, k4 * P:(k4 + 1) * P], xT[:, k, :],
                                                  start=(k == 0), stop=(k == KD - 1))
                        mm.then_inc(tile_ready.sem, 1)
                    if q == 2:
                        step_sizes()
                    if 1 <= q <= 6:
                        turn_chunk(q - 1)
                for q, c in enumerate(c_z):
                    w = ring.rows8(c)
                    ring.arrived(pe, c)
                    for tt in range(TT):
                        n = 2 * q + tt
                        if n < 4:
                            pe.wait_ge(conv_summed.sem, 29 + n)
                        else:
                            pe.wait_ge(z_done.sem, n - 3)
                        for k in range(KD):
                            mm = nc.tensor.matmul(ps[:, n % 4, :], xT[:, k, tt * P:(tt + 1) * P], w[:, k, :],
                                                  start=(k == 0), stop=(k == KD - 1))
                        mm.then_inc(z_ready.sem, 1)

            @block.scalar
            def _(act):
                act.wait_ge(params_copied.sem, 1)

                def begin(n):
                    act.wait_ge(tile_ready.sem, n + 1)
                    if n >= 2:
                        act.wait_ge(conv_done.sem, n - 1)
                    nc.scalar.activation(conv_acc[:, n % 2, :], ps[:, n % 4, 0:SEQ], ACT.Identity,
                                         bias=conv_bias[:, n:n + 1], scale=taps[:, 3, n:n + 1])\
                        .then_inc(conv_begun.sem, 1)

                def end(n):
                    act.wait_ge(conv_summed.sem, n + 1)
                    if n < 16:
                        q = n // 4
                        if q >= 2:
                            act.wait_ge(xs_turned.sem, 2 * (q - 1))
                        dst = xsT[:, q % 2, n % 4, :]
                    elif n < 24:
                        dst = bcT[:, 2 * (n - 16), :]
                    else:
                        dst = bcT[:, 2 * (n - 24) + 1, :]
                    nc.scalar.activation(dst, conv_acc[:, n % 2, :], ACT.Silu).then_inc(conv_done.sem, 1)

                for n in range(32):
                    begin(n)
                    if n:
                        end(n - 1)
                end(31)
                for n in range(8):
                    act.wait_ge(z_ready.sem, n + 1)
                    nc.scalar.activation(silu_z[:, n % 2, (n // 2) * 512:(n // 2 + 1) * 512], ps[:, n % 4, :],
                                         ACT.Silu).then_inc(z_done.sem, 1)

            def copy_turned(dve, q):
                for tt in range(TT if q < 4 else 1):
                    n = 2 * q + tt if q <= 4 else 9
                    dve.wait_ge(xs_turned.sem, n + 1)
                    dst = xs[:, tt, q * 512:(q + 1) * 512] if q < 4 else b_tok[:, (q - 4) * 512:(q - 3) * 512]
                    nc.vector.tensor_copy(dst, ps[:, 6 + tt, :]).then_inc(xs_copied.sem, 1)

            @block.vector
            def _(dve):
                dve_turn(dve, xT)
                dve.wait_ge(params_turned.sem, 1)
                nc.vector.tensor_copy(pcol[:, 0:176], ps[:, 4, 0:176]).then_inc(params_copied.sem, 1)
                dve.wait_ge(params_copied.sem, 1)
                for n in range(32):
                    q = n // 4
                    dve.wait_ge(conv_begun.sem, n + 1)
                    for j in (2, 1, 0):
                        back = 3 - j
                        acc = conv_acc[:, n % 2, back:SEQ]
                        ins = nc.vector.scalar_tensor_tensor(acc, ps[:, n % 4, 0:SEQ - back],
                                                             taps[:, j, n:n + 1], acc, ALU.mult, ALU.add)
                        if j:
                            V(ins)
                    ins.then_inc(conv_summed.sem, 1)
                    if n % 4 == 1 and 2 <= q:
                        copy_turned(dve, q - 2)
                dve.wait_ge(dt_ready.sem, 1)
                V(nc.vector.tensor_tensor(dtx, ps[:, 5, 0:TT * NH].rearrange("p (a b) -> p a b", a=TT),
                                          dt_rows[:, 0, :].unsqueeze(1).to_broadcast([P, TT, NH]), ALU.add))

        turn_done()

        UNITS = G * TT
        GW = R * HD
        cb_m = area(0, 2, P)
        seg = area(256, 2, R * P)
        state = area(1280, 2, GW)
        junk = area(1792, GW)
        decay = area(15360, 2, R * P)
        mixer = area(16384, 2, R * P)
        xdt = area(17408, 2, GW)
        xdt_end = area(17920, 2, GW)
        dt, dta, acum = area(18656, TT, NH), area(18720, TT, NH), area(18784, 3, NH)
        d_end, e_acum1, a_row = area(18880, NH), area(18912, NH), area(18944, NH)
        tmp1, tmp2 = area(18976, TT * NH), area(19040, TT * NH)
        xsd = area(19136, 2, GW)
        y_off = area(19648, GW)
        ssq = tiny[:, 104:120].rearrange("p (a b) -> p a b", a=G)
        nv, nr, nt = tiny[:, 120:122], tiny[:, 122:124], tiny[:, 124:126]

        dt_dve, dt_act, dt_pe = sem("dt_dve"), sem("dt_act"), sem("dt_pe")
        cb_ready, seg_ready, decay_ready, mixer_ready = (sem("cb_ready"), sem("seg_ready"), sem("decay_ready"),
                                                         sem("mixer_ready"))
        x_ready, y_ready, y_done = sem("x_ready"), sem("y_ready"), sem("y_done")
        ssq_ready, yn_ready, yn_turned, yT_ready = sem("ssq_ready"), sem("yn_ready"), sem("yn_turned"), sem("yT_ready")
        yT = bcT
        lnp = area(0, 2, D)
        release_summed(c_wout)

        def unit(u):
            return u // 2, u % 2, u % 2

        def grp(g):
            return slice(g * GW, (g + 1) * GW)

        with nc.Block() as block:
            @block.sync
            def _(sp):
                sp.wait_ge(yT_ready.sem, 2 * G)
                sp_ln_params(sp, lnp, t["ln_mix_g"][0], t["ln_mix_b"][0])
                ring.issue(sp, c_wout[-1] + 1 + RING_SLOTS)

            @block.tensor
            def _(pe):
                pe.wait_ge(dt_dve.sem, 4)
                for c in range(TT):
                    nc.tensor.matmul(ps[:, 6, c * NH:(c + 1) * NH], triu, dta[:, c, :], start=True, stop=True)
                nc.tensor.matmul(ps[:, 6, 64:96], ones, dta[:, 0, :], start=True, stop=True).then_inc(dt_pe.sem, 1)

                def scores(u):
                    g, c, b = unit(u)
                    if u >= 2:
                        pe.wait_ge(seg_ready.sem, u - 1)
                    tok = slice(c * P, (c + 1) * P)
                    nc.tensor.matmul(ps[:, b, 0:P], bcT[:, 2 * g, tok], bcT[:, 2 * g + 1, tok], start=True, stop=True)
                    for r in range(R):
                        hh = g * R + r
                        mm = nc.tensor.matmul(ps[:, 2 + b, r * P:(r + 1) * P],
                                              dta[:, c, hh:hh + 1].to_broadcast([P, P]), triu, start=True, stop=True)
                    mm.then_inc(cb_ready.sem, 1)

                def products(u):
                    g, c, b = unit(u)
                    pe.wait_ge(x_ready.sem, u + 1)
                    pe.wait_ge(mixer_ready.sem, u + 1)
                    if u >= 2:
                        pe.wait_ge(y_done.sem, u - 1)
                    for r in range(R):
                        nc.tensor.matmul(ps[:, 4 + b, r * HD:(r + 1) * HD], mixer[:, b, r * P:(r + 1) * P],
                                         xdt[:, b, r * HD:(r + 1) * HD], start=True, stop=True)
                    if c == 0:
                        mm = nc.tensor.matmul(ps[:, 4 + b, GW:2 * GW], b_tok[:, g * NST:(g + 1) * NST], xdt_end[:, g % 2, :],
                                              start=True, stop=True)
                    else:
                        pe.wait_ge(y_done.sem, u)
                        mm = nc.tensor.matmul(ps[:, 4 + b, GW:2 * GW], bcT[:, 2 * g + 1, P:SEQ], state[:, g % 2, :],
                                              start=True, stop=True)
                    mm.then_inc(y_ready.sem, 1)

                def turn_group(g):
                    pe.wait_ge(yn_ready.sem, g + 1)
                    if g >= 2:
                        pe.wait_ge(yT_ready.sem, 2 * (g - 1))
                    for f in range(2):
                        for c in range(TT):
                            mm = nc.tensor.transpose(ps[:, 6 + g % 2, (2 * f + c) * P:(2 * f + c + 1) * P],
                                                     xs[:, c, g * GW + f * P:g * GW + (f + 1) * P], ident)
                    mm.then_inc(yn_turned.sem, 1)

                scores(0)
                for u in range(UNITS):
                    if u + 1 < UNITS:
                        scores(u + 1)
                    products(u)
                    if u >= 4 and u % 2 == 0:
                        turn_group((u - 4) // 2)
                turn_group(G - 2)
                turn_group(G - 1)
                pe.wait_ge(yT_ready.sem, 2 * G)
                pe.wait_ge(y_done.sem, UNITS)
                pe_sum_chunks(pe, c_wout, lambda k, tt: yT[:, k, tt * P:(tt + 1) * P])

            @block.scalar
            def _(act):
                nc.scalar.activation(a_row, dt_rows[:, 1, :], ACT.Exp).then_inc(dt_act.sem, 1)
                act.wait_ge(dt_dve.sem, 1)
                nc.scalar.activation(tmp1, tmp1, ACT.Exp, scale=-1.0).then_inc(dt_act.sem, 1)
                act.wait_ge(dt_dve.sem, 2)
                nc.scalar.activation(y_off[:, 0:64], tmp2, ACT.Ln).then_inc(dt_act.sem, 1)
                act.wait_ge(dt_dve.sem, 5)
                nc.scalar.activation(e_acum1, acum[:, 1, :], ACT.Exp).then_inc(dt_act.sem, 1)
                nc.scalar.activation(d_end, d_end, ACT.Exp).then_inc(dt_act.sem, 1)

                def squares(g):
                    act.wait_ge(y_done.sem, 2 * g + 2)
                    if g:
                        act.wait_ge(ssq_ready.sem, g)
                    A(nc.scalar.activation(junk, xs[:, 0, grp(g)], ACT.Square, accum_out=ssq[:, g, 0:1]))
                    nc.scalar.activation(junk, xs[:, 1, grp(g)], ACT.Square, accum_out=ssq[:, g, 1:2])\
                        .then_inc(ssq_ready.sem, 1)

                def copy_group(g):
                    act.wait_ge(yn_turned.sem, g + 1)
                    for f in range(2):
                        nc.scalar.activation(yT[:, 2 * g + f, :], ps[:, 6 + g % 2, f * SEQ:(f + 1) * SEQ], ACT.Copy,
                                             scale=norm_w[:, 2 * g + f:2 * g + f + 1]).then_inc(yT_ready.sem, 1)

                for u in range(UNITS):
                    act.wait_ge(seg_ready.sem, u + 1)
                    if u >= 2:
                        act.wait_ge(mixer_ready.sem, u - 1)
                    nc.scalar.activation(decay[:, u % 2, :], seg[:, u % 2, :], ACT.Exp).then_inc(decay_ready.sem, 1)
                    if u >= 2 and u % 2 == 0:
                        squares((u - 2) // 2)
                    if u >= 4 and u % 2 == 0:
                        copy_group((u - 4) // 2)
                squares(G - 1)
                copy_group(G - 2)
                copy_group(G - 1)
                act_norm(act)

            @block.gpsimd
            def _(pool):
                pool.wait_ge(dt_dve.sem, 3)
                pool.wait_ge(dt_act.sem, 5)
                for u in range(UNITS):
                    g, c, b = unit(u)
                    x3 = xs[:, c, grp(g)].rearrange("p (r d) -> p r d", r=R)
                    heads = slice(g * R, (g + 1) * R)
                    if u >= 2:
                        pool.wait_ge(y_done.sem, u - 1)
                    Q(nc.gpsimd.tensor_tensor(xdt[:, b, :].rearrange("p (r d) -> p r d", r=R), x3,
                                              bcast(dt[:, c, heads], HD), ALU.mult))
                    if c == 0:
                        Q(nc.gpsimd.tensor_tensor(xdt_end[:, g % 2, :].rearrange("p (r d) -> p r d", r=R),
                                                  xdt[:, b, :].rearrange("p (r d) -> p r d", r=R),
                                                  bcast(d_end[:, heads], HD), ALU.mult))
                    nc.gpsimd.tensor_tensor(xsd[:, b, :].rearrange("p (r d) -> p r d", r=R), x3,
                                            bcast(dt_rows[:, 2, heads], HD), ALU.mult).then_inc(x_ready.sem, 1)
                    pool.wait_ge(decay_ready.sem, u + 1)
                    nc.gpsimd.tensor_tensor(mixer[:, b, :].rearrange("p (r l) -> p r l", r=R),
                                            decay[:, b, :].rearrange("p (r l) -> p r l", r=R),
                                            cb_m[:, b, :].unsqueeze(1).to_broadcast([P, R, P]), ALU.mult)\
                        .then_inc(mixer_ready.sem, 1)
                pool_norm(pool, lnp)

            @block.vector
            def _(dve):
                dx = dtx.rearrange("p a b -> p (a b)")
                dtf = dt.rearrange("p a b -> p (a b)")
                nc.vector.scalar_tensor_tensor(tmp1, dx, -1.0, dx, ALU.mult, ALU.max).then_inc(dt_dve.sem, 1)
                dve.wait_ge(dt_act.sem, 2)
                nc.vector.tensor_scalar(tmp2, tmp1, 1.0, None, ALU.add).then_inc(dt_dve.sem, 1)
                dve.wait_ge(dt_act.sem, 3)
                V(nc.vector.tensor_scalar(tmp2, tmp2, -1.0, 1e-30, ALU.add, ALU.max))
                V(nc.vector.reciprocal(dtf, tmp2))
                V(nc.vector.tensor_tensor(dtf, dtf, tmp1, ALU.mult))
                V(nc.vector.tensor_tensor(dtf, dtf, y_off[:, 0:64], ALU.mult))
                V(nc.vector.tensor_scalar(tmp2, tmp2, 1e-30, None, ALU.is_le))
                V(nc.vector.tensor_tensor(tmp2, tmp2, tmp1, ALU.mult))
                V(nc.vector.tensor_tensor(dtf, dtf, tmp2, ALU.add))
                nc.vector.scalar_tensor_tensor(dtf, dx, 0.0, dtf, ALU.max, ALU.add).then_inc(dt_dve.sem, 1)
                dve.wait_ge(dt_dve.sem, 3)
                nc.vector.scalar_tensor_tensor(dta, dt, -1.0, a_row.unsqueeze(1).to_broadcast([P, TT, NH]),
                                               ALU.mult, ALU.mult).then_inc(dt_dve.sem, 1)
                dve.wait_ge(dt_pe.sem, 1)
                V(nc.vector.tensor_copy(acum, ps[:, 6, 0:96].rearrange("p (a b) -> p a b", a=3)))
                nc.vector.tensor_tensor(d_end, acum[:, 2, :], acum[:, 0, :], ALU.subtract).then_inc(dt_dve.sem, 1)
                dve.wait_ge(dt_act.sem, 5)

                def segments(u):
                    g, c, b = unit(u)
                    dve.wait_ge(cb_ready.sem, u + 1)
                    if u >= 2:
                        dve.wait_ge(mixer_ready.sem, u - 1)
                    nc.vector.tensor_tensor(cb_m[:, b, :], ps[:, b, 0:P], triu, ALU.mult)
                    for r in range(R):
                        hh = g * R + r
                        ins = nc.vector.tensor_scalar(seg[:, b, r * P:(r + 1) * P], ps[:, 2 + b, r * P:(r + 1) * P],
                                                      acum[:, c, hh:hh + 1], 0.0, ALU.subtract, ALU.min)
                    ins.then_inc(seg_ready.sem, 1)

                def outputs(u):
                    g, c, b = unit(u)
                    y = xs[:, c, grp(g)]
                    dve.wait_ge(y_ready.sem, u + 1)
                    V(nc.vector.tensor_tensor(y, xsd[:, b, :], ps[:, 4 + b, 0:GW], ALU.add))
                    if c == 0:
                        V(nc.vector.tensor_copy(state[:, g % 2, :], ps[:, 4 + b, GW:2 * GW]))
                    else:
                        V(nc.vector.tensor_tensor(y_off.rearrange("p (r d) -> p r d", r=R),
                                                  ps[:, 4 + b, GW:2 * GW].rearrange("p (r d) -> p r d", r=R),
                                                  bcast(e_acum1[:, g * R:(g + 1) * R], HD), ALU.mult))
                        V(nc.vector.tensor_tensor(y, y, y_off, ALU.add))
                    nc.vector.tensor_tensor(y, y, silu_z[:, c, grp(g)], ALU.mult).then_inc(y_done.sem, 1)

                def normalise(g):
                    dve.wait_ge(ssq_ready.sem, g + 1)
                    V(nc.vector.tensor_scalar(nv, ssq[:, g, :], 1.0 / GW, EPS, ALU.mult, ALU.add))
                    rsqrt(nr, nv, nt)
                    for c in range(TT):
                        y = xs[:, c, grp(g)]
                        ins = nc.vector.tensor_scalar(y, y, nr[:, c:c + 1], None, ALU.mult)
                    ins.then_inc(yn_ready.sem, 1)

                for u in range(UNITS):
                    segments(u)
                    if u:
                        outputs(u - 1)
                    if u >= 3 and u % 2:
                        normalise((u - 3) // 2)
                outputs(UNITS - 1)
                normalise(G - 1)
                dve_add_sums(dve, len(c_wout), True)
                dve_layer_norm(dve, lnp)

        sums_done(len(c_wout))
        norm_done()

        W4 = 4 * CAP
        route_pe, route_act, route_dve = sem("route_pe"), sem("route_act"), sem("route_dve")
        router_loaded, pairs_loaded = sem("router_loaded"), sem("pairs_loaded")
        MAIN = {n: sem("moe_" + n) for n in ("slots", "picked", "xg", "gateup", "silu", "hidden", "turned", "hT",
                                             "down", "dest", "rows")}
        stored = [[sem(f"moe_stored{layer}{b}") for b in range(2)] for layer in range(2)]
        OVER = [{n: sem(f"over{layer}_" + n) for n in ("loaded", "shifted", "slots", "picked", "xg", "gateup", "silu", "hidden",
                                                       "turned", "hT", "down", "dest", "rows")} for layer in range(2)]
        ticked = [sem("ticked0"), sem("ticked1")]
        w1_loaded = sem("w1_loaded")
        NECOL = NE + 2

        def moe(layer, lnp_g, lnp_b, sp_next=None):
            first = c_moe[layer]
            xT = area(0, KD, SEQ)
            wr = area(2048, KD, NG + NE)
            lg = area(2336, TT, NG + NE)
            slots = area(2408, 2, TT, W4)
            xg = area(2920, 2, KD * CAP + 2)
            sg = area(3436, 2, 256)
            hid = area(3948, 2, 256)
            hT = area(4460, 2, 2, 2 * CAP)
            rows = area(4716, 2, 256)
            pos1 = area(5228, TT, NECOL)
            info = area(5300, TT, NECOL, 2)
            chosen = area(5440, TT, 2, NE)
            both = area(5568, TT, NE)
            t8 = area(5632, 8, TT, 8)
            esel = area(5760, TT, 8)
            r1 = area(5776, 16, TT)
            dest = area(5808, 2)
            wcol = area(5810, 2)
            cnt = area(5812, 2)
            cnti = area(5814, 2).bitcast(I32)
            gmask = area(5820, TT, NG)
            gsel = area(5828, TT, NG, EG)
            wpart = area(5892, TT, 2, NE)
            pairs = area(6144, TT, 2, D)
            lnp = area(10240, 2, D)
            tick = area(5816, 1, 1)[0:1, 0, :]
            w1 = [area(7824, KD, FF), area(7824 + CHUNK, KD, FF), area(7824 + 2 * CHUNK, FF // P, D)]
            m, o = MAIN, OVER[layer]
            y_st = stored[layer]

            def gate_w(c):
                return ring.rows8(c)

            def step_slots(dve, s, v, prev, b, e, pos):
                if prev:
                    dve.wait_ge(s["picked"].sem, prev(s["picked"]))
                for tt in range(TT):
                    ins = nc.vector.tensor_scalar(slots[:, b, tt, :], cst[:, C_IOTA4:C_IOTA4 + W4],
                                                  pos[:, tt, bass.ds(e, 1)], None, ALU.is_equal)
                ins.then_inc(s["slots"].sem, 1)

            def step_pick(pe, s, v, prev, b, e):
                pe.wait_ge(s["slots"].sem, v(s["slots"]))
                if prev:
                    pe.wait_ge(s["xg"].sem, prev(s["xg"]))
                for k in range(KD):
                    for tt in range(TT):
                        nc.tensor.matmul(ps[:, b, k * CAP:(k + 1) * CAP], h[:, tt, k * P:(k + 1) * P],
                                         slots[:, b, tt, 0:CAP], start=(tt == 0), stop=(tt == TT - 1))
                for tt in range(TT):
                    mm = nc.tensor.matmul(ps[:, b, KD * CAP:KD * CAP + 2], slots[:, b, tt, :],
                                          info[:, tt, bass.ds(e, 1), :].rearrange("p a b -> p (a b)"),
                                          start=(tt == 0), stop=(tt == TT - 1))
                mm.then_inc(s["picked"].sem, 1)

            def step_xg(act, s, v, prev, b):
                act.wait_ge(s["picked"].sem, v(s["picked"]))
                if prev:
                    act.wait_ge(s["gateup"].sem, prev(s["gateup"]))
                    act.wait_ge(s["dest"].sem, prev(s["dest"]))
                nc.scalar.activation(xg[:, b, :], ps[:, b, 0:KD * CAP + 2], ACT.Copy).then_inc(s["xg"].sem, 1)

            def step_gateup(pe, s, v, prev, b, wg, wu):
                pe.wait_ge(s["xg"].sem, v(s["xg"]))
                if prev:
                    pe.wait_ge(s["hidden"].sem, prev(s["hidden"]))
                for k in range(KD):
                    for j in range(4):
                        w = (wg, wu)[j // 2]
                        mm = nc.tensor.matmul(ps[j * CAP:(j + 1) * CAP, 2 + b, 0:256], xg[:, b, k * CAP:(k + 1) * CAP],
                                              w[:, k, (j % 2) * 256:(j % 2 + 1) * 256],
                                              start=(k == 0), stop=(k == KD - 1))
                mm.then_inc(s["gateup"].sem, 1)

            def step_silu(act, s, v, prev, b):
                act.wait_ge(s["gateup"].sem, v(s["gateup"]))
                if prev:
                    act.wait_ge(s["hidden"].sem, prev(s["hidden"]))
                nc.scalar.activation(sg[64:128, b, :], ps[0:64, 2 + b, 0:256], ACT.Silu).then_inc(s["silu"].sem, 1)

            def step_hidden(dve, s, v, prev, b):
                dve.wait_ge(s["silu"].sem, v(s["silu"]))
                if prev:
                    dve.wait_ge(s["turned"].sem, prev(s["turned"]))
                nc.vector.tensor_tensor(hid[64:128, b, :], sg[64:128, b, :], ps[64:128, 2 + b, 0:256], ALU.mult)\
                    .then_inc(s["hidden"].sem, 1)

            def step_turn(pe, s, v, prev, b):
                pe.wait_ge(s["hidden"].sem, v(s["hidden"]))
                if prev:
                    pe.wait_ge(s["hT"].sem, prev(s["hT"]))
                for c2 in range(2):
                    mm = nc.tensor.matmul(ps[:, 4 + b, c2 * 64:(c2 + 1) * 64], hid[64:128, b, c2 * P:(c2 + 1) * P],
                                          ident[64:128, 64:128], start=True, stop=True)
                mm.then_inc(s["turned"].sem, 1)

            def step_hT(dve, s, v, prev, b):
                dve.wait_ge(s["turned"].sem, v(s["turned"]))
                if prev:
                    dve.wait_ge(s["down"].sem, prev(s["down"]))
                nc.vector.tensor_copy(hT[:, b, :, :], ps[:, 4 + b, 0:128].rearrange("p (a b) -> p a b", a=2))\
                    .then_inc(s["hT"].sem, 1)

            def step_down(pe, s, v, prev, b, wd):
                pe.wait_ge(s["hT"].sem, v(s["hT"]))
                if prev:
                    pe.wait_ge(s["rows"].sem, prev(s["rows"]))
                for k in range(4):
                    for j in range(4):
                        mm = nc.tensor.matmul(ps[j * CAP:(j + 1) * CAP, 6 + b, 0:256],
                                              hT[:, b, k % 2, (k // 2) * CAP:(k // 2 + 1) * CAP],
                                              wd[:, k, j * 256:(j + 1) * 256], start=(k == 0), stop=(k == 3))
                mm.then_inc(s["down"].sem, 1)

            def step_dest(dve, s, v, prev, b, stored_before):
                dve.wait_ge(s["xg"].sem, v(s["xg"]))
                if prev:
                    dve.wait_ge(s["rows"].sem, prev(s["rows"]))
                if stored_before is not None:
                    dve.wait_ge(y_st[b].sem, stored_before)
                nc.vector.tensor_copy(wcol[:, b:b + 1], xg[:, b, KD * CAP + 1:KD * CAP + 2])
                nc.vector.tensor_tensor(dest[:, b:b + 1].bitcast(I32), xg[:, b, KD * CAP:KD * CAP + 1],
                                        cst[:, C_JCOL:C_JCOL + 1], ALU.add).then_inc(s["dest"].sem, 1)

            def step_rows(dve, s, v, b, stored_before):
                dve.wait_ge(s["down"].sem, v(s["down"]))
                dve.wait_ge(s["dest"].sem, v(s["dest"]))
                if stored_before is not None:
                    dve.wait_ge(y_st[b].sem, stored_before)
                nc.vector.tensor_scalar(rows[:, b, :], ps[:, 6 + b, 0:256], wcol[:, b:b + 1], None, ALU.mult)\
                    .then_inc(s["rows"].sem, 1)

            def step_store(pool, s, v, b, last_row, step):
                pool.wait_ge(s["dest"].sem, v(s["dest"]))
                pool.wait_ge(s["rows"].sem, v(s["rows"]))
                if not (isinstance(step, int) and step == 0):
                    pool.wait_ge(ticked[layer].sem, step)
                nc.gpsimd.tensor_tensor(tick, cst[0:1, 0:1], cst[0:1, 0:1], ALU.mult).then_inc(ticked[layer].sem, 1)
                nc.gpsimd.indirect_dma_start(moe_rows[layer], bass.IndirectOffsetOnAxis(
                    ap=dest[:, b:b + 1].bitcast(I32), axis=0), rows[:, b, :], None, bounds_check=last_row,
                    oob_is_err=False).then_inc(y_st[b].sem, 16)

            def pair_view(pair, b):
                e = 2 * pair + b
                v = lambda s: s.at(e + 1)
                prev = None if isinstance(pair, int) and pair == 0 else (lambda s: s.at(e - 1))
                before = None if prev is None else 16 * pair
                return e, v, prev, before

            def next_view(pair, b):
                return pair_view(pair, 1) if b == 0 else pair_view(pair + 1, 0)

            def over_view(z):
                return lambda s: s.at(z + 1)

            for e in (NE - 2, NE - 1):
                c = first + 3 * (e - 1)
                ring.release(c, m["gateup"], e + 1)
                ring.release(c + 1, m["gateup"], e + 1)
                ring.release(c + 2, m["down"], e + 1)
            wf = [[ring.rows8(first + 3 * s), ring.rows8(first + 3 * s + 1), ring.rows4(first + 3 * s + 2)]
                  for s in range(2)]

            with nc.Block() as block:
                @block.sync
                def _(sp):
                    sp.dma_start(wr[:, :, 0:NG], t["moe_w_group"][layer].rearrange("(k p) n -> p k n", p=P))\
                        .then_inc(router_loaded.sem, 16)
                    sp.dma_start(wr[:, :, NG:NG + NE], t["moe_w_expert"][layer].rearrange("(k p) n -> p k n", p=P))\
                        .then_inc(router_loaded.sem, 16)
                    for part, name in enumerate(("moe_w_gate", "moe_w_up", "moe_w_down")):
                        sp.dma_start(w1[part], t[name][layer, 1].rearrange("(k p) n -> p k n", p=P))\
                            .then_inc(w1_loaded.sem, 16)

                    def load(e, half, used):
                        for part, name in enumerate(("moe_w_gate", "moe_w_up", "moe_w_down")):
                            c = first + 3 * half + part
                            w = t[name][layer, bass.ds(e, 1)]
                            if part == 2:
                                src, dst = w.rearrange("a (k p) n -> p (a k) n", p=P), ring.rows4(c)
                            else:
                                src, dst = w.rearrange("a (k p) n -> p (a k) n", p=P), ring.rows8(c)
                            done = m["down"] if part == 2 else m["gateup"]
                            sp.wait_ge(done.sem, done.at(used))
                            sp.dma_start(dst, src).then_inc(ring.loaded[c % RING_SLOTS], 16)

                    load(3, 0, 1)
                    with sp.Fori(1, NE // 2 - 1) as pair:
                        load(2 * pair + 2, 1, 2 * pair + 1)
                        load(2 * pair + 3, 0, 2 * pair + 2)
                    ring.issued = first + 3 * (NE - 1)
                    sp_ln_params(sp, lnp, lnp_g, lnp_b)
                    sp.wait_ge(route_dve.sem, route_dve.at(5))
                    crowded = sp.value_load(cnti[0:1, 0:1], min_val=0, max_val=SEQ)
                    with sp.If(crowded > CAP):
                        for part in range(3):
                            done = m["down"] if part == 2 else m["gateup"]
                            sp.wait_ge(done.sem, done.at(NE))
                        with sp.Fori(1, SEQ // CAP) as r:
                            with sp.Fori(0, NE) as e:
                                z = (r - 1) * NE + e
                                sp.wait_ge(y_st[0].sem, 16 * (NE // 2) + 16 * z)
                                for part, name in enumerate(("moe_w_gate", "moe_w_up", "moe_w_down")):
                                    w = t[name][layer, bass.ds(e, 1)].rearrange("a (k p) n -> p (a k) n", p=P)
                                    dst = ring.rows4(first + part) if part == 2 else ring.rows8(first + part)
                                    sp.dma_start(dst, w).then_inc(o["loaded"].sem, 16)
                        sp.wait_ge(y_st[0].sem, 16 * (NE // 2) + 16 * (SEQ // CAP - 1) * NE)
                    for b in range(2):
                        sp.wait_ge(y_st[b].sem, 16 * (NE // 2))
                    for tt in range(TT):
                        sp.dma_start(pairs[:, tt, :, :].rearrange("p j d -> p (j d)"),
                                     moe_rows[layer][8 * P * tt:8 * P * (tt + 1), :].rearrange(
                                         "(p j) d -> p (j d)", p=P)).then_inc(pairs_loaded.sem, 16)
                    if sp_next:
                        sp_next(sp, 0)
                    ring.issue(sp, first + 3 * (NE - 1) + RING_SLOTS)

                @block.tensor
                def _(pe):
                    pe_turn(pe, h)
                    pe.wait_ge(router_loaded.sem, router_loaded.at(32))
                    pe.wait_ge(turned_copied.sem, turned_copied.at(4))
                    for tt in range(TT):
                        for k in range(KD):
                            mm = nc.tensor.matmul(ps[:, 4, tt * 36:(tt + 1) * 36], xT[:, k, tt * P:(tt + 1) * P],
                                                  wr[:, k, :], start=(k == 0), stop=(k == KD - 1))
                    mm.then_inc(route_pe.sem, 1)
                    pe.wait_ge(route_dve.sem, route_dve.at(3))
                    nc.tensor.matmul(ps[:, 5, 0:NE], striu, both[:, 0, :], start=True, stop=True)
                    nc.tensor.matmul(ps[:, 5, NE:2 * NE], striu, both[:, 1, :], start=True, stop=False)
                    nc.tensor.matmul(ps[:, 5, NE:2 * NE], ones, both[:, 0, :], start=False, stop=True)
                    nc.tensor.matmul(ps[:, 5, 64:64 + NE], ones, both[:, 0, :], start=True, stop=False)
                    nc.tensor.matmul(ps[:, 5, 64:64 + NE], ones, both[:, 1, :], start=False, stop=True)\
                        .then_inc(route_pe.sem, 1)
                    pe.wait_ge(route_dve.sem, route_dve.at(5))

                    def expert(pair, b):
                        e, v, prev, before = pair_view(pair, b)
                        peeled = isinstance(pair, int) and pair == 0
                        in_arena = peeled and b == 1
                        half, turn = (0, 0) if peeled else (1 - b, pair - 1 + b)
                        w = w1 if in_arena else wf[half]
                        if in_arena:
                            pe.wait_ge(w1_loaded.sem, w1_loaded.at(48))
                        else:
                            for part in range(2):
                                ring.arrived(pe, first + 3 * half + part, turn)
                        step_gateup(pe, m, v, prev, b, w[0], w[1])
                        if not (isinstance(pair, int) and pair == NE // 2):
                            e1, v1, prev1, _ = next_view(pair, b)
                            step_pick(pe, m, v1, prev1, 1 - b, e1)
                        step_turn(pe, m, v, prev, b)
                        if not in_arena:
                            ring.arrived(pe, first + 3 * half + 2, turn)
                        step_down(pe, m, v, prev, b, w[2])

                    step_pick(pe, m, lambda s: s.at(1), None, 0, 0)
                    expert(0, 0)
                    expert(0, 1)
                    with pe.Fori(1, NE // 2) as pair:
                        expert(pair, 0)
                        expert(pair, 1)
                    crowded = pe.value_load(cnti[0:1, 0:1], min_val=0, max_val=SEQ)
                    with pe.If(crowded > CAP):
                        with pe.Fori(1, SEQ // CAP) as r:
                            with pe.Fori(0, NE) as e:
                                z = (r - 1) * NE + e
                                v = over_view(z)
                                pe.wait_ge(o["loaded"].sem, 48 * (z + 1))
                                step_pick(pe, o, v, None, 0, e)
                                step_gateup(pe, o, v, None, 0, wf[0][0], wf[0][1])
                                step_turn(pe, o, v, None, 0)
                                step_down(pe, o, v, None, 0, wf[0][2])

                @block.scalar
                def _(act):
                    act.wait_ge(route_dve.sem, route_dve.at(1))
                    for tt in range(TT):
                        nc.scalar.activation(t8[:, 0, tt, 0:NG], lg[:, tt, 0:NG], ACT.Exp, bias=r1[:, 1, tt:tt + 1],
                                             accum_out=r1[:, 2, tt:tt + 1]).then_inc(route_act.sem, 1)
                    act.wait_ge(route_dve.sem, route_dve.at(2))
                    for tt in range(TT):
                        nc.scalar.activation(t8[:, 1, tt, :], esel[:, tt, :], ACT.Exp, bias=r1[:, 4, tt:tt + 1],
                                             accum_out=r1[:, 5, tt:tt + 1]).then_inc(route_act.sem, 1)

                    def expert(pair, b):
                        e, v, prev, before = pair_view(pair, b)
                        step_silu(act, m, v, prev, b)
                        e1, v1, prev1, _ = next_view(pair, b)
                        step_xg(act, m, v1, prev1, 1 - b)

                    step_xg(act, m, lambda s: s.at(1), None, 0)
                    expert(0, 0)
                    expert(0, 1)
                    with act.Fori(1, NE // 2) as pair:
                        expert(pair, 0)
                        expert(pair, 1)
                    act.wait_ge(route_dve.sem, route_dve.at(5))
                    crowded = act.value_load(cnti[0:1, 0:1], min_val=0, max_val=SEQ)
                    with act.If(crowded > CAP):
                        with act.Fori(1, SEQ // CAP) as r:
                            with act.Fori(0, NE) as e:
                                v = over_view((r - 1) * NE + e)
                                step_xg(act, o, v, None, 0)
                                step_silu(act, o, v, None, 0)
                    act_norm(act)

                @block.gpsimd
                def _(pool):
                    last_row = pool.to_reg(8 * SEQ - 1)
                    for b in range(2):
                        step_store(pool, m, pair_view(0, b)[1], b, last_row, b)
                    with pool.Fori(1, NE // 2) as pair:
                        for b in range(2):
                            step_store(pool, m, pair_view(pair, b)[1], b, last_row, 2 * pair + b)
                    pool.wait_ge(route_dve.sem, route_dve.at(5))
                    crowded = pool.value_load(cnti[0:1, 0:1], min_val=0, max_val=SEQ)
                    with pool.If(crowded > CAP):
                        with pool.Fori(1, SEQ // CAP) as r:
                            with pool.Fori(0, NE) as e:
                                step_store(pool, o, over_view((r - 1) * NE + e), 0, last_row, r * NE + e)
                    pool_norm(pool, lnp)

                @block.vector
                def _(dve):
                    dve_turn(dve, xT)
                    V(nc.vector.memset(t8, -1.0))
                    V(nc.vector.memset(pos1, 0.0))
                    V(nc.vector.memset(info.rearrange("p a b c -> p (a b c)"), 0.0))
                    dve.wait_ge(route_pe.sem, route_pe.at(1))
                    V(nc.vector.tensor_copy(lg, ps[:, 4, 0:72].rearrange("p (a b) -> p a b", a=TT)))
                    c = [r1[:, i, :] for i in range(16)]
                    V(nc.vector.reduce_max(c[0], lg[:, :, 0:NG], AX_X))
                    nc.vector.tensor_scalar(c[1], c[0], -1.0, None, ALU.mult).then_inc(route_dve.sem, 1)
                    dve.wait_ge(route_act.sem, route_act.at(2))
                    V(nc.vector.reciprocal(c[3], c[2]))
                    V(nc.vector.tensor_tensor(t8[:, 0, :, 0:NG], t8[:, 0, :, 0:NG], bcast(c[3], NG), ALU.mult))
                    for tt in range(TT):
                        ins = nc.vector.max(t8[:, 2, tt, :], t8[:, 0, tt, :])
                    V(ins)
                    for tt in range(TT):
                        ins = nc.vector.max_index(t8[:, 3, tt, :].bitcast(U32), t8[:, 2, tt, :], t8[:, 0, tt, :])
                    V(ins)
                    V(nc.vector.tensor_copy(c[6], t8[:, 3, :, 0].bitcast(U32)))
                    V(nc.vector.tensor_tensor(gmask, cst[:, C_IOTA:C_IOTA + NG].unsqueeze(1).to_broadcast([P, TT, NG]),
                                              bcast(c[6], NG), ALU.is_equal))
                    for tt in range(TT):
                        ins = nc.vector.tensor_tensor(gsel[:, tt, :, :],
                                                      lg[:, tt, NG:NG + NE].rearrange("p (g e) -> p g e", g=NG),
                                                      bcast(gmask[:, tt, :], EG), ALU.mult)
                    V(ins)
                    V(nc.vector.tensor_reduce(esel, gsel.rearrange("p t g e -> p t e g"), AX_X, ALU.add))
                    V(nc.vector.reduce_max(c[8], esel, AX_X))
                    nc.vector.tensor_scalar(c[4], c[8], -1.0, None, ALU.mult).then_inc(route_dve.sem, 1)
                    dve.wait_ge(route_act.sem, route_act.at(4))
                    V(nc.vector.reciprocal(c[9], c[5]))
                    V(nc.vector.tensor_tensor(t8[:, 1, :, :], t8[:, 1, :, :], bcast(c[9], EG), ALU.mult))
                    for tt in range(TT):
                        ins = nc.vector.max(t8[:, 4, tt, :], t8[:, 1, tt, :])
                    V(ins)
                    for tt in range(TT):
                        ins = nc.vector.max_index(t8[:, 5, tt, :].bitcast(U32), t8[:, 4, tt, :], t8[:, 1, tt, :])
                    V(ins)
                    for j in range(2):
                        ins = nc.vector.tensor_copy(c[14 + j], t8[:, 5, :, j].bitcast(U32))
                    V(ins)
                    for j in range(2):
                        ins = nc.vector.scalar_tensor_tensor(c[14 + j], c[6], float(EG), c[14 + j], ALU.mult, ALU.add)
                    V(ins)
                    for j in range(2):
                        ins = nc.vector.tensor_tensor(chosen[:, :, j, :],
                                                      cst[:, C_IOTA:C_IOTA + NE].unsqueeze(1).to_broadcast([P, TT, NE]),
                                                      bcast(c[14 + j], NE), ALU.is_equal)
                    V(ins)
                    nc.vector.tensor_tensor(both, chosen[:, :, 0, :], chosen[:, :, 1, :], ALU.add)\
                        .then_inc(route_dve.sem, 1)
                    dve.wait_ge(route_dve.sem, route_dve.at(3))
                    V(nc.vector.tensor_tensor(c[10], t8[:, 4, :, 0], t8[:, 4, :, 1], ALU.add))
                    V(nc.vector.reciprocal(c[11], c[10]))
                    V(nc.vector.tensor_tensor(c[11], c[11], t8[:, 2, :, 0], ALU.mult))
                    for j in range(2):
                        ins = nc.vector.tensor_tensor(c[12 + j], t8[:, 4, :, j], c[11], ALU.mult)
                    V(ins)
                    for j in range(2):
                        ins = nc.vector.tensor_tensor(wpart[:, :, j, :], chosen[:, :, j, :], bcast(c[12 + j], NE),
                                                      ALU.mult)
                    V(ins)
                    V(nc.vector.tensor_tensor(info[:, :, 0:NE, 1], wpart[:, :, 0, :], wpart[:, :, 1, :], ALU.add))
                    V(nc.vector.tensor_tensor(info[:, :, 0:NE, 0], both, bcast(cst[:, C_TOK8:C_TOK8 + TT], NE),
                                              ALU.mult))
                    V(nc.vector.scalar_tensor_tensor(info[:, :, 0:NE, 0], chosen[:, :, 1, :], 4.0,
                                                     info[:, :, 0:NE, 0], ALU.mult, ALU.add))
                    V(nc.vector.memset(cnt[:, 1:2], 0.0))
                    dve.wait_ge(route_pe.sem, route_pe.at(2))
                    for tt in range(TT):
                        V(nc.vector.scalar_tensor_tensor(pos1[:, tt, 0:NE], ps[:, 5, tt * NE:(tt + 1) * NE], 1.0,
                                                         both[:, tt, :], ALU.add, ALU.mult))
                    nc.vector.reduce_max(cnt[:, 0:1], ps[:, 5, 64:64 + NE], AX_X).then_inc(route_dve.sem, 1)
                    dve.wait_ge(route_dve.sem, route_dve.at(4))
                    nc.vector.tensor_copy(cnti[:, 0:1], cnt[:, 0:1]).then_inc(route_dve.sem, 1)

                    def expert(pair, b):
                        e, v, prev, before = pair_view(pair, b)
                        e1, v1, prev1, before1 = next_view(pair, b)
                        step_slots(dve, m, v1, prev1, 1 - b, e1, pos1)
                        step_hidden(dve, m, v, prev, b)
                        step_dest(dve, m, v1, prev1, 1 - b, before1)
                        step_hT(dve, m, v, prev, b)
                        step_rows(dve, m, v, b, before)

                    step_slots(dve, m, lambda s: s.at(1), None, 0, 0, pos1)
                    step_dest(dve, m, lambda s: s.at(1), None, 0, None)
                    expert(0, 0)
                    expert(0, 1)
                    with dve.Fori(1, NE // 2) as pair:
                        expert(pair, 0)
                        expert(pair, 1)
                    crowded = dve.value_load(cnti[0:1, 0:1], min_val=0, max_val=SEQ)
                    with dve.If(crowded > CAP):
                        with dve.Fori(1, SEQ // CAP) as r:
                            nc.vector.tensor_scalar(pos1[:, :, 0:NE], pos1[:, :, 0:NE], -float(CAP), None, ALU.add)\
                                .then_inc(o["shifted"].sem, 1)
                            with dve.Fori(0, NE) as e:
                                z = (r - 1) * NE + e
                                v = over_view(z)
                                dve.wait_ge(o["loaded"].sem, 48 * (z + 1))
                                dve.wait_ge(o["shifted"].sem, r)
                                step_slots(dve, o, v, None, 0, e, pos1)
                                step_dest(dve, o, v, None, 0, None)
                                step_hidden(dve, o, v, None, 0)
                                step_hT(dve, o, v, None, 0)
                                step_rows(dve, o, v, 0, None)
                    dve.wait_ge(pairs_loaded.sem, pairs_loaded.at(32))
                    for tt in range(TT):
                        V(nc.vector.scalar_tensor_tensor(h[:, tt, :], h[:, tt, :], ALPHA, pairs[:, tt, 0, :],
                                                         ALU.mult, ALU.add))
                    for tt in range(TT):
                        V(nc.vector.tensor_tensor(h[:, tt, :], h[:, tt, :], pairs[:, tt, 1, :], ALU.add))
                        dve_stats(tt)
                    dve_layer_norm(dve, lnp)

            turn_done()
            for s, n in ((route_pe, 2), (route_act, 4), (route_dve, 5), (router_loaded, 32), (w1_loaded, 48), (pairs_loaded, 32)):
                s.advance(n)
            norm_done()
            for name, s in m.items():
                s.advance(NE + 1 if name in ("slots", "picked", "xg", "dest") else NE)

        moe(0, t["ln_ffn_g"][0], t["ln_ffn_b"][0])

        projected, projected_copied = sem("projected"), sem("projected_copied")
        jobs_turned, jobs_copied = sem("jobs_turned"), sem("jobs_copied")

        def pe_project(pe, chunks, lo, hi, bank):
            for n in range(lo, hi):
                c, tt = chunks[n // 2], n % 2
                n_cols = ring.chunks[c].shape[2]
                w = ring.rows8(c, n_cols)
                if tt == 0 or n == lo:
                    ring.arrived(pe, c)
                if n >= 4:
                    pe.wait_ge(projected_copied.sem, projected_copied.at(n - 3))
                for k in range(KD):
                    mm = nc.tensor.matmul(ps[:, bank + n % 4, 0:n_cols], xT_att[:, k, tt * P:(tt + 1) * P], w[:, k, :],
                                          start=(k == 0), stop=(k == KD - 1))
                mm.then_inc(projected.sem, 1)

        def act_project(act, chunks, dst, cols, lo, hi, bank):
            for n in range(lo, hi):
                q, tt = n // 2, n % 2
                n_cols = ring.chunks[chunks[q]].shape[2]
                act.wait_ge(projected.sem, projected.at(n + 1))
                nc.scalar.activation(dst[:, tt, cols[q]:cols[q] + n_cols], ps[:, bank + n % 4, 0:n_cols], ACT.Copy)\
                    .then_inc(projected_copied.sem, 1)

        def release_projected(chunks):
            for q, c in enumerate(chunks):
                ring.release(c, projected, 2 * q + 2)

        def project_done(chunks):
            projected.advance(2 * len(chunks))
            projected_copied.advance(2 * len(chunks))

        def pe_jobs(pe, jobs, first=0):
            for m, (blocks, dst, gain) in enumerate(jobs, first):
                if m >= 4:
                    pe.wait_ge(jobs_copied.sem, jobs_copied.at(m - 3))
                n_rows = blocks[0].shape[1]
                for i, src in enumerate(blocks):
                    mm = nc.tensor.transpose(ps[0:n_rows, m % 4, i * P:(i + 1) * P], src, ident)
                mm.then_inc(jobs_turned.sem, 1)

        def dve_jobs(dve, jobs, first=0):
            for m, (blocks, dst, gain) in enumerate(jobs, first):
                dve.wait_ge(jobs_turned.sem, jobs_turned.at(m + 1))
                src = ps[0:blocks[0].shape[1], m % 4, 0:len(blocks) * P]
                if len(dst.shape) == 3:
                    src = src.rearrange("p (a b) -> p a b", a=dst.shape[1])
                if gain is None:
                    ins = nc.vector.tensor_copy(dst, src)
                else:
                    ins = nc.vector.tensor_scalar(dst, src, gain, None, ALU.mult)
                ins.then_inc(jobs_copied.sem, 1)

        def jobs_done(n):
            jobs_turned.advance(n)
            jobs_copied.advance(n)

        def rope(x, heads, half, cos, sin, tmp):
            r1, r2 = x[:, :, 0:half], x[:, :, half:2 * half]
            c = cos.unsqueeze(1).to_broadcast([P, heads, half])
            s = sin.unsqueeze(1).to_broadcast([P, heads, half])
            t = [tmp[:, i * heads * half:(i + 1) * heads * half].rearrange("p (a b) -> p a b", a=heads)
                 for i in range(4)]
            nc.vector.tensor_tensor(t[0], r1, c, ALU.mult)
            nc.vector.tensor_tensor(t[1], r2, s, ALU.mult)
            nc.vector.tensor_tensor(t[2], r2, c, ALU.mult)
            V(nc.vector.tensor_tensor(t[3], r1, s, ALU.mult))
            nc.vector.tensor_tensor(r1, t[0], t[1], ALU.subtract)
            V(nc.vector.tensor_tensor(r2, t[2], t[3], ALU.add))

        U = {n: sem("att_" + n) for n in ("scores", "masked", "exps", "probs", "turned", "probsT", "out", "copied")}
        st = tiny[:, 130:170]
        st_max = st[:, 0:4].rearrange("p (a b) -> p a b", a=2)
        st_nmax = st[:, 4:8].rearrange("p (a b) -> p a b", a=2)
        st_sum = st[:, 8:12].rearrange("p (a b) -> p a b", a=2)
        st_inv = st[:, 12:16].rearrange("p (a b) -> p a b", a=2)
        neg_lam = st[:, 16:17]

        class Unit:

            def __init__(self, i, q, k, mask, times, scale, v, pair):
                self.i, self.q, self.k, self.mask, self.times = i, q, k, mask, times
                self.scale, self.v, self.pair, self.kv = scale, v, pair, (i + 1) * P

        def pe_units(pe, units, pT, probs, joined):
            def scores(n):
                u, b = units[n], n % 2
                if n >= 2:
                    pe.wait_ge(U["masked"].sem, U["masked"].at(n - 1))
                for c in range(2):
                    mm = nc.tensor.matmul(ps[:, 2 * b + c, 0:u.kv], u.q[c], u.k[c], start=True, stop=True)
                mm.then_inc(U["scores"].sem, 1)

            def turn(n):
                u, b = units[n], n % 2
                pe.wait_ge(U["probs"].sem, U["probs"].at(n + 1))
                if n >= 2:
                    pe.wait_ge(U["probsT"].sem, U["probsT"].at(n - 1))
                nk = u.kv // P
                for c in range(1 if joined is not None else 2):
                    src = joined[:, b, :] if joined is not None else probs[:, b, c, :]
                    for kt in range(nk):
                        at = (c * nk + kt) * P
                        mm = nc.tensor.transpose(ps[:, 4 + b, at:at + P], src[:, kt * P:(kt + 1) * P], ident)
                mm.then_inc(U["turned"].sem, 1)

            def values(n):
                u, b = units[n], n % 2
                pe.wait_ge(U["probsT"].sem, U["probsT"].at(n + 1))
                if n >= 2:
                    pe.wait_ge(U["copied"].sem, U["copied"].at(n - 1))
                nk = u.kv // P
                if joined is not None:
                    for kt in range(nk):
                        mm = nc.tensor.matmul(ps[:, 6 + b, 0:P], pT[:, b, kt * P:(kt + 1) * P], u.v(0, kt),
                                              start=(kt == 0), stop=(kt == nk - 1))
                else:
                    for c in range(2):
                        for kt in range(nk):
                            at = (c * nk + kt) * P
                            mm = nc.tensor.matmul(ps[c * HD:(c + 1) * HD, 6 + b, 0:P], u.v(c, kt), pT[:, b, at:at + P],
                                                  start=(kt == 0), stop=(kt == nk - 1))
                mm.then_inc(U["out"].sem, 1)

            N = len(units)
            scores(0)
            scores(1)
            for n in range(N):
                if n + 2 < N:
                    scores(n + 2)
                turn(n)
                if n:
                    values(n - 1)
            values(N - 1)

        def act_units(act, units, sm, probs, pT, joined, copy_out):
            def exps(n):
                u, b = units[n], n % 2
                act.wait_ge(U["masked"].sem, U["masked"].at(n + 1))
                if n >= 2:
                    act.wait_ge(U["turned"].sem, U["turned"].at(n - 1))
                for c in range(2):
                    ins = nc.scalar.activation(probs[:, b, c, 0:u.kv], sm[:, b, c, 0:u.kv], ACT.Exp,
                                               bias=st_nmax[:, b, c:c + 1], scale=u.scale,
                                               accum_out=st_sum[:, b, c:c + 1])
                ins.then_inc(U["exps"].sem, 1)

            def copy_turned(n):
                u, b = units[n], n % 2
                act.wait_ge(U["turned"].sem, U["turned"].at(n + 1))
                if n >= 2:
                    act.wait_ge(U["out"].sem, U["out"].at(n - 1))
                w = u.kv * (1 if joined is not None else 2)
                nc.scalar.activation(pT[:, b, 0:w], ps[:, 4 + b, 0:w], ACT.Copy).then_inc(U["probsT"].sem, 1)

            def outputs(n):
                act.wait_ge(U["out"].sem, U["out"].at(n + 1))
                copy_out(act, units[n], n).then_inc(U["copied"].sem, 1)

            N = len(units)
            exps(0)
            for n in range(N):
                if n + 1 < N:
                    exps(n + 1)
                copy_turned(n)
                if n:
                    outputs(n - 1)
            outputs(N - 1)

        def dve_units(dve, units, sm, probs, joined):
            def mask(n):
                u, b = units[n], n % 2
                dve.wait_ge(U["scores"].sem, U["scores"].at(n + 1))
                if n >= 2:
                    dve.wait_ge(U["exps"].sem, U["exps"].at(n - 1))
                V(nc.vector.tensor_tensor(sm[:, b, :, 0:u.kv], ps[:, 2 * b:2 * b + 2, 0:u.kv],
                                          u.mask.unsqueeze(1).to_broadcast([P, 2, u.kv]), ALU.add))
                V(nc.vector.reduce_max(st_max[:, b, :], sm[:, b, :, 0:u.kv], AX_X))
                nc.vector.tensor_scalar(st_nmax[:, b, :], st_max[:, b, :], -u.scale, None, ALU.mult)\
                    .then_inc(U["masked"].sem, 1)

            def normalise(n):
                u, b = units[n], n % 2
                dve.wait_ge(U["exps"].sem, U["exps"].at(n + 1))
                if u.times is not None:
                    for c in range(2):
                        ins = nc.vector.scalar_tensor_tensor(probs[:, b, c, 0:u.kv], probs[:, b, c, 0:u.kv], 1.0,
                                                             u.times, ALU.mult, ALU.mult,
                                                             accum_out=st_sum[:, b, c:c + 1])
                    V(ins)
                V(nc.vector.reciprocal(st_inv[:, b, :], st_sum[:, b, :]))
                if joined is not None:
                    if n >= 2:
                        dve.wait_ge(U["turned"].sem, U["turned"].at(n - 1))
                    nc.vector.tensor_scalar(st_inv[:, b, 1:2], st_inv[:, b, 1:2], neg_lam, None, ALU.mult)
                    V(nc.vector.tensor_scalar(joined[:, b, 0:u.kv], probs[:, b, 0, 0:u.kv], st_inv[:, b, 0:1], None,
                                              ALU.mult))
                    nc.vector.scalar_tensor_tensor(joined[:, b, 0:u.kv], probs[:, b, 1, 0:u.kv], st_inv[:, b, 1:2],
                                                   joined[:, b, 0:u.kv], ALU.mult, ALU.add)\
                        .then_inc(U["probs"].sem, 1)
                else:
                    nc.vector.tensor_tensor(probs[:, b, :, 0:u.kv], probs[:, b, :, 0:u.kv],
                                            bcast(st_inv[:, b, :], u.kv), ALU.mult).then_inc(U["probs"].sem, 1)

            N = len(units)
            mask(0)
            mask(1)
            for n in range(N):
                normalise(n)
                if n + 2 < N:
                    mask(n + 2)

        def units_done(n):
            for s in U.values():
                s.advance(n)

        caus = [cst[:, C_CAUS0:C_CAUS0 + P], cst[:, C_CAUS1:C_CAUS1 + SEQ]]

        AH = 8
        qkv = area(0, TT, 3 * D)
        xT_att = area(6144, KD, SEQ)
        oT = xT_att
        qkT = area(8192, 2, AH, SEQ)
        sm = area(12288, 2, 2, SEQ)
        probs = area(13312, 2, 2, SEQ)
        joined = area(14336, 2, SEQ)
        pT = area(14848, 2, SEQ)
        o_tok = area(15360, TT, AH, P)
        lam_rows = area(17408, 4, 64)
        lam_prod = area(17664, 2, 64)
        rt = area(17792, 200)
        posi = rt[:, 0:2].bitcast(I32)
        posf = rt[:, 2:4]
        ang, turns, red, cosr = rt[:, 4:20], rt[:, 20:36], rt[:, 36:52], rt[:, 52:68]
        sin_t, cos_t, over_t = rt[:, 68:84], rt[:, 84:100], rt[:, 100:116]
        lam_sum = rt[:, 116:118]
        subln = rt[:, 118:119]
        subln_s = rt[:, 119:120]
        ossq = rt[:, 120:136].rearrange("p (a b) -> p a b", a=TT)
        ov, orr, ot = rt[:, 136:152], rt[:, 152:168], rt[:, 168:184]
        rope_tmp = area(17992, 4 * 32 * 8)
        osq = area(19016, P)
        lnp = area(0, 2, D)
        att_loaded, tables, lam_ready, tables_dve, o_scaled, oT_ready = (
            sem("att_loaded"), sem("tables"), sem("lam_ready"), sem("tables_dve"), sem("o_scaled"), sem("oT_ready"))
        roped = sem("roped")
        release_projected(c_qkv)
        release_summed(c_wo)

        units = []
        for hh in range(AH):
            for i in range(TT):
                units.append(Unit(
                    i, [qkT[64 * c:64 * c + 64, 0, hh, i * P:(i + 1) * P] for c in range(2)],
                    [qkT[64 * c:64 * c + 64, 1, hh, 0:(i + 1) * P] for c in range(2)], caus[i], None, 64 ** -0.5,
                    lambda c, kt, hh=hh: qkv[:, kt, 2 * D + hh * P:2 * D + (hh + 1) * P], hh))
        head_jobs = [([qkv[:, tt, a * D + hh * P:a * D + (hh + 1) * P] for hh in (2 * hp, 2 * hp + 1)
                       for tt in range(TT)],
                      qkT[:, a, 2 * hp:2 * hp + 2, :].rearrange("p a b -> p (a b)"), None)
                     for a in range(2) for hp in range(4)]
        out_jobs = [([o_tok[:, tt, hh, :] for hh in (2 * hp, 2 * hp + 1) for tt in range(TT)],
                     oT[:, 2 * hp:2 * hp + 2, :].rearrange("p a b -> p (a b)"), subln_s) for hp in range(4)]
        with nc.Block() as block:
            @block.sync
            def _(sp):
                for i, name in enumerate(("attn_lam_q1", "attn_lam_k1", "attn_lam_q2", "attn_lam_k2")):
                    sp.dma_start(lam_rows[:, i, :], t[name][0].partition_broadcast(P)).then_inc(att_loaded.sem, 16)
                sp.dma_start(posi, t["positions"][0].rearrange("(a p) -> p a", p=P), allow_slow_non_contiguous=True).then_inc(att_loaded.sem, 16)
                sp.dma_start(subln, t["attn_subln_w"][0].rearrange("(p a) -> p a", a=1),
                             allow_slow_non_contiguous=True).then_inc(att_loaded.sem, 16)
                ring.issue(sp, c_qkv[-1] + 1 + RING_SLOTS)
                sp.wait_ge(U["copied"].sem, U["copied"].at(len(units)))
                sp_ln_params(sp, lnp, t["ln_mix_g"][1], t["ln_mix_b"][1])
                ring.issue(sp, c_wo[-1] + 1 + RING_SLOTS)

            @block.tensor
            def _(pe):
                pe_turn(pe, h)
                pe.wait_ge(turned_copied.sem, turned_copied.at(4))
                pe_project(pe, c_qkv, 0, 12, 0)
                pe.wait_ge(projected_copied.sem, projected_copied.at(12))
                pe.wait_ge(roped.sem, 1)
                pe_jobs(pe, head_jobs)
                pe.wait_ge(jobs_copied.sem, jobs_copied.at(8))
                pe_units(pe, units, pT, probs, joined)
                pe.wait_ge(o_scaled.sem, 1)
                pe_jobs(pe, out_jobs, 8)
                pe.wait_ge(jobs_copied.sem, jobs_copied.at(12))
                pe_sum_chunks(pe, c_wo, lambda k, tt: oT[:, k, tt * P:(tt + 1) * P])

            @block.scalar
            def _(act):
                act.wait_ge(tables.sem, 1)
                nc.scalar.activation(sin_t, red, ACT.Sin)
                nc.scalar.activation(cos_t, cosr, ACT.Sin).then_inc(tables_dve.sem, 1)
                act.wait_ge(tables.sem, 2)
                nc.scalar.activation(lam_sum, lam_sum, ACT.Exp).then_inc(tables_dve.sem, 1)
                act_project(act, c_qkv, qkv, [512 * q for q in range(6)], 0, 12, 0)

                def copy_out(act, u, n):
                    o = o_tok[:, u.i, u.pair, :]
                    nc.scalar.activation(o, ps[:, 6 + n % 2, 0:P], ACT.Copy)
                    if n:
                        act.wait_ge(U["copied"].sem, U["copied"].at(n))
                    return nc.scalar.activation(osq, ps[:, 6 + n % 2, 0:P], ACT.Square,
                                                accum_out=ossq[:, u.i, u.pair:u.pair + 1])

                act_units(act, units, sm, probs, pT, joined, copy_out)
                act_norm(act)

            @block.gpsimd
            def _(pool):
                pool_norm(pool, lnp)

            @block.vector
            def _(dve):
                dve_turn(dve, xT_att)
                dve.wait_ge(att_loaded.sem, 6 * 16)
                V(nc.vector.tensor_copy(posf, posi))
                for tt in range(TT):
                    V(nc.vector.tensor_scalar(ang[:, 8 * tt:8 * tt + 8], cst[:, C_INVF:C_INVF + 8], posf[:, tt:tt + 1],
                                              None, ALU.mult))
                V(nc.vector.tensor_scalar(turns, ang, 1 / TWO_PI, ROUND, ALU.mult, ALU.add))
                V(nc.vector.tensor_scalar(turns, turns, ROUND, None, ALU.subtract))
                V(nc.vector.scalar_tensor_tensor(red, turns, -6.28125, ang, ALU.mult, ALU.add))
                V(nc.vector.scalar_tensor_tensor(red, turns, -(TWO_PI - 6.28125), red, ALU.mult, ALU.add))
                V(nc.vector.tensor_scalar(cosr, red, TWO_PI / 4, None, ALU.add))
                V(nc.vector.tensor_scalar(over_t, cosr, TWO_PI / 2, -TWO_PI, ALU.is_gt, ALU.mult))
                V(nc.vector.tensor_tensor(cosr, cosr, over_t, ALU.add))
                V(nc.vector.tensor_scalar(cosr, cosr, 3.1415925, -3.1415925, ALU.min, ALU.max))
                nc.vector.tensor_scalar(red, red, 3.1415925, -3.1415925, ALU.min, ALU.max).then_inc(tables.sem, 1)
                V(nc.vector.tensor_tensor(lam_prod, lam_rows[:, 0:4:2, :], lam_rows[:, 1:4:2, :], ALU.mult))
                nc.vector.reduce_sum(lam_sum, lam_prod, AX_X).then_inc(tables.sem, 1)
                dve.wait_ge(tables_dve.sem, 2)
                V(nc.vector.tensor_tensor(neg_lam, lam_sum[:, 1:2], lam_sum[:, 0:1], ALU.subtract))
                V(nc.vector.tensor_scalar(neg_lam, neg_lam, -LAMBDA_INIT, None, ALU.add))
                V(nc.vector.tensor_scalar(subln_s, subln, 1.0 - LAMBDA_INIT, None, ALU.mult))
                dve.wait_ge(projected_copied.sem, projected_copied.at(8))
                for tt in range(TT):
                    rope(qkv[:, tt, 0:2 * D].rearrange("p (a b) -> p a b", b=64), 32, 8,
                         cos_t[:, 8 * tt:8 * tt + 8], sin_t[:, 8 * tt:8 * tt + 8], rope_tmp)
                nc.vector.memset(ot, 0.0).then_inc(roped.sem, 1)
                dve_jobs(dve, head_jobs)
                dve_units(dve, units, sm, probs, joined)
                dve.wait_ge(U["copied"].sem, U["copied"].at(len(units)))
                V(nc.vector.tensor_scalar(ov, ossq.rearrange("p a b -> p (a b)"), 1.0 / P, EPS, ALU.mult, ALU.add))
                rsqrt(orr, ov, ot)
                for tt in range(TT):
                    ins = nc.vector.tensor_tensor(o_tok[:, tt, :, :], o_tok[:, tt, :, :],
                                                  bcast(orr[:, 8 * tt:8 * tt + 8], P), ALU.mult)
                ins.then_inc(o_scaled.sem, 1)
                dve_jobs(dve, out_jobs, 8)
                dve_add_sums(dve, len(c_wo), True)
                dve_layer_norm(dve, lnp)

        turn_done()
        project_done(c_qkv)
        jobs_done(12)
        units_done(len(units))
        sums_done(len(c_wo))
        norm_done()

        prm2 = area(17808, 2, P)
        w_uq, w_ukv = area(16528, 2, 384), area(17296, 512)
        small_loaded = sem("small_loaded")

        def sp_small_params(sp, l):
            rows = [(0, 0, t["conv_w_2"][l, 0:2].rearrange("j (f p) -> (j f) p", p=P)),
                    (0, 88, t["g_attn_2"][l].rearrange("(f p) -> f p", p=P)),
                    (0, 96, t["g_ffn_2"][l].rearrange("(f p) -> f p", p=P)),
                    (0, 104, t["g_q_lat_2"][l].rearrange("(f p) -> f p", p=P)),
                    (0, 106, t["g_kv_lat_2"][l].rearrange("(f p) -> f p", p=P)),
                    (1, 0, t["conv_w_2"][l, 2].rearrange("(f p) -> f p", p=P)),
                    (1, 44, t["conv_b_2"][l].rearrange("(f p) -> f p", p=P))]
            for a, r, src in rows:
                sp.dma_start(prm2[r:r + src.shape[0], a, :], src).then_inc(small_loaded.sem, 16)
            sp.dma_start(w_uq, t["w_uq_2"][l].rearrange("(k p) n -> p k n", p=P)).then_inc(small_loaded.sem, 16)
            sp.dma_start(w_ukv, t["w_ukv_2"][l]).then_inc(small_loaded.sem, 16)

        moe(1, t["ln_ffn_g"][1], t["ln_ffn_b"][1], sp_small_params)

        TOPK = min(256, SEQ // 4)
        LH, DH, SH, IH = 4, 8, 4, 8
        Z_KV, Z_PE, Z_DIL, Z_DSA, Z_IDX, Z_W = 256, 384, 416, 1952, 2720, 3008
        TAKEN = -3e38
        zz = area(0, TT, N_IN2)
        xT_att = area(6032, KD, SEQ)
        latT = area(6032, 2, LH, SEQ)
        tn = area(8080, TT, D)
        dilT = area(8080, 2, 4, SEQ)
        idx_terms = area(8080, 2, 4, SEQ)
        rtmp = area(19088, 4 * 16 * 8)
        mixT = area(10128, KD, SEQ)
        cn = area(10128, TT, 384)
        cT = area(10896, 3, SEQ)
        kidx4 = area(11664, TT, P)
        qkm = area(12176, TT, 2, LH, 96)
        kvb = area(13712, TT, 512)
        dsaT = area(14736, 2, 2, SEQ)
        idxT = area(15760, 3, SEQ)
        sm2, probs2, pT2 = area(16528, 2, 2, SEQ), area(17552, 2, 2, SEQ), area(18576, 2, 512)
        best = area(18064, 2, 8)
        work = area(18576, 2, SEQ)
        dsa_mask = area(19600, 2, SEQ)
        rms_s, rms_v, rms_r, rms_t = tiny[:, 170:176], tiny[:, 176:182], tiny[:, 182:188], tiny[:, 188:194]
        w_idx = tiny[:, 194:210].rearrange("p (a b) -> p a b", a=TT)
        taps2 = [pcol[:, 0:44], pcol[:, 44:88], pcol[:, 107:151]]
        bias2 = pcol[:, 151:195]
        g_att, g_mlp, g_ql, g_kvl = pcol[:, 88:96], pcol[:, 96:104], pcol[:, 104:106], pcol[:, 106:107]

        squared, scaled, lat_squared, lat_ready, lat_copied = (
            sem("squared"), sem("scaled"), sem("lat_squared"), sem("lat_ready"), sem("lat_copied"))
        params2_turned, params2_copied = sem("params2_turned"), sem("params2_copied")
        ready2, idx_scores, idx_read = sem("ready2"), sem("idx_scores"), sem("idx_read")
        dsa_masked = sem("dsa_masked")
        up_ready, up_begun, up_summed, gate_done, up_done = (sem("up_ready"), sem("up_begun"), sem("up_summed"),
                                                             sem("gate_done"), sem("up_done"))
        final_loaded, final_stored, final_done = sem("final_loaded"), sem("final_stored"), sem("final_done")

        def act_squares(act, junk):
            for tt in range(TT):
                A(nc.scalar.activation(junk[:, tt, :], h[:, tt, :], ACT.Square, accum_out=rms_s[:, tt:tt + 1]))
            nc.scalar.activation(rms_v[:, 2:3], rms_s[:, 0:1], ACT.Copy).then_inc(squared.sem, 1)

        def dve_scale(dve, dst):
            dve.wait_ge(squared.sem, squared.at(1))
            V(nc.vector.tensor_scalar(rms_v[:, 0:2], rms_s[:, 0:2], 1.0 / D, EPS2, ALU.mult, ALU.add))
            rsqrt(rms_r[:, 0:2], rms_v[:, 0:2], rms_t[:, 0:2])
            for tt in range(TT):
                ins = nc.vector.tensor_scalar(dst[:, tt, :], h[:, tt, :], rms_r[:, tt:tt + 1], None, ALU.mult)
            ins.then_inc(scaled.sem, 1)

        def attention_layer(l):
            release_projected(c_in2[l])
            release_summed(c_wo2[l])
            chunk_cols = [(tt, k) for tt in range(TT) for k in range(KD)]
            lat_jobs = [([cn[:, tt, i * P:(i + 1) * P] for tt in range(TT)], cT[:, i, :],
                         g_ql[:, i:i + 1] if i < 2 else g_kvl) for i in range(3)]
            idx_jobs = [([zz[:, tt, Z_IDX + p2 * P:Z_IDX + (p2 + 1) * P] for p2 in range(2) for tt in range(TT)],
                         idxT[:, 0:2, :].rearrange("p a b -> p (a b)"), None),
                        ([kidx4[:, tt, :] for tt in range(TT)], idxT[:, 2, :], None)]
            dil_jobs = [([zz[:, tt, Z_DIL + a * 512 + p2 * P:Z_DIL + a * 512 + (p2 + 1) * P]
                          for p2 in (2 * hp, 2 * hp + 1) for tt in range(TT)],
                         dilT[:, a, 2 * hp:2 * hp + 2, :].rearrange("p a b -> p (a b)"), None)
                        for a in range(2) for hp in range(2)]
            head_jobs = [([qkm[:, tt, a, hh, :] for hh in (2 * hp, 2 * hp + 1) for tt in range(TT)],
                          latT[0:96, a, 2 * hp:2 * hp + 2, :].rearrange("p a b -> p (a b)"), None)
                         for a in range(2) for hp in range(2)]
            head_jobs += [([zz[:, tt, Z_DSA + a * 256 + p2 * P:Z_DSA + a * 256 + (p2 + 1) * P]
                            for p2 in range(2) for tt in range(TT)],
                           dsaT[:, a, :, :].rearrange("p a b -> p (a b)"), None) for a in range(2)]
            units = []
            for p2 in range(LH // 2):
                for i in range(TT):
                    units.append(Unit(
                        i, [latT[0:96, 0, 2 * p2 + c, i * P:(i + 1) * P] for c in range(2)],
                        [latT[0:96, 1, 2 * p2 + c, 0:(i + 1) * P] for c in range(2)], caus[i], None, 96 ** -0.5,
                        lambda c, kt, p2=p2: kvb[:, kt, (2 * p2 + c) * P + HD:(2 * p2 + c + 1) * P], p2))
            for p2 in range(DH // 2):
                for i in range(TT):
                    mask = caus[0] if i == 0 else cst[:, C_WIN1:C_WIN1 + SEQ]
                    times = cst[:, C_MUL0:C_MUL0 + P] if i == 0 else cst[:, C_MUL1:C_MUL1 + SEQ]
                    units.append(Unit(
                        i, [dilT[64 * c:64 * c + 64, 0, p2, i * P:(i + 1) * P] for c in range(2)],
                        [dilT[64 * c:64 * c + 64, 1, p2, 0:(i + 1) * P] for c in range(2)], mask, times, HD ** -0.5,
                        lambda c, kt, p2=p2: zz[:, kt, Z_DIL + 1024 + (2 * p2 + c) * HD:
                                                Z_DIL + 1024 + (2 * p2 + c + 1) * HD], 2 + p2))
            for p2 in range(SH // 2):
                for i in range(TT):
                    units.append(Unit(
                        i, [dsaT[64 * c:64 * c + 64, 0, p2, i * P:(i + 1) * P] for c in range(2)],
                        [dsaT[64 * c:64 * c + 64, 1, p2, 0:(i + 1) * P] for c in range(2)],
                        dsa_mask[:, i, 0:(i + 1) * P], None, HD ** -0.5,
                        lambda c, kt, p2=p2: zz[:, kt, Z_DSA + 512 + (2 * p2 + c) * HD:
                                                Z_DSA + 512 + (2 * p2 + c + 1) * HD], 6 + p2))
            n_units = len(units)

            def tables_of(tt):
                out, col = [], C_ROPE + 56 * tt
                for half in (16, 8, 4):
                    out.append((cst[:, col:col + half], cst[:, col + half:col + 2 * half]))
                    col += 2 * half
                return out

            with nc.Block() as block:
                @block.sync
                def _(sp):
                    ring.issue(sp, c_wo2[l][-1] + 1 + RING_SLOTS)

                @block.tensor
                def _(pe):
                    pe.wait_ge(small_loaded.sem, small_loaded.at(9 * 16))
                    nc.tensor.transpose(ps[:, 4, 0:107], prm2[0:107, 0, :], ident[0:107, 0:107])
                    nc.tensor.transpose(ps[:, 4, 107:195], prm2[0:88, 1, :], ident[0:88, 0:88])\
                        .then_inc(params2_turned.sem, 1)
                    pe.wait_ge(scaled.sem, scaled.at(1))
                    pe_turn(pe, tn)
                    pe.wait_ge(turned_copied.sem, turned_copied.at(4))
                    def idx_products(i):
                        kv = (i + 1) * P
                        for a in range(2):
                            for m in range(4):
                                rows = slice(32 * m, 32 * m + 32)
                                mm = nc.tensor.matmul(ps[:, m, a * SEQ:a * SEQ + kv], idxT[rows, a, i * P:(i + 1) * P],
                                                      idxT[rows, 2, 0:kv], start=True, stop=True)
                        mm.then_inc(idx_scores.sem, 1)

                    pe_project(pe, c_in2[l], 0, 6, 4)
                    pe.wait_ge(ready2.sem, ready2.at(1))
                    pe_jobs(pe, lat_jobs + idx_jobs)
                    pe_project(pe, c_in2[l], 6, 7, 4)
                    pe.wait_ge(jobs_copied.sem, jobs_copied.at(5))
                    idx_products(0)
                    pe_project(pe, c_in2[l], 7, 8, 4)
                    pe.wait_ge(idx_read.sem, idx_read.at(1))
                    idx_products(1)
                    pe_project(pe, c_in2[l], 8, 10, 4)
                    pe.wait_ge(idx_read.sem, idx_read.at(2))
                    for tt in range(TT):
                        tok = slice(tt * P, (tt + 1) * P)
                        for k in range(2):
                            nc.tensor.matmul(ps[:, tt, 0:384], cT[:, k, tok], w_uq[:, k, :], start=(k == 0),
                                             stop=(k == 1))
                        mm = nc.tensor.matmul(ps[:, 2 + tt, :], cT[:, 2, tok], w_ukv, start=True, stop=True)
                    mm.then_inc(lat_ready.sem, 1)
                    pe_project(pe, c_in2[l], 10, 11, 4)
                    pe.wait_ge(lat_copied.sem, lat_copied.at(1))
                    pe.wait_ge(ready2.sem, ready2.at(2))
                    pe_jobs(pe, dil_jobs, 5)
                    pe_project(pe, c_in2[l], 11, 12, 4)
                    pe.wait_ge(ready2.sem, ready2.at(3))
                    pe_jobs(pe, head_jobs, 9)
                    pe.wait_ge(projected_copied.sem, projected_copied.at(12))
                    pe.wait_ge(jobs_copied.sem, jobs_copied.at(15))
                    pe_units(pe, units, pT2, probs2, None)
                    pe.wait_ge(U["copied"].sem, U["copied"].at(n_units))
                    pe_sum_chunks(pe, c_wo2[l], lambda k, tt: mixT[:, k, tt * P:(tt + 1) * P])

                @block.scalar
                def _(act):
                    act_squares(act, mixT.rearrange("p a b -> p (a b)").rearrange("p (a b) -> p a b", a=TT))
                    cols = [512 * i for i in IN2_ORDER]
                    act_project(act, c_in2[l], zz, cols, 0, 4, 4)
                    act.wait_ge(projected_copied.sem, projected_copied.at(4))
                    for tt in range(TT):
                        A(nc.scalar.activation(cn[:, tt, 0:256], zz[:, tt, 0:256], ACT.Square,
                                               accum_out=rms_s[:, 2 + tt:3 + tt]))
                        ins = nc.scalar.activation(cn[:, tt, 256:384], zz[:, tt, Z_KV:Z_PE], ACT.Square,
                                                   accum_out=rms_s[:, 4 + tt:5 + tt])
                    ins.then_inc(lat_squared.sem, 1)
                    act_project(act, c_in2[l], zz, cols, 4, 10, 4)
                    act.wait_ge(lat_ready.sem, lat_ready.at(1))
                    for tt in range(TT):
                        nc.scalar.activation(qkm[:, tt, 0, :, :].rearrange("p a b -> p (a b)"), ps[:, tt, 0:384],
                                             ACT.Copy)
                        ins = nc.scalar.activation(kvb[:, tt, :], ps[:, 2 + tt, :], ACT.Copy)
                    ins.then_inc(lat_copied.sem, 1)
                    act_project(act, c_in2[l], zz, cols, 10, 12, 4)

                    def copy_out(act, u, n):
                        return nc.scalar.activation(mixT[:, u.pair, u.i * P:(u.i + 1) * P], ps[:, 6 + n % 2, 0:P],
                                                    ACT.Copy)

                    act_units(act, units, sm2, probs2, pT2, None, copy_out)

                @block.vector
                def _(dve):
                    dve_scale(dve, tn)
                    dve.wait_ge(params2_turned.sem, params2_turned.at(1))
                    V(nc.vector.tensor_copy(pcol[:, 0:195], ps[:, 4, 0:195]))
                    dve_turn_scaled(dve, xT_att, g_att)
                    dve.wait_ge(projected_copied.sem, projected_copied.at(2))
                    for tt in range(TT):
                        _, _, (ci, si) = tables_of(tt)
                        z = zz[:, tt, :]
                        rope(z[:, Z_IDX:Z_IDX + 288].rearrange("p (a b) -> p a b", b=32), 9, 4, ci, si, rtmp)
                        V(nc.vector.tensor_copy(kidx4[:, tt, :].rearrange("p (a b) -> p a b", a=4),
                                                z[:, Z_W - 32:Z_W].unsqueeze(1).to_broadcast([P, 4, 32])))
                    V(nc.vector.tensor_scalar(w_idx, zz[:, :, Z_W:N_IN2], 256 ** -0.5, None, ALU.mult))
                    dve.wait_ge(lat_squared.sem, lat_squared.at(1))
                    V(nc.vector.tensor_scalar(rms_v[:, 2:4], rms_s[:, 2:4], 1.0 / Q_LAT, EPS2, ALU.mult, ALU.add))
                    V(nc.vector.tensor_scalar(rms_v[:, 4:6], rms_s[:, 4:6], 1.0 / KV_LAT, EPS2, ALU.mult, ALU.add))
                    rsqrt(rms_r[:, 2:6], rms_v[:, 2:6], rms_t[:, 2:6])
                    for tt in range(TT):
                        (ca, sa), _, _ = tables_of(tt)
                        V(nc.vector.tensor_scalar(cn[:, tt, 0:256], zz[:, tt, 0:256], rms_r[:, 2 + tt:3 + tt], None,
                                                  ALU.mult))
                        V(nc.vector.tensor_scalar(cn[:, tt, 256:384], zz[:, tt, Z_KV:Z_PE], rms_r[:, 4 + tt:5 + tt],
                                                  None, ALU.mult))
                    nc.vector.memset(rms_t, 0.0).then_inc(ready2.sem, 1)
                    dve_jobs(dve, lat_jobs + idx_jobs)
                    for i in range(TT):
                        kv = (i + 1) * P
                        dve.wait_ge(idx_scores.sem, idx_scores.at(i + 1))
                        for a in range(2):
                            for m in range(4):
                                ins = nc.vector.tensor_scalar(idx_terms[:, a, m, 0:kv], ps[:, m, a * SEQ:a * SEQ + kv],
                                                              0.0, w_idx[:, i, 4 * a + m:4 * a + m + 1], ALU.max,
                                                              ALU.mult)
                        ins.then_inc(idx_read.sem, 1)
                        dve.wait_ge(idx_read.sem, idx_read.at(i + 1))
                        wk = work[:, i, 0:kv]
                        V(nc.vector.tensor_reduce(wk, idx_terms[:, :, :, 0:kv].rearrange("p a m k -> p k a m"),
                                                  XY, ALU.add))
                        V(nc.vector.tensor_tensor(wk, wk, caus[i], ALU.add))
                        for _ in range(TOPK // 8):
                            V(nc.vector.max(best[:, i, :], wk))
                            V(nc.vector.match_replace(out=wk, in_to_replace=best[:, i, :], in_values=wk,
                                                      imm_value=TAKEN))
                        V(nc.vector.tensor_scalar(wk, wk, TAKEN, NEG, ALU.not_equal, ALU.mult))
                        V(nc.vector.tensor_tensor(dsa_mask[:, i, 0:kv], wk, caus[i], ALU.add))
                    dve.wait_ge(projected_copied.sem, projected_copied.at(8))
                    for tt in range(TT):
                        (ca, sa), (ch, sh), _ = tables_of(tt)
                        z = zz[:, tt, :]
                        rope(z[:, Z_PE:Z_DIL].rearrange("p (a b) -> p a b", b=32), 1, 16, ca, sa, rtmp)
                        rope(z[:, Z_DIL:Z_DIL + 1024].rearrange("p (a b) -> p a b", b=HD), 16, 8, ch, sh, rtmp)
                    nc.vector.memset(rms_t, 0.0).then_inc(ready2.sem, 1)
                    dve.wait_ge(lat_copied.sem, lat_copied.at(1))
                    for tt in range(TT):
                        (ca, sa), _, _ = tables_of(tt)
                        rope(qkm[:, tt, 0, :, 64:96], LH, 16, ca, sa, rtmp)
                        V(nc.vector.tensor_copy(qkm[:, tt, 1, :, 0:64],
                                                kvb[:, tt, :].rearrange("p (a b) -> p a b", a=LH)[:, :, 0:64]))
                        V(nc.vector.tensor_copy(qkm[:, tt, 1, :, 64:96],
                                                zz[:, tt, Z_PE:Z_DIL].unsqueeze(1).to_broadcast([P, LH, 32])))
                    dve_jobs(dve, dil_jobs, 5)
                    dve.wait_ge(projected_copied.sem, projected_copied.at(12))
                    for tt in range(TT):
                        _, (ch, sh), _ = tables_of(tt)
                        rope(zz[:, tt, Z_DSA:Z_DSA + 512].rearrange("p (a b) -> p a b", b=HD), 8, 8, ch, sh, rtmp)
                    nc.vector.memset(rms_t, 0.0).then_inc(ready2.sem, 1)
                    dve_jobs(dve, head_jobs, 9)
                    dve_units(dve, units, sm2, probs2, None)
                    dve_add_sums(dve, 2, False)

            turn_done()
            project_done(c_in2[l])
            jobs_done(15)
            units_done(n_units)
            for s, n in ((squared, 1), (scaled, 1), (small_loaded, 9 * 16), (lat_squared, 1), (lat_ready, 1),
                         (lat_copied, 1), (params2_turned, 1), (ready2, 3), (idx_scores, 2), (idx_read, 2),
                         (summed, 2), (summed_first, 1)):
                s.advance(n)

        gT = area(4096, FT2, SEQ)
        acc2 = area(9728, 2, SEQ)
        xT_mlp = area(0, KD, SEQ)
        tn_mlp = area(2048, TT, D)
        junk_mlp = area(10240, TT, D)

        def mlp_layer(l):
            for q, c in enumerate(c_up2[l]):
                ring.release(c, up_ready, 4 * q + 4)
            release_summed(c_dn2[l])

            def wait_acc_free(eng, n):
                if 2 <= n < FT2 + 2:
                    eng.wait_ge(gate_done.sem, gate_done.at(n - 1))
                elif n >= FT2 + 2:
                    eng.wait_ge(up_done.sem, up_done.at(n - 1 - FT2))

            with nc.Block() as block:
                @block.sync
                def _(sp):
                    if l == 0:
                        sp_small_params(sp, 1)
                    ring.issue(sp, c_dn2[l][-1] + 1 + RING_SLOTS)

                @block.tensor
                def _(pe):
                    pe.wait_ge(scaled.sem, scaled.at(1))
                    pe_turn(pe, tn_mlp)
                    pe.wait_ge(turned_copied.sem, turned_copied.at(4))
                    for q, c in enumerate(c_up2[l]):
                        w = ring.rows8(c)
                        ring.arrived(pe, c)
                        for k4 in range(4):
                            n = 4 * q + k4
                            if n >= 4:
                                pe.wait_ge(up_summed.sem, up_summed.at(n - 3))
                            for k in range(KD):
                                mm = nc.tensor.matmul(ps[:, n % 4, 0:SEQ], w[:, k, k4 * P:(k4 + 1) * P], xT_mlp[:, k, :],
                                                      start=(k == 0), stop=(k == KD - 1))
                            mm.then_inc(up_ready.sem, 1)
                    pe_sum_chunks(pe, c_dn2[l], lambda k, tt: gT[:, k, tt * P:(tt + 1) * P],
                                  lambda k: pe.wait_ge(up_done.sem, up_done.at(k)))

                @block.scalar
                def _(act):
                    act_squares(act, junk_mlp)

                    def begin(n):
                        act.wait_ge(up_ready.sem, up_ready.at(n + 1))
                        wait_acc_free(act, n)
                        nc.scalar.activation(acc2[:, n % 2, :], ps[:, n % 4, 0:SEQ], ACT.Identity,
                                             bias=bias2[:, n:n + 1], scale=taps2[2][:, n:n + 1])\
                            .then_inc(up_begun.sem, 1)

                    for n in range(HALF_UP):
                        begin(n)
                        if 1 <= n <= FT2:
                            act.wait_ge(up_summed.sem, up_summed.at(n))
                            nc.scalar.activation(gT[:, n - 1, :], acc2[:, (n - 1) % 2, :], ACT.Silu)\
                                .then_inc(gate_done.sem, 1)

                @block.gpsimd
                def _(pool):
                    for n in range(FT2):
                        pool.wait_ge(gate_done.sem, gate_done.at(n + 1))
                        pool.wait_ge(up_summed.sem, up_summed.at(FT2 + n + 1))
                        nc.gpsimd.tensor_tensor(gT[:, n, :], gT[:, n, :], acc2[:, (FT2 + n) % 2, :], ALU.mult)\
                            .then_inc(up_done.sem, 1)

                @block.vector
                def _(dve):
                    dve_scale(dve, tn_mlp)
                    dve_turn_scaled(dve, xT_mlp, g_mlp)
                    for n in range(HALF_UP):
                        dve.wait_ge(up_begun.sem, up_begun.at(n + 1))
                        for j in (1, 0):
                            acc = acc2[:, n % 2, 2 - j:SEQ]
                            ins = nc.vector.scalar_tensor_tensor(acc, ps[:, n % 4, 0:SEQ - 2 + j],
                                                                 taps2[j][:, n:n + 1], acc, ALU.mult, ALU.add)
                            if j:
                                V(ins)
                        ins.then_inc(up_summed.sem, 1)
                    dve_add_sums(dve, 6, False)

            turn_done()
            for s, n in ((squared, 1), (scaled, 1), (up_ready, HALF_UP), (up_begun, HALF_UP), (up_summed, HALF_UP),
                         (gate_done, FT2), (up_done, FT2), (summed, 6), (summed_first, 1)):
                s.advance(n)

        for l in range(2):
            attention_layer(l)
            mlp_layer(l)

        g_final = area(0, D)
        result = area(2048, TT, D)
        with nc.Block() as block:
            @block.sync
            def _(sp):
                sp.dma_start(g_final, t["g_final_2"].partition_broadcast(P)).then_inc(final_loaded.sem, 16)
                sp.wait_ge(final_done.sem, 1)
                sp.dma_start(out[0].rearrange("(a p) n -> p a n", p=P), result).then_inc(final_stored.sem, 16)
                sp.wait_ge(final_stored.sem, 16)

            @block.scalar
            def _(act):
                act_squares(act, junk_mlp)

            @block.vector
            def _(dve):
                dve_scale(dve, result)
                dve.wait_ge(scaled.sem, scaled.at(1))
                dve.wait_ge(final_loaded.sem, 16)
                nc.vector.tensor_tensor(result, result, g_final.unsqueeze(1).to_broadcast([P, TT, D]), ALU.mult)\
                    .then_inc(final_done.sem, 1)


def shape_constants():
    import numpy as np

    c = np.zeros((P, C_ALL), np.float32)
    i, j = np.arange(P)[:, None], np.arange(P)[None, :]
    c[:, C_ID:C_ID + P] = i == j
    c[:, C_TRIU:C_TRIU + P] = i <= j
    c[:, C_STRIU:C_STRIU + P] = i < j
    c[:, C_ONES:C_ONES + P] = 1
    c[:, C_IOTA4:C_IOTA4 + P] = j % CAP + 1
    c[:, C_IOTA:C_IOTA + NE] = np.arange(NE)
    c[:, C_JCOL] = 4 * 1024 + np.arange(P) // CAP
    for tt in range(TT):
        c[:, C_TOK8 + tt] = 8 * (P * tt + np.arange(P)) - 4 * 1024
    c[:, C_INVF:C_INVF + 8] = np.float32(500000.0) ** (-np.arange(0, 16, 2, dtype=np.float32) / np.float32(16))
    c[:, C_CAUS0:C_CAUS0 + P] = np.where(j <= i, 0, NEG)
    k = np.arange(SEQ)[None, :]
    for tt, col, n in ((0, C_MUL0, P), (1, C_MUL1, SEQ)):
        q = P * tt + i
        dist = q - k[:, :n]
        c[:, col:col + n] = (dist >= 0) * ((dist <= 128) * 1.0 + (dist % 4 == 0) + (dist % 16 == 0))
    c[:, C_WIN1:C_WIN1 + SEQ] = np.where(c[:, C_MUL1:C_MUL1 + SEQ] > 0, 0, NEG)
    c[:, C_CAUS1:C_CAUS1 + SEQ] = np.where(k <= P + i, 0, NEG)
    col = C_ROPE
    for tt in range(TT):
        for dim in (32, 16, 8):
            inv = np.float32(500000.0) ** (-np.arange(0, dim, 2, dtype=np.float32) / np.float32(dim))
            ang = (P * tt + np.arange(P, dtype=np.float32))[:, None] * inv[None, :].astype(np.float32)
            for table in (np.cos(ang), np.sin(ang)):
                c[:, col:col + dim // 2] = table
                col += dim // 2
    return c


_INS = ["x", "positions", "ln_mix_g", "ln_mix_b", "ln_ffn_g", "ln_ffn_b", "ssm_w_in", "ssm_conv_w", "ssm_conv_b",
        "ssm_dt_bias", "ssm_a_log", "ssm_d", "ssm_norm_w", "ssm_w_out", "attn_w_qkv", "attn_lam_q1", "attn_lam_k1",
        "attn_lam_q2", "attn_lam_k2", "attn_subln_w", "attn_w_o", "moe_w_group", "moe_w_expert", "moe_w_gate",
        "moe_w_up", "moe_w_down", "g_attn_2", "w_in_2", "g_q_lat_2", "w_uq_2", "g_kv_lat_2", "w_ukv_2", "w_o_2",
        "g_ffn_2", "w_up_2", "conv_w_2", "conv_b_2", "w_down_2", "g_final_2"]


def kernel(**inputs):
    import numpy as _np
    import concourse.bacc as _bacc
    from concourse import mybir as _mybir
    from concourse.bass_utils import run_bass_kernel_spmd as _run

    nc = _bacc.Bacc("TRN2", target_bir_lowering=False, num_devices=1)
    arrays, tensors = {}, {}
    for name in _INS + ["constants"]:
        a = shape_constants() if name == "constants" else _np.ascontiguousarray(inputs[name])
        arrays[f"in_{name}_dram"] = a
        tensors[name] = nc.dram_tensor(f"in_{name}_dram", a.shape, _mybir.dt.from_np(a.dtype),
                                       kind="ExternalInput").ap()
    tensors["out"] = nc.dram_tensor("out_0_dram", (1, SEQ, D), F32, kind="ExternalOutput").ap()
    hybrid_stack(nc, tensors)
    r = _run(nc, [arrays], core_ids=[0])
    return r.results[0]["out_0_dram"]
```
